# Optimizing a Trainium2 kernel written in Bass

```python
import jax
import jax.numpy as jnp
from jax import lax
import numpy as np

D_MODEL = 1024
BATCH = 1
SEQ = 256
DEPTH = 2

GRID_W = 64
CTX_LEN = 256
N_EVEN = (DEPTH + 1) // 2
N_ODD = DEPTH // 2

MLA_HEADS = 8
MLA_NOPE = 64
MLA_ROPE = 32
MLA_V = 64
Q_LORA = 256
KV_LORA = 128
Q_BLOCK = 128

POOL_WINDOWS = (2, 4, 8, 16)
POOL_GROUP = 128
POOL_WIDTH = POOL_GROUP * len(POOL_WINDOWS)

RET_HEADS = 8
RET_DK = 128
RET_DV = 256
RET_CHUNK = 128
RET_QK_W = RET_HEADS * RET_DK
RET_V_W = RET_HEADS * RET_DV

D_FF = 4 * D_MODEL
ROPE_BASE = 10000.0
EPS = 1e-6

EVEN_IN = Q_LORA + KV_LORA + MLA_ROPE + POOL_WIDTH
EVEN_MIX = MLA_HEADS * MLA_V + POOL_WIDTH
ODD_IN = 2 * RET_QK_W + 2 * RET_V_W
ODD_MIX = RET_V_W

kernel_name = 'hybrid_mla_pool_retention_dit'

def rms_norm(x, g):
    xf = x.astype(jnp.float32)
    y = xf * lax.rsqrt(jnp.mean(xf * xf, axis=-1, keepdims=True) + EPS)
    return (y * g.astype(jnp.float32)).astype(x.dtype)

def modulate(h, shift, scale):
    return h * (1.0 + scale) + shift

def grid_positions(n):
    rows = n // GRID_W
    row = jnp.repeat(jnp.arange(rows, dtype=jnp.float32), GRID_W)
    col = jnp.tile(jnp.arange(GRID_W, dtype=jnp.float32), rows)
    return row, col

def rope_axis(x, pos):
    d = x.shape[-1]
    freqs = ROPE_BASE ** (-jnp.arange(0, d, 2, dtype=jnp.float32) / d)
    ang = pos[:, None] * freqs[None, :]
    cos = jnp.cos(ang)[None, :, None, :].astype(x.dtype)
    sin = jnp.sin(ang)[None, :, None, :].astype(x.dtype)
    x1, x2 = jnp.split(x, 2, axis=-1)
    return jnp.concatenate([x1 * cos - x2 * sin, x1 * sin + x2 * cos], axis=-1)

def rope_2d(x, pos):
    xr, xc = jnp.split(x, 2, axis=-1)
    return jnp.concatenate([rope_axis(xr, pos[0]), rope_axis(xc, pos[1])], axis=-1)

def split_even(u):
    a = Q_LORA
    b = a + KV_LORA
    r = b + MLA_ROPE
    return u[..., :a], u[..., a:b], u[..., b:r], u[..., r:]

def mla_queries(u_q, g_q, w_uq, pos):
    B, L, _ = u_q.shape
    q = (rms_norm(u_q, g_q) @ w_uq).reshape(B, L, MLA_HEADS, MLA_NOPE + MLA_ROPE)
    q_nope, q_rope = q[..., :MLA_NOPE], q[..., MLA_NOPE:]
    if pos is not None:
        q_rope = rope_2d(q_rope, pos)
    return q_nope, q_rope

def mla_keys_values(u_kv, u_kr, g_kv, w_ukv, pos):
    B, L, _ = u_kv.shape
    kv = (rms_norm(u_kv, g_kv) @ w_ukv).reshape(B, L, MLA_HEADS, MLA_NOPE + MLA_V)
    k_nope, v = kv[..., :MLA_NOPE], kv[..., MLA_NOPE:]
    k_rope = u_kr
    if pos is not None:
        k_rope = rope_2d(u_kr[:, :, None, :], pos)[:, :, 0, :]
    return k_nope, k_rope, v

def block_attention(q_nope, q_rope, k_nope, k_rope, v):
    B, S, H, _ = q_nope.shape
    nb = S // Q_BLOCK
    scale = (MLA_NOPE + MLA_ROPE) ** -0.5

    def blocks(t):
        return t.reshape(B, nb, Q_BLOCK, H, t.shape[-1]).swapaxes(0, 1)

    def attend(qb):
        qn, qr = qb
        s = jnp.einsum('bqhd,bkhd->bhqk', qn, k_nope) + jnp.einsum('bqhr,bkr->bhqk', qr, k_rope)
        p = jax.nn.softmax(s.astype(jnp.float32) * scale, axis=-1).astype(v.dtype)
        return jnp.einsum('bhqk,bkhe->bqhe', p, v)

    o = lax.map(attend, (blocks(q_nope), blocks(q_rope)))
    return o.swapaxes(0, 1).reshape(B, S, H * MLA_V)

def multiscale_pool(p, w_pool, pool_scale):
    B, L, _ = p.shape
    cs = jnp.concatenate([jnp.zeros((B, 1, POOL_WIDTH), jnp.float32),
                          jnp.cumsum(p.astype(jnp.float32), axis=1)], axis=1)
    t = jnp.arange(L)
    outs = []
    for g, w in enumerate(POOL_WINDOWS):
        lo = jnp.clip(t - w // 2, 0, L)
        hi = jnp.clip(t + (w - w // 2), 0, L)
        sl = slice(g * POOL_GROUP, (g + 1) * POOL_GROUP)
        csg = cs[:, :, sl]
        mean = (csg[:, hi] - csg[:, lo]) / (hi - lo).astype(jnp.float32)[None, :, None]
        outs.append((mean.astype(p.dtype) - p[..., sl]) @ w_pool[g])
    return jnp.concatenate(outs, axis=-1) * pool_scale

def mla_pool_mixer(h_lat, h_ctx, w_in, g_q, g_kv, w_uq, w_ukv, w_pool, pool_scale, w_out,
                   pos, need_ctx):
    lq, lkv, lkr, lp = split_even(h_lat @ w_in)
    if need_ctx:
        cq, ckv, ckr, cp = split_even(h_ctx @ w_in)
    else:
        ukv = h_ctx @ w_in[:, Q_LORA:Q_LORA + KV_LORA + MLA_ROPE]
        ckv, ckr = ukv[..., :KV_LORA], ukv[..., KV_LORA:]
    ck_nope, ck_rope, cv = mla_keys_values(ckv, ckr, g_kv, w_ukv, None)
    lk_nope, lk_rope, lv = mla_keys_values(lkv, lkr, g_kv, w_ukv, pos)
    lq_nope, lq_rope = mla_queries(lq, g_q, w_uq, pos)
    k_nope = jnp.concatenate([ck_nope, lk_nope], axis=1)
    k_rope = jnp.concatenate([ck_rope, lk_rope], axis=1)
    v = jnp.concatenate([cv, lv], axis=1)
    o_lat = block_attention(lq_nope, lq_rope, k_nope, k_rope, v)
    y_lat = jnp.concatenate([o_lat, multiscale_pool(lp, w_pool, pool_scale)], axis=-1) @ w_out
    y_ctx = None
    if need_ctx:
        cq_nope, cq_rope = mla_queries(cq, g_q, w_uq, None)
        o_ctx = block_attention(cq_nope, cq_rope, ck_nope, ck_rope, cv)
        y_ctx = jnp.concatenate([o_ctx, multiscale_pool(cp, w_pool, pool_scale)], axis=-1) @ w_out
    return y_lat, y_ctx

def retention_log_decays():
    fwd = jnp.log1p(-jnp.exp2(-5.0 - jnp.arange(RET_HEADS, dtype=jnp.float32)))
    return fwd, fwd[::-1]

def retention_scan(q, k, v, log_g, state0, inclusive):
    B, L, H, _ = q.shape
    nc = L // RET_CHUNK
    idx = jnp.arange(RET_CHUNK, dtype=jnp.float32)
    diff = idx[:, None] - idx[None, :]
    mask = diff >= 0 if inclusive else diff > 0
    decay_in = jnp.where(mask, jnp.exp(jnp.where(mask, diff, 0.0)[None] * log_g[:, None, None]),
                         0.0).astype(q.dtype)
    decay_q = jnp.exp((idx[:, None] + 1.0) * log_g[None, :]).astype(q.dtype)
    decay_k = jnp.exp((RET_CHUNK - 1.0 - idx[:, None]) * log_g[None, :]).astype(q.dtype)
    decay_c = jnp.exp(RET_CHUNK * log_g)

    def chunks(t):
        return t.reshape(B, nc, RET_CHUNK, H, t.shape[-1]).swapaxes(0, 1)

    def step(state, qkv):
        qc, kc, vc = qkv
        s = jnp.einsum('bnhd,bmhd->bhnm', qc, kc) * decay_in
        inner = jnp.einsum('bhnm,bmhe->bnhe', s, vc)
        cross = jnp.einsum('bnhd,bhde->bnhe', qc * decay_q[None, :, :, None], state)
        new = state * decay_c[None, :, None, None] + jnp.einsum(
            'bmhd,bmhe->bhde', kc * decay_k[None, :, :, None], vc)
        return new, inner + cross

    final, out = lax.scan(step, state0, (chunks(q), chunks(k), chunks(v)))
    return out.swapaxes(0, 1).reshape(B, L, H, v.shape[-1]), final

def retention_final_state(k, v, log_g, reverse):
    L = k.shape[1]
    t = jnp.arange(L, dtype=jnp.float32)
    steps = t if reverse else (L - 1.0 - t)
    w = jnp.exp(steps[:, None] * log_g[None, :]).astype(k.dtype)
    return jnp.einsum('blhd,blhe->bhde', k * w[None, :, :, None], v).astype(jnp.float32)

def retention_bidir(q, k, v, state_f, state_b, log_f, log_b):
    o_f, s_f = retention_scan(q, k, v, log_f, state_f, True)
    flip = lambda t: jnp.flip(t, axis=1)
    o_b, s_b = retention_scan(flip(q), flip(k), flip(v), log_b, state_b, False)
    return o_f + flip(o_b), s_f, s_b

def head_group_norm(o):
    of = o.astype(jnp.float32)
    mu = jnp.mean(of, axis=-1, keepdims=True)
    var = jnp.mean(jnp.square(of - mu), axis=-1, keepdims=True)
    return (of - mu) * lax.rsqrt(var + EPS)

def to_heads(t, d):
    return t.reshape(t.shape[0], t.shape[1], RET_HEADS, d)

def retention_output(o, g, w_out):
    B, L = g.shape[0], g.shape[1]
    y = jax.nn.silu(g) * head_group_norm(o).astype(g.dtype).reshape(B, L, ODD_MIX)
    return y @ w_out

def retention_mixer(h_lat, h_ctx, w_in, w_out, pos, need_ctx):
    log_f, log_b = retention_log_decays()
    kscale = RET_DK ** -0.5
    a, b, c = RET_QK_W, 2 * RET_QK_W, 2 * RET_QK_W + RET_V_W
    u = h_lat @ w_in
    q = rope_2d(to_heads(u[..., :a], RET_DK), pos)
    k = rope_2d(to_heads(u[..., a:b], RET_DK), pos) * kscale
    v = to_heads(u[..., b:c], RET_DV)
    g = u[..., c:]
    y_ctx = None
    if need_ctx:
        uc = h_ctx @ w_in
        cq = to_heads(uc[..., :a], RET_DK)
        ck = to_heads(uc[..., a:b], RET_DK) * kscale
        cv = to_heads(uc[..., b:c], RET_DV)
        zero = jnp.zeros((h_ctx.shape[0], RET_HEADS, RET_DK, RET_DV), jnp.float32)
        o_ctx, s_f, s_b = retention_bidir(cq, ck, cv, zero, zero, log_f, log_b)
        y_ctx = retention_output(o_ctx, uc[..., c:], w_out)
    else:
        ukv = h_ctx @ w_in[:, a:c]
        ck = to_heads(ukv[..., :RET_QK_W], RET_DK) * kscale
        cv = to_heads(ukv[..., RET_QK_W:], RET_DV)
        s_f = retention_final_state(ck, cv, log_f, False)
        s_b = retention_final_state(ck, cv, log_b, True)
    o_lat, _, _ = retention_bidir(q, k, v, s_f, s_b, log_f, log_b)
    return retention_output(o_lat, g, w_out), y_ctx

def sq_relu_mlp(h, w1, w2):
    return jnp.square(jax.nn.relu(h @ w1)) @ w2

def setup_inputs(seed: int = 0) -> dict:
    key = jax.random.key(seed)
    keys = jax.random.split(key, 22)

    def nrm(i, shape, scale=1.0):
        return jax.random.normal(keys[i], shape, jnp.float32) * scale

    def gain(i, shape):
        return 1.0 + nrm(i, shape, 0.02)

    D = D_MODEL
    return {
        'x': nrm(0, (BATCH, SEQ, D)),
        'c': nrm(1, (BATCH, D)),
        'ctx': nrm(2, (BATCH, CTX_LEN, D)),
        'c_ctx': nrm(3, (D,)),
        'w_ada': nrm(4, (DEPTH, D, 6 * D), 0.5 * D ** -0.5),
        'b_ada': nrm(5, (DEPTH, 6 * D), 0.02),
        'g_mix_pre': gain(6, (DEPTH, D)),
        'g_mix_post': gain(7, (DEPTH, D)),
        'g_ffn_pre': gain(8, (DEPTH, D)),
        'g_ffn_post': gain(9, (DEPTH, D)),
        'w_ffn_in': nrm(10, (DEPTH, D, D_FF), D ** -0.5),
        'w_ffn_out': nrm(11, (DEPTH, D_FF, D), D_FF ** -0.5),
        'w_in_even': nrm(12, (N_EVEN, D, EVEN_IN), D ** -0.5),
        'g_q_lora': gain(13, (N_EVEN, Q_LORA)),
        'g_kv_lora': gain(14, (N_EVEN, KV_LORA)),
        'w_uq': nrm(15, (N_EVEN, Q_LORA, MLA_HEADS * (MLA_NOPE + MLA_ROPE)), Q_LORA ** -0.5),
        'w_ukv': nrm(16, (N_EVEN, KV_LORA, MLA_HEADS * (MLA_NOPE + MLA_V)), KV_LORA ** -0.5),
        'w_pool': nrm(17, (N_EVEN, len(POOL_WINDOWS), POOL_GROUP, POOL_GROUP), POOL_GROUP ** -0.5),
        'pool_scale': gain(18, (N_EVEN, POOL_WIDTH)),
        'w_out_even': nrm(19, (N_EVEN, EVEN_MIX, D), EVEN_MIX ** -0.5),
        'w_in_odd': nrm(20, (N_ODD, D, ODD_IN), D ** -0.5),
        'w_out_odd': nrm(21, (N_ODD, ODD_MIX, D), ODD_MIX ** -0.5),
    }

def reference(x, c, ctx, c_ctx, w_ada, b_ada, g_mix_pre, g_mix_post, g_ffn_pre, g_ffn_post,
              w_ffn_in, w_ffn_out, w_in_even, g_q_lora, g_kv_lora, w_uq, w_ukv, w_pool,
              pool_scale, w_out_even, w_in_odd, w_out_odd):
    pos = grid_positions(x.shape[1])
    cond_lat = jax.nn.silu(c)
    cond_ctx = jax.nn.silu(c_ctx)
    for layer in range(DEPTH):
        need_ctx = layer < DEPTH - 1
        mod_lat = (cond_lat @ w_ada[layer] + b_ada[layer])[:, None, :]
        mod_ctx = cond_ctx @ w_ada[layer] + b_ada[layer]
        sh1, sc1, gt1, sh2, sc2, gt2 = jnp.split(mod_lat, 6, axis=-1)
        csh1, csc1, cgt1, csh2, csc2, cgt2 = jnp.split(mod_ctx, 6, axis=-1)

        h_lat = modulate(rms_norm(x, g_mix_pre[layer]), sh1, sc1)
        h_ctx = modulate(rms_norm(ctx, g_mix_pre[layer]), csh1, csc1)
        if layer % 2 == 0:
            i = layer // 2
            y_lat, y_ctx = mla_pool_mixer(h_lat, h_ctx, w_in_even[i], g_q_lora[i], g_kv_lora[i],
                                          w_uq[i], w_ukv[i], w_pool[i], pool_scale[i],
                                          w_out_even[i], pos, need_ctx)
        else:
            i = layer // 2
            y_lat, y_ctx = retention_mixer(h_lat, h_ctx, w_in_odd[i], w_out_odd[i], pos, need_ctx)

        x = x + gt1 * rms_norm(y_lat, g_mix_post[layer])
        f_lat = sq_relu_mlp(modulate(rms_norm(x, g_ffn_pre[layer]), sh2, sc2),
                            w_ffn_in[layer], w_ffn_out[layer])
        x = x + gt2 * rms_norm(f_lat, g_ffn_post[layer])

        if need_ctx:
            ctx = ctx + cgt1 * rms_norm(y_ctx, g_mix_post[layer])
            f_ctx = sq_relu_mlp(modulate(rms_norm(ctx, g_ffn_pre[layer]), csh2, csc2),
                                w_ffn_in[layer], w_ffn_out[layer])
            ctx = ctx + cgt2 * rms_norm(f_ctx, g_ffn_post[layer])
    return x


_drawn_inputs = setup_inputs


def setup_inputs(seed=0):
    import zlib

    import numpy as np

    out = dict(_drawn_inputs(seed))
    spreads = {}
    factors = {'g_mix_pre': 4.609,
     'g_mix_post': 6.765,
     'g_ffn_pre': 6.223,
     'g_ffn_post': 6.592,
     'g_q_lora': 8.0,
     'g_kv_lora': 8.0,
     'pool_scale': 8.0}
    for name, (base, spread) in spreads.items():
        noise = np.random.default_rng([zlib.crc32(name.encode()), seed]).standard_normal(out[name].shape)
        drawn = base * np.exp(spread * noise) if base else spread * noise
        out[name] = jnp.asarray(drawn.astype(out[name].dtype))
    for name, factor in factors.items():
        out[name] = (out[name] * factor).astype(out[name].dtype)
    return out
```

```python
from contextlib import ExitStack, contextmanager

import numpy as np

import concourse.bass as bass
from concourse import mybir

F32 = mybir.dt.float32
F32R = mybir.dt.float32r
ALU = mybir.AluOpType
ACT = mybir.ActivationFunctionType
AXX = mybir.AxisListType.X

P = 128
D = 1024
KD = D // P
SEG = 256
T = 2 * SEG
LAT = SEG
EPS = 1e-6

Q_LORA, KV_LORA, ROPE, NOPE, VD = 256, 128, 32, 64, 64
HEADS = 8
PAIRS = HEADS // 2
QH = NOPE + ROPE
ATT_SCALE = float(QH) ** -0.5
POOL_GROUPS = 4
POOL0 = Q_LORA + KV_LORA + ROPE
PAD = 8

R_DK, R_DV = 128, 256
R_Q0, R_K0, R_V0, R_G0 = 0, HEADS * R_DK, 2 * HEADS * R_DK, 2 * HEADS * R_DK + HEADS * R_DV

DFF = 4 * D
HALF = DFF // 2
HC = HALF // P
PANEL_COLS = 256
PANEL = KD * PANEL_COLS
RAW_SLOTS = 4
BANKS = 8

SHIFT1, SCALE1, GATE1, SHIFT2, SCALE2, GATE2 = range(6)


def panel_plan():
    ada, one, two = ("ada", 1), ("split", 1), ("split", 2)
    plan = [one] + [ada] * 8 + [one] * 4 + [two]
    plan += [ada] * 4 * (PAIRS - 1) + [one] + [ada] * 4
    plan += [one] * 5
    plan += [ada] * 8
    plan += [one] * 30
    plan += [two, one]
    plan += [ada] * 8
    plan += [one, two, one, one] * (HEADS - 1)
    plan += [one, two, one] + [ada] * 4 + [one] + [ada] * 4
    plan += [one] * 30
    return plan


PLAN = panel_plan()
SPLIT_AT = [n for n, (kind, _) in enumerate(PLAN) if kind == "split"]
ADA_AT = [n for n, (kind, _) in enumerate(PLAN) if kind == "ada"]


def arrivals(n):
    return 16 * sum(PLAN[m][1] for m in range(n % RAW_SLOTS, n + 1, RAW_SLOTS))


def job_plan():
    jobs = [("params", "d")] * 2 + [("x", "ad")] * KD + [("norm", "ad")]
    ada = [("ada", "a"), ("ada", "d")]
    jobs += ada * 2
    jobs += [("lora", "ad")] * 3 + [("kr", "a")] + [("norm", "ad")] * 2 + [("pool_in", "a")] * POOL_GROUPS
    jobs += [("v", "ad")] * 4
    qk = [("q", "a")] * 2 + [("k", "ad")] * 2
    jobs += qk
    for p in range(PAIRS):
        jobs += [("scores", "ad")] * 6 + (qk if p + 1 < PAIRS else []) + ada + [("values", "ad")] * 8
    jobs += [("pool_out", "ad")] * POOL_GROUPS + [("mix_out", "ad")] * KD + [("norm", "ad")]
    jobs += ada + [("norm", "ad")] + ada
    ffn = ([("hidden", "ad")] * HC + [("ffn_out", "d")] * KD) * 2 + [("norm", "ad")]
    jobs += ffn + ada + [("norm", "ad")] + ada
    r_qk, swap, r_v = [("r_qk", "a")] * 2, [("r_swap", "d")], [("r_v", "ad")] * 2
    attend = [("r_scores", "d")] * 2 + [("r_gate", "ad")] * 2 + [("r_values", "d")] * 2
    turn, r_out = [("r_turn", "ad")], [("r_out", "d")] * 4
    jobs += r_qk + swap + r_v + (attend + r_qk + turn + swap + r_v + r_out) * (HEADS - 1)
    jobs += attend + ada + turn + r_out
    jobs += [("norm", "ad")] + ada + [("norm", "ad")] + ffn
    jobs += [("rows", "a")] * 4
    return jobs


JOBS = job_plan()


def part_of(engine, j):
    return sum(engine in JOBS[m][1] for m in range(j + 1))


def first_job(stage, nth=0):
    starts = [m for m in range(len(JOBS)) if JOBS[m][0] == stage and (m == 0 or JOBS[m - 1][0] != stage)]
    return starts[nth]


class Tally:

    def __init__(self):
        self.n = {}
        self.reg = None
        self.per = {}

    def at(self, name, more=0):
        v = self.n.get(name, 0) + more
        if self.reg is not None and self.per.get(name, 0):
            return self.reg * self.per[name] + v
        return v

    def evacuated(self, engine, j):
        if self.reg is None:
            return part_of(engine, j)
        rounds_jobs = self.per["job"]
        per = part_of(engine, self.start + rounds_jobs - 1) - part_of(engine, self.start - 1)
        v = part_of(engine, j) if j >= self.start else part_of(engine, j + rounds_jobs) - per
        return self.reg * per + v if per else v

    def first(self, name):
        return self.n.get(name, 0)

    def add(self, name, k=1):
        self.n[name] = self.n.get(name, 0) + k

    @contextmanager
    def loop(self, eng, rounds, **per):
        start = dict(self.n)
        with eng.Fori(0, rounds) as i:
            self.reg, self.per, self.start = i, per, start.get("job", 0)
            yield i
            self.reg = None
        for name in set(self.n) | set(per):
            added = self.n.get(name, 0) - start.get(name, 0)
            assert added == per.get(name, 0), (name, added, per.get(name, 0))
            self.n[name] = start.get(name, 0) + rounds * added


def mm3(pe, out, stat, mov, first, last):
    pe.matmul(out, stat[0], mov[0], start=first, stop=False)
    pe.matmul(out, stat[0], mov[1], start=False, stop=False)
    return pe.matmul(out, stat[1], mov[0], start=False, stop=last)


def build(nc, A, out):
    with ExitStack() as ctx:
        base = [16512]

        def place(name, shape, dt, at=None):
            size = 4 * int(np.prod(shape[1:]))
            if at is None:
                at = base[0]
                base[0] += (size + 31) // 32 * 32
            return nc.alloc_sbuf_tensor_at(name, shape, dt, offset=at)

        X = place("X", [P, KD, T], F32)
        h_hi_at = base[0]
        H_hi = place("H_hi", [P, KD, T], F32R)
        h_lo_at = base[0]
        H_lo = place("H_lo", [P, KD, T], F32R)
        RAW = [place(f"RAW{n}", [P, PANEL], F32) for n in range(RAW_SLOTS)]
        W_hi = [place(f"W_hi{n}", [P, PANEL], F32R) for n in range(2)]
        W_lo = [place(f"W_lo{n}", [P, PANEL], F32R) for n in range(2)]
        big = base[0]
        base[0] += 80 * 1024
        SQ = place("SQ", [P, 2, T], F32)
        tmp_at = base[0]
        TMP = place("TMP", [P, 2, T], F32)
        ACC = place("ACC", [P, T], F32, tmp_at + 4 * T)
        R = place("R", [P, T], F32)
        ident = place("ident", [P, P], F32)
        ones = place("ones", [P, P], F32)
        bcol = place("bcol", [P, 96], F32)
        gcol = place("gcol", [P, 88], F32)
        cond = place("cond", [P, KD, 32], F32)
        mod = place("mod", [P, 2, 6, KD, 2], F32)
        pre_gain = place("pre_gain", [P, 2, 2, KD, 2], F32)
        post_gain = place("post_gain", [P, 2, 2, KD, 2], F32)
        adarow = place("adarow", [P, 256], F32)
        small = place("small", [P, 48], F32)
        assert base[0] <= nc.sbuf_usable_end, base[0]
        eps_col = small[:, 0:1]

        xrows = place("xrows", [P, 4, D], F32, big + 16384)
        brows = place("brows", [P, P], F32, big + 32768)
        grows = place("grows", [P, P], F32, big + 32768 + 512)
        silu_e = place("silu_e", [P, 16], F32, big + 32768 + 1024)
        at = [big]

        def region(name, shape, dt):
            t = place(name, shape, dt, at[0])
            at[0] += (4 * int(np.prod(shape[1:])) + 31) // 32 * 32
            return t

        Q_hi, Q_lo = region("Q_hi", [P, 2, T], F32R), region("Q_lo", [P, 2, T], F32R)
        K_hi, K_lo = region("K_hi", [P, 2, T], F32R), region("K_lo", [P, 2, T], F32R)
        V_hi, V_lo = region("V_hi", [P, 4, T], F32R), region("V_lo", [P, 4, T], F32R)
        QN_hi, QN_lo = region("QN_hi", [P, 3, T], F32R), region("QN_lo", [P, 3, T], F32R)
        lora_at = at[0]
        PROB = region("PROB", [P, 4, T], F32)
        PROBC = region("PROBC", [P, 2, 2, SEG], F32)
        pt_at = at[0]
        PT_hi, PT_lo = region("PT_hi", [P, 4, T], F32R), region("PT_lo", [P, 4, T], F32R)
        QF = region("QF", [P, 2, T], F32)
        SW = region("SW", [P, 2, T], F32)
        assert at[0] <= big + 80 * 1024
        LORA = place("LORA", [P, 3, T], F32, lora_at)
        KR = place("KR", [P, T], F32, lora_at + 12 * T)
        ropeA = place("ropeA", [P, 2, T], F32, tmp_at)
        PRAW = place("PRAW", [P, POOL_GROUPS, T], F32, pt_at)
        PD = place("PD", [P, POOL_GROUPS, T], F32, h_lo_at + 16 * T)
        pool_inv = place("pool_inv", [P, POOL_GROUPS, SEG], F32, h_lo_at)
        WIDE = SEG + 2 * PAD
        PP = place("PP", [P, 2, WIDE], F32, h_hi_at)
        PS = [place(f"PS{n}", [P, 2, WIDE], F32, h_hi_at + (n + 1) * 8 * WIDE) for n in range(2)]
        PD_hi, PD_lo = place("PD_hi", [P, 4, T], F32R, pt_at), place("PD_lo", [P, 4, T], F32R, pt_at + 16 * T)
        HID_hi, HID_lo = place("HID_hi", [P, HC, T], F32R, big), place("HID_lo", [P, HC, T], F32R, big + 32768)
        Y = place("Y", [P, KD, T], F32, big + 65536)
        at[0] = big
        QK = region("QK", [P, 3, SEG], F32)
        ROT = region("ROT", [P, 2, SEG], F32)
        QK_hi, QK_lo = region("QK_hi", [P, 3, SEG], F32R), region("QK_lo", [P, 3, SEG], F32R)
        ropeR = region("ropeR", [P, 2, SEG], F32)
        perm = region("perm", [P, P], F32)
        DEC = region("DEC", [P, 4, SEG], F32)
        RV_hi, RV_lo = region("RV_hi", [P, 4, SEG], F32R), region("RV_lo", [P, 4, SEG], F32R)
        SA = region("SA", [P, 4, SEG], F32)
        SA_hi, SA_lo = region("SA_hi", [P, 4, SEG], F32R), region("SA_lo", [P, 4, SEG], F32R)
        GE = region("GE", [P, 2, SEG], F32)
        GS = region("GS", [P, 2, SEG], F32)
        ON = region("ON", [P, 2, SEG], F32)
        YT_hi, YT_lo = region("YT_hi", [P, 2, SEG], F32R), region("YT_lo", [P, 2, SEG], F32R)
        stats = region("stats", [P, 2, 6], F32)
        mv = region("mv", [P, 2, 2], F32)
        rstd = region("rstd", [P, 2], F32)
        neg_half = region("neg_half", [P, 2], F32)
        assert at[0] <= big + 65536
        OUTR = place("OUTR", [P, 2, D], F32, big)

        bank = [ctx.enter_context(nc.psum_tensor(f"bank{n}", [P, 512], F32)) for n in range(BANKS)]

        def sem(name):
            return ctx.enter_context(nc.semaphore(name))

        raw_in = [sem(f"raw_in{n}") for n in range(RAW_SLOTS)]
        split_hi, split_lo = sem("split_hi"), sem("split_lo")
        half_sum, ada_used = sem("half_sum"), sem("ada_used")
        acc_full, act_out, dve_out = sem("acc_full"), sem("act_out"), sem("dve_out")
        full_ready, hi_ready, lo_ready = sem("full_ready"), sem("hi_ready"), sem("lo_ready")
        sq_ready, ones_done, acc_done = sem("sq_ready"), sem("ones_done"), sem("acc_done")
        x_ready, rowmax = sem("x_ready"), sem("rowmax")
        params_in, x_in, consts_in, ret_in = sem("params_in"), sem("x_in"), sem("consts_in"), sem("ret_in")
        inv_in, rows_zero, ident_ready = sem("inv_in"), sem("rows_zero"), sem("ident_ready")
        cond_e, cond_ready = sem("cond_e"), sem("cond_ready")
        act_chain, dve_chain, pool_chain = sem("act_chain"), sem("dve_chain"), sem("pool_chain")
        pool_d = sem("pool_d")
        rows_ready = sem("rows_ready")
        decay_in, stat_ready, rstd_ready, y_zero = sem("decay_in"), sem("stat_ready"), sem("rstd_ready"), sem("y_zero")
        out_done = sem("out_done")

        def by_chunk(w):
            return w.rearrange("(k p) n -> p k n", p=P)

        ada_v = [by_chunk(A["w_ada"][l]) for l in range(2)]
        in_even = by_chunk(A["w_in_even"][0])
        out_even = by_chunk(A["w_out_even"][0])
        in_odd = by_chunk(A["w_in_odd"][0])
        out_odd = by_chunk(A["w_out_odd"][0])
        ffn_in = [by_chunk(A["w_ffn_in"][l]) for l in range(2)]
        ffn_out = [by_chunk(A["w_ffn_out"][l]) for l in range(2)]
        IN_PANELS = (0, 256, POOL0, POOL0 + 256)

        def w8(pair, s, k, c0, n):
            at = k * PANEL_COLS + c0
            return pair[0][s % 2][:, at:at + n], pair[1][s % 2][:, at:at + n]

        WW = (W_hi, W_lo)
        HH = (H_hi, H_lo)

        def ffn_bank(first, j):
            return bank[(first + (j - first) % 4) % BANKS]

        block = ctx.enter_context(nc.Block())

        @block.sync
        def _(sp):
            t = Tally()

            def load(*pairs):
                n = t.first("panel")
                slot = n % RAW_SLOTS
                kind, dmas = PLAN[n]
                assert dmas == len(pairs)
                if n >= RAW_SLOTS:
                    splits = sum(m <= n - RAW_SLOTS for m in SPLIT_AT)
                    adas = sum(m <= n - RAW_SLOTS for m in ADA_AT)
                    if t.reg is not None:
                        before = [PLAN[m][0] for m in range(n - RAW_SLOTS, n)]
                        assert before[0] == "ada" or "ada" not in before
                        splits = t.reg * RAW_SLOTS + (t.first("split") - 3)
                        sp.wait_ge(split_lo, splits)
                    elif splits:
                        sp.wait_ge(split_lo, splits)
                    if adas:
                        sp.wait_ge(ada_used, adas)
                for c0, src in pairs:
                    size = int(np.prod(src.shape[1:]))
                    dst = RAW[slot][:, c0:c0 + size]
                    if len(src.shape) == 3:
                        dst = dst.rearrange("p (k n) -> p k n", k=src.shape[1])
                    sp.dma_start(dst, src).then_inc(raw_in[slot], 16)
                t.add("panel")
                t.add("split", kind == "split")

            def ada(layer, part):
                for kk in range(4):
                    load((0, ada_v[layer][:, 2 * kk:2 * kk + 2, part * D:(part + 1) * D]))

            def ffn_panel(layer, n):
                load((0, ffn_in[layer][:, :, n * 256:(n + 1) * 256]))

            def ffn(layer, last):
                for n in range(2, 8):
                    ffn_panel(layer, n)
                for half in range(2):
                    if half:
                        with t.loop(sp, 2, panel=4, split=4) as i:
                            for n in range(4):
                                load((0, ffn_in[layer][:, :, bass.ds(i * 1024 + (HALF + n * 256), 256)]))
                    if last and half:
                        for c in range(4):
                            for kg in range(2):
                                load((0, ffn_out[layer][:, 16 * half + 8 * kg:16 * half + 8 * kg + 8,
                                                        c * 256:(c + 1) * 256]))
                        continue
                    with t.loop(sp, 2, panel=4, split=4) as i:
                        for n in range(4):
                            k0 = 16 * half + 8 * (n % 2)
                            load((0, ffn_out[layer][:, k0:k0 + 8, bass.ds(i * 512 + (n // 2) * 256, 256)]))

            def head_qk(h):
                q = in_odd[:, :, bass.ds(h * R_DK + R_Q0, R_DK)] if not isinstance(h, int) else \
                    in_odd[:, :, R_Q0 + h * R_DK:R_Q0 + (h + 1) * R_DK]
                k = in_odd[:, :, bass.ds(h * R_DK + R_K0, R_DK)] if not isinstance(h, int) else \
                    in_odd[:, :, R_K0 + h * R_DK:R_K0 + (h + 1) * R_DK]
                load((0, q), (KD * R_DK, k))

            load((0, in_even[:, :, 0:256]))
            ada(0, SHIFT1)
            ada(0, SCALE1)
            for c0 in IN_PANELS[1:]:
                load((0, in_even[:, :, c0:c0 + 256]))
            load((0, by_chunk(A["w_uq"][0])))
            load((0, by_chunk(A["w_ukv"][0])), (D, A["w_pool"][0].rearrange("g p n -> p g n")))
            for part in (GATE1, SHIFT2, SCALE2):
                ada(0, part)
            load((0, out_even[:, :, 0:256]))
            ada(0, GATE2)
            for c in range(1, 4):
                load((0, out_even[:, :, c * 256:(c + 1) * 256]))
            ffn_panel(0, 0)
            ffn_panel(0, 1)
            ada(1, SHIFT1)
            ada(1, SCALE1)
            ffn(0, False)

            def head_cols(h, first):
                c = bass.ds(h * R_DV + first, R_DV) if not isinstance(h, int) else \
                    slice(first + h * R_DV, first + (h + 1) * R_DV)
                load((0, in_odd[:, :, c]))

            head_qk(0)
            head_cols(0, R_V0)
            ada(1, GATE1)
            ada(1, SHIFT2)
            with t.loop(sp, HEADS - 1, panel=4, split=4) as h:
                head_cols(h, R_G0)
                head_qk(h + 1)
                head_cols(h + 1, R_V0)
                load((0, out_odd[:, bass.ds(h * 2, 2), :]))
            head_cols(HEADS - 1, R_G0)
            load((0, out_odd[:, 2 * HEADS - 2, :]), (D, out_odd[:, 2 * HEADS - 1, :]))
            ffn_panel(1, 0)
            ada(1, SCALE2)
            ffn_panel(1, 1)
            ada(1, GATE2)
            ffn(1, True)
            for n in range(4):
                sp.wait_ge(act_out, part_of("a", first_job("rows") + n))
                tt, half = n % 2, n // 2
                sp.dma_start(out[0, tt * P:(tt + 1) * P, half * 512:(half + 1) * 512],
                             OUTR[:, tt, half * 512:(half + 1) * 512]).then_inc(out_done, 16)
            sp.wait_ge(out_done, 64)

        @block.gpsimd
        def _(pool):
            t = Tally()

            def chain(ins):
                ins.then_inc(pool_chain, 1)
                t.add("chain")
                pool.wait_ge(pool_chain, t.at("chain"))

            pool.memset(brows[:, :], 0.0).then_inc(rows_zero, 1)
            pool.memset(grows[:, :], 0.0).then_inc(rows_zero, 1)
            pool.memset(cond[:, :, :], 0.0).then_inc(rows_zero, 1)
            pool.memset(eps_col, EPS).then_inc(rows_zero, 1)
            pool.memset(ones[:, :], 1.0).then_inc(rows_zero, 1)
            chain(pool.memset(ident[:, :], 0.0))
            pool.affine_select(out=ident[:, :], in_=ident[:, :], compare_op=ALU.not_equal, fill=1.0, base=0,
                               pattern=[[-1, P]], channel_multiplier=1).then_inc(ident_ready, 1)

            pool.wait_ge(lo_ready, KD)
            pool.dma_start(ropeA[NOPE:QH, :, :], A["rope_att"]).then_inc(consts_in, 16)
            pool.wait_ge(act_out, part_of("a", first_job("pool_in") + POOL_GROUPS - 1))
            pool.dma_start(pool_inv[:, :, :], A["pool_inv"]).then_inc(inv_in, 16)
            pool.wait_ge(inv_in, 16)
            chain(pool.memset(PP[:, :, :], 0.0))
            for g in range(POOL_GROUPS):
                raw = PRAW[:, g, :].rearrange("p (s n) -> p s n", s=2)
                chain(pool.tensor_copy(PP[:, :, PAD:PAD + SEG], raw))
                src = PP
                lo, hi = 1, WIDE - 1
                chain(pool.tensor_tensor(PS[0][:, :, lo:hi], src[:, :, lo - 1:hi - 1], src[:, :, lo:hi], ALU.add))
                cur = 0
                for step in range(g):
                    d = 1 << step
                    lo, hi = lo + d, hi - d
                    chain(pool.tensor_tensor(PS[1 - cur][:, :, lo:hi], PS[cur][:, :, lo - d:hi - d],
                                             PS[cur][:, :, lo + d:hi + d], ALU.add))
                    cur = 1 - cur
                inv = pool_inv[:, g, :]
                for s in range(2):
                    chain(pool.tensor_tensor(PS[1 - cur][:, s, PAD:PAD + SEG], PS[cur][:, s, PAD:PAD + SEG], inv,
                                             ALU.mult))
                diff = PD[:, g, :].rearrange("p (s n) -> p s n", s=2)
                pool.tensor_tensor(diff, PS[1 - cur][:, :, PAD:PAD + SEG], raw, ALU.subtract).then_inc(pool_d, 1)
                pool.wait_ge(pool_d, g + 1)

            pool.wait_ge(dve_out, part_of("d", first_job("norm", 4) - 1))
            pool.dma_start(ropeR[:, :, :], A["rope_ret"]).then_inc(ret_in, 16)
            pool.dma_start(perm[:, :], A["swap"]).then_inc(ret_in, 16)

            chain(pool.memset(neg_half[:, :], -0.5))
            with t.loop(pool, HEADS, head=1):
                t.add("head")
                pool.wait_ge(stat_ready, t.at("head"))
                pool.tensor_tensor(rstd[:, :], mv[:, :, 1], neg_half[:, :], ALU.pow).then_inc(rstd_ready, 1)

        @block.tensor
        def _(pe):
            t = Tally()

            def open_job(ahead=0):
                j = t.first("job") + ahead
                if j >= 4:
                    wait_job(j - 4)
                return bank[j % BANKS]

            def wait_job(j):
                m = j if t.reg is None or j >= t.start else j + t.per["job"]
                if "d" in JOBS[m][1]:
                    pe.wait_ge(dve_out, t.evacuated("d", j))
                else:
                    pe.wait_ge(act_out, t.evacuated("a", j))

            def wait_all():
                pe.wait_ge(dve_out, t.evacuated("d", t.first("job") - 1))
                pe.wait_ge(act_out, t.evacuated("a", t.first("job") - 1))

            def close_job(ins):
                ins.then_inc(acc_full, 1)
                t.add("job")

            def wait_panel():
                pe.wait_ge(split_lo, t.at("split", 1))
                return t.first("split")

            def wait_lo(k=1):
                t.add("lo", k)
                pe.wait_ge(lo_ready, t.at("lo"))

            def ada(layer, part):
                b = open_job()
                for kk in range(4):
                    n = ADA_AT[t.first("ada")]
                    pe.wait_ge(raw_in[n % RAW_SLOTS], arrivals(n))
                    raw = RAW[n % RAW_SLOTS]
                    for k2 in range(2):
                        for j in range(4):
                            ins = pe.matmul(b[32 * j:32 * j + 32, 0:256], cond[:, 2 * kk + k2, :],
                                            raw[:, k2 * 1024 + j * 256:k2 * 1024 + (j + 1) * 256],
                                            start=(kk == 0 and k2 == 0), stop=(kk == 3 and k2 == 1))
                    t.add("ada")
                    if kk < 3:
                        ins.then_inc(ada_used, 1)
                close_job(ins)
                b = open_job()
                wait_job(t.first("job") - 1)
                pe.transpose(b[:, 0:P], adarow[:, 0:P], ident[:, :]).then_inc(ada_used, 1)
                close_job(pe.transpose(b[:, P:2 * P], adarow[:, P:2 * P], ident[:, :]))

            def sum_squares(count, width, c0=0, jobs=None):
                b = open_job()
                for k in range(count):
                    if jobs is None:
                        t.add("sq")
                        pe.wait_ge(sq_ready, t.at("sq"))
                    else:
                        pe.wait_ge(act_out, part_of("a", jobs + k))
                    ins = pe.matmul(b[:, 0:width], ones[:, :], SQ[:, k % 2, c0:c0 + width],
                                    start=(k == 0), stop=(k == count - 1))
                    if k < count - 1:
                        ins.then_inc(ones_done, 1)
                close_job(ins)

            def sum_acc(width, c0=0, from_sbuf=True):
                t.add("acc", KD)
                t.add("sq", KD * from_sbuf)
                pe.wait_ge(acc_done, t.at("acc"))
                b = open_job()
                close_job(pe.matmul(b[:, 0:width], ones[:, :], ACC[:, c0:c0 + width], start=True, stop=True))

            pe.wait_ge(ident_ready, 1)
            pe.wait_ge(params_in, 16 * 10)
            for rows in (brows, grows):
                b = open_job()
                close_job(pe.transpose(b[:, 0:P], rows[:, :], ident[:, :]))
            pe.wait_ge(x_in, 32)
            for k in range(KD):
                b = open_job()
                for tt in range(4):
                    ins = pe.transpose(b[:, tt * P:(tt + 1) * P], xrows[:, tt, k * P:(k + 1) * P], ident[:, :])
                close_job(ins)
            sum_acc(T, from_sbuf=False)
            pe.wait_ge(cond_ready, 2)
            ada(0, SHIFT1)
            ada(0, SCALE1)

            def pair_of_jobs(ready, stats, movs):
                banks = [open_job(), open_job(1)]
                for k in range(KD):
                    ready(k)
                    for m in range(2):
                        mov = movs[m](k)
                        ins = mm3(pe, banks[m][:, 0:mov[0].shape[-1]], stats(k, m), mov, k == 0, k == KD - 1)
                        if k == KD - 1:
                            close_job(ins)

            def project(s, c0):
                b = open_job()
                for k in range(KD):
                    ins = mm3(pe, b[:, :], w8(WW, s, k, c0, P), (H_hi[:, k, :], H_lo[:, k, :]), k == 0, k == KD - 1)
                return ins

            def project_two(ready):
                s = wait_panel()
                full = lambda k: (H_hi[:, k, :], H_lo[:, k, :])
                pair_of_jobs(ready, lambda k, m: w8(WW, s, k, m * P, P), [full, full])
                t.add("split")

            project_two(lambda k: wait_lo())
            s = wait_panel()
            close_job(project(s, 0))
            close_job(project(s, NOPE))
            t.add("split")
            sum_squares(2, T, jobs=first_job("lora"))
            sum_squares(1, T, jobs=first_job("lora") + 2)
            for _ in range(2):
                s = wait_panel()
                close_job(project(s, 0))
                close_job(project(s, P))
                t.add("split")

            pe.wait_ge(split_lo, t.at("split", 2))
            uq, ukv = t.first("split") % 2, (t.first("split") + 1) % 2
            t.add("split", 2)
            wait_lo(3)
            v_cols = [w[ukv][:, 0:1024].rearrange("p (h x e) -> p h x e", h=HEADS, x=2)[:, :, 1, :] for w in WW]
            for tt in range(4):
                b = open_job()
                cs = slice(tt * P, (tt + 1) * P)
                close_job(mm3(pe, b[:, :], (QN_hi[:, 2, cs], QN_lo[:, 2, cs]), v_cols, True, True))

            def pair_qk(p):
                for hh in range(2):
                    b = open_job()
                    for k in range(2):
                        c0 = k * HEADS * QH + (2 * p + hh) * QH
                        ins = mm3(pe, b[0:QH, :], (W_hi[uq][:, c0:c0 + QH], W_lo[uq][:, c0:c0 + QH]),
                                  (QN_hi[:, k, :], QN_lo[:, k, :]), k == 0, k == 1)
                    close_job(ins)
                for hh in range(2):
                    b = open_job()
                    c0 = (2 * p + hh) * P
                    close_job(mm3(pe, b[:, :], (W_hi[ukv][:, c0:c0 + P], W_lo[ukv][:, c0:c0 + P]),
                                  (QN_hi[:, 2, :], QN_lo[:, 2, :]), True, True))

            def pair_scores(p):
                wait_lo(1)
                for tt in range(2):
                    for hh in range(2):
                        b = open_job()
                        cs = slice(LAT + tt * P, LAT + (tt + 1) * P)
                        close_job(mm3(pe, b[:, :], (Q_hi[0:QH, hh, cs], Q_lo[0:QH, hh, cs]),
                                      (K_hi[0:QH, hh, :], K_lo[0:QH, hh, :]), True, True))
                for tt in range(2):
                    b = open_job()
                    cs = slice(tt * P, (tt + 1) * P)
                    for hh in range(2):
                        ins = mm3(pe, b[:, hh * SEG:(hh + 1) * SEG], (Q_hi[0:QH, hh, cs], Q_lo[0:QH, hh, cs]),
                                  (K_hi[0:QH, hh, 0:SEG], K_lo[0:QH, hh, 0:SEG]), True, True)
                    close_job(ins)

            def pair_values(p):
                def turn(src, kt):
                    b = open_job()
                    for hh in range(2):
                        for tt in range(2):
                            c = (hh * 2 + tt) * P
                            ins = pe.transpose(b[:, c:c + P], src(tt, hh)[:, kt * P:(kt + 1) * P], ident[:, :])
                    close_job(ins)

                def values(tiles, slot0):
                    b = open_job()
                    for kt in tiles:
                        vs = slice(p * P, (p + 1) * P)
                        ins = mm3(pe, b[:, :], (V_hi[:, kt, vs], V_lo[:, kt, vs]),
                                  (PT_hi[:, slot0 + kt, :], PT_lo[:, slot0 + kt, :]), kt == tiles[0], kt == tiles[-1])
                    close_job(ins)

                wait_job(first_job("scores", p) + 5)
                for kt in range(2):
                    turn(lambda tt, hh: PROBC[:, tt, hh, :], kt)
                for kt in range(2):
                    turn(lambda tt, hh: PROB[:, tt * 2 + hh, :], kt)
                wait_job(t.first("job") - 3)
                values((0, 1), 2)
                for kt in range(2, 4):
                    turn(lambda tt, hh: PROB[:, tt * 2 + hh, :], kt)
                wait_job(t.first("job") - 1)
                values((0, 1, 2, 3), 0)

            pair_qk(0)
            wait_lo(1)
            for p in range(PAIRS):
                wait_job(first_job("k", p) + 1)
                pair_scores(p)
                if p + 1 < PAIRS:
                    pair_qk(p + 1)
                ada(0, (GATE1, SHIFT2, SCALE2, GATE2)[p])
                pair_values(p)
            wait_lo(POOL_GROUPS)
            for g in range(POOL_GROUPS):
                b = open_job()
                c0 = D + g * P
                ins = mm3(pe, b[:, :], (W_hi[ukv][:, c0:c0 + P], W_lo[ukv][:, c0:c0 + P]),
                          (PD_hi[:, g, :], PD_lo[:, g, :]), True, True)
                close_job(ins)

            last_value, pool_out = first_job("values", PAIRS - 1) + 7, first_job("pool_out")
            wait_job(last_value)
            project_two(lambda k: wait_job(pool_out + k - 4) if k >= 4 else None)
            for _ in range(3):
                s = wait_panel()
                close_job(project(s, 0))
                close_job(project(s, P))
                t.add("split")
            sum_acc(T, from_sbuf=False)
            ada(1, SHIFT1)
            sum_squares(KD, T)
            ada(1, SCALE1)

            def ffn(c0, last_layer):
                w = T - c0
                wait_all()
                lo0 = t.first("lo")
                t.add("lo", KD)
                for half in range(2):
                    hidden0 = t.first("job")
                    with t.loop(pe, 2, job=8, split=4):
                        for n in range(4):
                            s = wait_panel()
                            chunk = lambda k: (H_hi[:, k, c0:T], H_lo[:, k, c0:T])
                            if n == 0 and half == 0:
                                pair_of_jobs(lambda k: pe.wait_ge(lo_ready, lo0 + k + 1),
                                             lambda k, m: w8(WW, s, k, m * P, P), [chunk, chunk])
                                t.add("split")
                                continue
                            for m in range(2):
                                b = open_job()
                                for k in range(KD):
                                    ins = mm3(pe, b[:, 0:w], w8(WW, s, k, m * P, P), chunk(k), k == 0, k == KD - 1)
                                close_job(ins)
                            t.add("split")
                    sums0 = t.first("job")

                    def two_chunks():
                        banks = []
                        for kg in range(2):
                            s = wait_panel()
                            pe.wait_ge(dve_out, part_of("d", hidden0 + 8 * kg + 7))
                            for m in range(2):
                                if kg == 0:
                                    j = t.first("job")
                                    if m == 0:
                                        wait_job(j - 3)
                                    banks.append(ffn_bank(sums0, j + m))
                                for k in range(KD):
                                    ins = mm3(pe, banks[m][:, 0:w], w8(WW, s, k, m * P, P),
                                              (HID_hi[:, kg * 8 + k, c0:T], HID_lo[:, kg * 8 + k, c0:T]),
                                              kg == 0 and k == 0, kg == 1 and k == KD - 1)
                                if kg == 1:
                                    ins.then_inc(acc_full, 1)
                                    t.add("job")
                                elif m == 1:
                                    ins.then_inc(half_sum, 1)
                            t.add("split")

                    if last_layer and half:
                        for _ in range(4):
                            two_chunks()
                    else:
                        with t.loop(pe, 2, job=4, split=4):
                            two_chunks()
                            two_chunks()
                sum_acc(w, c0)

            ffn(0, False)
            ada(1, GATE1)
            sum_squares(KD, T)
            ada(1, SHIFT2)

            def qk_weights(s, k, m):
                at = (m * KD + k) * R_DK
                return [w[s % 2][:, at:at + R_DK] for w in WW]

            q_and_k = [lambda k: (H_hi[:, k, LAT:T], H_lo[:, k, LAT:T]), lambda k: (H_hi[:, k, :], H_lo[:, k, :])]

            def head_qk():
                s = wait_panel()
                for m, width in enumerate((SEG, T)):
                    b = open_job()
                    for k in range(KD):
                        ins = mm3(pe, b[:, 0:width], qk_weights(s, k, m), q_and_k[m](k), k == 0, k == KD - 1)
                    close_job(ins)
                t.add("split")

            def head_swap(qk_job):
                wait_job(qk_job)
                b = open_job()
                close_job(pe.matmul(b[:, :], perm[:, :], QK[:, 0:2, :], start=True, stop=True))

            def head_tokens(s, b, col, tile):
                for k in range(KD):
                    cs = slice(tile * P, (tile + 1) * P)
                    ins = mm3(pe, b[:, col:col + 256], (H_hi[:, k, cs], H_lo[:, k, cs]), w8(WW, s, k, 0, 256),
                              k == 0, k == KD - 1)
                return ins

            def head_v():
                s = wait_panel()
                for jj in range(2):
                    b = open_job()
                    head_tokens(s, b, 0, 2 * jj)
                    close_job(head_tokens(s, b, 256, 2 * jj + 1))
                t.add("split")

            def head_attend():
                wait_lo(1)
                for jj in range(2):
                    b = open_job()
                    for n in range(2):
                        part = 2 if jj == 0 else 1
                        ins = mm3(pe, b[:, n * SEG:(n + 1) * SEG],
                                  (QK_hi[:, part, n * P:(n + 1) * P], QK_lo[:, part, n * P:(n + 1) * P]),
                                  (QK_hi[:, 0, :], QK_lo[:, 0, :]), True, True)
                    close_job(ins)
                s = wait_panel()
                for tt in range(2):
                    b = open_job()
                    close_job(head_tokens(s, b, 0, 2 + tt))
                t.add("split")
                wait_lo(2)
                for tt in range(2):
                    b = open_job()
                    for kt in range(4):
                        cs = slice(tt * P, (tt + 1) * P)
                        ins = mm3(pe, b[:, 0:R_DV], (SA_hi[:, kt, cs], SA_lo[:, kt, cs]),
                                  (RV_hi[:, kt, :], RV_lo[:, kt, :]), kt == 0, kt == 3)
                    close_job(ins)

            def head_turn():
                t.add("rows")
                pe.wait_ge(rows_ready, t.at("rows"))
                b = open_job()
                for c in range(2):
                    for tt in range(2):
                        ins = pe.transpose(b[:, (c * 2 + tt) * P:(c * 2 + tt + 1) * P],
                                           ON[:, tt, c * P:(c + 1) * P], ident[:, :])
                close_job(ins)

            def head_out(turn_job):
                s = wait_panel()
                wait_job(turn_job)
                for jj in range(4):
                    b = open_job()
                    for n in range(2):
                        for c in range(2):
                            c0 = c * D + (2 * jj + n) * P
                            ins = mm3(pe, b[:, n * SEG:(n + 1) * SEG], [w[s % 2][:, c0:c0 + P] for w in WW],
                                      (YT_hi[:, c, :], YT_lo[:, c, :]), c == 0, c == 1)
                    close_job(ins)
                t.add("split")

            s = wait_panel()
            pair_of_jobs(lambda k: wait_lo(), lambda k, m: qk_weights(s, k, m), q_and_k)
            t.add("split")
            pe.wait_ge(ret_in, 32)
            head_swap(t.first("job") - 1)
            head_v()
            wait_all()
            with t.loop(pe, HEADS - 1, job=16, split=4, lo=3, rows=1):
                head_attend()
                head_qk()
                head_turn()
                head_swap(t.first("job") - 2)
                head_v()
                head_out(t.first("job") - 4)
            head_attend()
            ada(1, SCALE2)
            head_turn()
            head_out(t.first("job") - 1)
            sum_squares(KD, SEG, LAT)
            ada(1, GATE2)
            sum_squares(KD, SEG, LAT)
            ffn(LAT, True)

            for half in range(2):
                t.add("xr", 4)
                pe.wait_ge(x_ready, 3 * KD + t.at("xr"))
                for tt in range(2):
                    b = open_job()
                    for k in range(4):
                        ins = pe.transpose(b[:, k * P:(k + 1) * P],
                                           X[:, half * 4 + k, LAT + tt * P:LAT + (tt + 1) * P], ident[:, :])
                    close_job(ins)
            assert t.first("job") == len(JOBS) and t.first("split") == len(SPLIT_AT), (t.n, len(JOBS))

        @block.scalar
        def _(act):
            t = Tally()

            def split():
                act.wait_ge(acc_full, t.at("job"))
                s = t.first("split")
                n = SPLIT_AT[s]
                v = arrivals(n)
                if t.reg is not None:
                    v = t.reg * (16 * PLAN[n + RAW_SLOTS][1]) + v
                act.wait_ge(raw_in[n % RAW_SLOTS], v)
                act.activation(W_hi[s % 2][:, :], RAW[n % RAW_SLOTS][:, :], ACT.Copy).then_inc(split_hi, 1)
                t.add("split")

            def split_part(cols):
                s = t.first("split")
                n = SPLIT_AT[s]
                act.wait_ge(raw_in[n % RAW_SLOTS], arrivals(n))
                act.activation(W_hi[s % 2][:, 0:cols], RAW[n % RAW_SLOTS][:, 0:cols], ACT.Copy).then_inc(split_hi, 1)
                t.add("split")

            def job(banks=BANKS):
                t.add("job")
                act.wait_ge(acc_full, t.at("job"))
                return bank[(t.first("job") - 1) % banks]

            def skip(k=1):
                t.add("job", k)

            def done(ins):
                ins.then_inc(act_out, 1)

            def squares_free(n):
                if n >= 2:
                    act.wait_ge(ones_done, t.first("ones") + n - 1)

            def norm_root(width, n, c0=0):
                b = job()
                done(act.activation(R[:, c0:c0 + width], b[:, 0:width], ACT.Sqrt, bias=eps_col, scale=1.0 / n))

            def job_square(k):
                b = job()
                if k >= 2:
                    act.wait_ge(acc_done, t.first("acc") + k - 1)
                done(act.activation(SQ[:, k % 2, :], b[:, :], ACT.Square))

            def hi(out, in_):
                t.add("full")
                act.wait_ge(full_ready, t.at("full"))
                act.activation(out, in_, ACT.Copy).then_inc(hi_ready, 1)

            def ada():
                b = job()
                done(act.activation(adarow[:, :], b[:, 0:256], ACT.Copy))
                skip()

            def chunks_hi(layer, part_shift, segs, midway=None):
                for k in range(KD):
                    if k == KD // 2 and midway:
                        midway()
                    t.add("full")
                    act.wait_ge(full_ready, t.at("full"))
                    for s in segs:
                        cs = slice(s * SEG, (s + 1) * SEG)
                        ins = act.activation(H_hi[:, k, cs], TMP[:, k % 2, cs], ACT.Identity,
                                             bias=mod[:, layer, part_shift, k, s:s + 1])
                    ins.then_inc(hi_ready, 1)

            def squares_of_x(c0, n0):
                for k in range(KD):
                    act.wait_ge(x_ready, n0 + k + 1)
                    squares_free(k)
                    act.activation(SQ[:, k % 2, c0:T], X[:, k, c0:T], ACT.Square).then_inc(sq_ready, 1)
                t.add("ones", KD - 1)

            act.wait_ge(rows_zero, 2)
            act.dma_start(brows[0:96, :], A["b_ada"].rearrange("l (c p) -> (l c) p", p=P)).then_inc(params_in, 16)
            r = 0
            for name in ("g_mix_pre", "g_mix_post", "g_ffn_pre", "g_ffn_post", "g_q_lora", "g_kv_lora",
                         "pool_scale", "c", "c_ctx"):
                src = A[name] if len(A[name].shape) == 2 else A[name].rearrange("(a n) -> a n", a=1)
                rows = src.shape[0] * src.shape[1] // P
                act.dma_start(grows[r:r + rows, :], src.rearrange("l (c p) -> (l c) p", p=P)).then_inc(params_in, 16)
                r += rows
            act.dma_start(xrows[:, 0:2, :], A["ctx"][0].rearrange("(t p) n -> p t n", p=P)).then_inc(x_in, 16)
            act.dma_start(xrows[:, 2:4, :], A["x"][0].rearrange("(t p) n -> p t n", p=P)).then_inc(x_in, 16)
            skip(2)
            split_part(PANEL)
            act.wait_ge(cond_e, 1)
            act.activation(silu_e[:, :], gcol[:, 71:87], ACT.Exp, scale=-1.0).then_inc(cond_e, 1)
            for k in range(KD):
                job_square(k)
            t.add("acc", KD)
            act.wait_ge(rows_zero, 4)
            norm_root(T, D)
            ada()
            ada()
            chunks_hi(0, SHIFT1, (0, 1), midway=split)

            for k in range(2):
                b = job()
                done(act.activation(SQ[:, k, :], b[:, :], ACT.Square))
            split()
            b = job()
            act.wait_ge(ones_done, t.first("ones") + 1)
            done(act.activation(SQ[:, 0, :], b[:, :], ACT.Square))
            t.add("ones")
            b = job()
            done(act.activation(KR[NOPE:QH, :], b[NOPE:QH, :], ACT.Copy))
            norm_root(T, Q_LORA)
            split()
            for k in range(2):
                hi(QN_hi[:, k, :], LORA[:, k, :])
            norm_root(T, KV_LORA)
            hi(QN_hi[:, 2, :], LORA[:, 2, :])
            for g in range(POOL_GROUPS):
                b = job()
                done(act.activation(PRAW[:, g, :], b[:, :], ACT.Copy))
                if g == 1:
                    split_part(2 * HEADS * QH)
            split_part(D + POOL_GROUPS * P)

            def both(out, in_):
                done(act.activation(out, in_, ACT.Copy))

            t.add("full")
            act.wait_ge(full_ready, t.at("full"))
            act.activation(K_hi[NOPE:QH, 0, :], KR[NOPE:QH, :], ACT.Copy)
            act.activation(K_hi[NOPE:QH, 1, :], KR[NOPE:QH, :], ACT.Copy).then_inc(hi_ready, 1)
            for tt in range(4):
                both(V_hi[:, tt, :], job()[:, :])

            def pair_qk():
                for hh in range(2):
                    both(QF[0:QH, hh, :], job()[0:QH, :])
                for hh in range(2):
                    both(K_hi[0:NOPE, hh, :], job()[0:NOPE, :])
                hi(Q_hi[0:QH, :, :], QF[0:QH, :, :])

            def pair_softmax():
                for tt in range(2):
                    for hh in range(2):
                        b = job()
                        t.add("max")
                        act.wait_ge(rowmax, t.at("max"))
                        n = tt * 2 + hh
                        done(act.activation(PROB[:, n, :], b[:, :], ACT.Exp, bias=small[:, 1 + n:2 + n],
                                            scale=ATT_SCALE, accum_out=small[:, 9 + n:10 + n]))
                for tt in range(2):
                    b = job()
                    t.add("max")
                    act.wait_ge(rowmax, t.at("max"))
                    for hh in range(2):
                        n = 4 + tt * 2 + hh
                        ins = act.activation(PROBC[:, tt, hh, :], b[:, hh * SEG:(hh + 1) * SEG], ACT.Exp,
                                             bias=small[:, 1 + n:2 + n], scale=ATT_SCALE,
                                             accum_out=small[:, 9 + n:10 + n])
                    done(ins)

            def pair_values(p):
                def out(s):
                    b = job()
                    cs = slice(s * SEG, (s + 1) * SEG)
                    act.activation(H_hi[0:VD, p, cs], b[0:VD, 0:SEG], ACT.Copy)
                    both(H_hi[VD:P, p, cs], b[VD:P, SEG:T])

                if p == 0:
                    act.wait_ge(pool_d, POOL_GROUPS)
                for kt in (2, 3, 0, 1):
                    both(PT_hi[:, kt, :], job()[:, :])
                out(0)
                for kt in (2, 3):
                    both(PT_hi[:, kt, :], job()[:, :])
                out(1)

            pair_qk()
            for p in range(PAIRS):
                pair_softmax()
                if p + 1 < PAIRS:
                    pair_qk()
                else:
                    split()
                ada()
                pair_values(p)
            for g in range(POOL_GROUPS):
                act.activation(PD_hi[:, g, :], PD[:, g, :], ACT.Copy).then_inc(hi_ready, 1)
            for g in range(POOL_GROUPS):
                b = job()
                done(act.activation(H_hi[:, 4 + g, :], b[:, :], ACT.Copy, scale=gcol[:, 67 + g:68 + g]))

            split()
            for c in range(4):
                for m in range(2):
                    job_square(2 * c + m)
                split()
            t.add("acc", KD)
            norm_root(T, D)
            ada()
            squares_of_x(0, 0)
            norm_root(T, D)
            ada()

            def ffn(layer, c0, last_layer):
                segs = (0, 1) if c0 == 0 else (1,)
                w = T - c0
                chunks_hi(layer, SHIFT2, segs)
                for half in range(2):
                    with t.loop(act, 2, job=8, split=4, chain=8) as i:
                        for n in range(4):
                            for m in range(2):
                                b = job()
                                r = m % 2
                                act.wait_ge(dve_out, t.evacuated("d", t.first("job") - 3))
                                act.activation(TMP[:, r, c0:T], b[:, 0:w], ACT.Relu).then_inc(act_chain, 1)
                                t.add("chain")
                                act.wait_ge(act_chain, t.at("chain"))
                                done(act.activation(HID_hi[:, bass.ds(i * 8 + (2 * n + m), 1), c0:T],
                                                    TMP[:, r:r + 1, c0:T], ACT.Square))
                            split()

                    def two_chunks(i, c, more):
                        t.add("half_sum")
                        if more:
                            act.wait_ge(half_sum, t.at("half_sum"))
                            split()
                        for m in range(2):
                            t.add("job")
                            if half:
                                act.wait_ge(dve_out, t.evacuated("d", t.first("job") - 1))
                                act.wait_ge(acc_done, t.at("acc", -1))
                                y = Y[:, bass.ds(i * 4 + (2 * c + m), 1), c0:T] if t.reg is not None else \
                                    Y[:, 2 * c + m:2 * c + m + 1, c0:T]
                                act.activation(SQ[:, m:m + 1, c0:T], y, ACT.Square).then_inc(sq_ready, 1)
                                t.add("acc")
                        if more:
                            split()

                    if last_layer and half:
                        for c in range(4):
                            two_chunks(0, c, c < 3)
                    else:
                        extra = dict(acc=4) if half else {}
                        with t.loop(act, 2, job=4, split=4, half_sum=2, **extra) as i:
                            for c in range(2):
                                two_chunks(i, c, True)
                norm_root(w, D, c0)

            ffn(0, 0, False)
            ada()
            squares_of_x(0, KD)
            norm_root(T, D)
            ada()

            def decay_load(h):
                act.dma_start(DEC[:, :, :], A["decay"][h]).then_inc(decay_in, 16)

            def head_qk():
                both(QK[:, 0, :], job()[:, 0:SEG])
                b = job()
                act.activation(QK[:, 1, :], b[:, LAT:T], ACT.Copy)
                both(QK[:, 2, :], b[:, 0:SEG])
                split()

            def head_rotated():
                skip()
                hi(QK_hi[:, :, :], QK[:, :, :])

            def head_v():
                for jj in range(2):
                    both(RV_hi[:, 2 * jj:2 * jj + 2, :], job()[:, :])

            def head_attend(h, last):
                skip(2)
                for jj in range(2):
                    hi(SA_hi[:, 2 * jj:2 * jj + 2, :], SA[:, 2 * jj:2 * jj + 2, :])
                if not last:
                    act.dma_start(DEC[:, :, :], A["decay"][bass.ds(h + 1, 1)].rearrange("a p k n -> p (a k) n"))\
                       .then_inc(decay_in, 16)
                split()
                for tt in range(2):
                    done(act.activation(GE[:, tt, :], job()[:, 0:R_DV], ACT.Exp, scale=-1.0))
                split()
                skip(2)

            chunks_hi(1, SHIFT1, (0, 1))
            decay_load(0)
            head_qk()
            head_rotated()
            head_v()
            with t.loop(act, HEADS - 1, job=16, split=4, full=3) as h:
                head_attend(h, False)
                head_qk()
                both(YT_hi[:, :, :], job()[:, :])
                head_rotated()
                head_v()
                split()
                skip(4)
            head_attend(HEADS - 1, True)
            ada()
            both(YT_hi[:, :, :], job()[:, :])
            skip(4)
            split()
            for k in range(KD):
                if k == 0:
                    act.wait_ge(dve_out, part_of("d", t.first("job") - 1))
                squares_free(k)
                act.activation(SQ[:, k % 2, LAT:T], Y[:, k, LAT:T], ACT.Square).then_inc(sq_ready, 1)
            t.add("ones", KD - 1)
            norm_root(SEG, D, LAT)
            ada()
            squares_of_x(LAT, 2 * KD)
            norm_root(SEG, D, LAT)
            ffn(1, LAT, True)
            for half in range(2):
                for tt in range(2):
                    both(OUTR[:, tt, half * 512:(half + 1) * 512], job()[:, :])
            assert t.first("job") == len(JOBS) and t.first("split") == len(SPLIT_AT), (t.n, len(JOBS))

        @block.vector
        def _(dve):
            t = Tally()

            def split(cols=PANEL):
                s = t.first("split")
                t.add("split")
                dve.wait_ge(split_hi, t.at("split"))
                raw = RAW[SPLIT_AT[s] % RAW_SLOTS]
                dve.tensor_tensor(W_lo[s % 2][:, 0:cols], raw[:, 0:cols], W_hi[s % 2][:, 0:cols].bitcast(F32),
                                  ALU.subtract).then_inc(split_lo, 1)

            def job(banks=BANKS):
                j = t.first("job")
                t.add("job")
                if "a" in JOBS[j][1]:
                    dve.wait_ge(act_out, t.evacuated("a", j))
                else:
                    dve.wait_ge(acc_full, t.at("job"))
                return bank[j % banks]

            def skip(k=1):
                t.add("job", k)

            def done(ins):
                ins.then_inc(dve_out, 1)

            def chain(ins):
                ins.then_inc(dve_chain, 1)
                t.add("chain")

            def settle():
                dve.wait_ge(dve_chain, t.at("chain"))

            def lo(out, full, hi_part):
                t.add("hi")
                dve.wait_ge(hi_ready, t.at("hi"))
                dve.tensor_tensor(out, full, hi_part.bitcast(F32), ALU.subtract).then_inc(lo_ready, 1)
                t.add("lo")

            def job_lo(out, hi_part):
                b = job()
                done(dve.tensor_tensor(out, b[:, :], hi_part.bitcast(F32), ALU.subtract))

            def norm_recip(width, c0=0):
                job()
                done(dve.reciprocal(R[:, c0:c0 + width], R[:, c0:c0 + width]))
                dve.wait_ge(dve_out, part_of("d", t.first("job") - 1))

            def ada(layer, part):
                skip()
                b = job()
                rows = b[:, 0:256].rearrange("p (c j s) -> p c j s", c=2, s=32)
                bias = bcol[:, layer * 48 + part * 8:layer * 48 + part * 8 + 8]
                for c in range(2):
                    o = mod[:, layer, part, :, :].rearrange("p (j c) s -> p c j s", c=2)[:, c, :, :]
                    ins = dve.tensor_tensor(o, rows[:, c, :, 0:2],
                                            bias.rearrange("p (j c) -> p c j", c=2)[:, c, :].unsqueeze(2)
                                            .to_broadcast([P, 4, 2]), ALU.add)
                    if c == 0:
                        chain(ins)
                done(ins)
                dve.wait_ge(dve_out, part_of("d", t.first("job") - 1))
                which = int(part >= SHIFT2)
                m = mod[:, layer, part, :, :]
                if part in (SCALE1, SCALE2):
                    g = gcol[:, which * 32 + layer * 8:which * 32 + layer * 8 + 8].unsqueeze(2).to_broadcast([P, 8, 2])
                    chain(dve.scalar_tensor_tensor(out=pre_gain[:, layer, which, :, :], in0=m, scalar=1.0, in1=g,
                                                   op0=ALU.add, op1=ALU.mult))
                if part in (GATE1, GATE2):
                    c0 = 16 + which * 32 + layer * 8
                    g = gcol[:, c0:c0 + 8].unsqueeze(2).to_broadcast([P, 8, 2])
                    chain(dve.tensor_tensor(post_gain[:, layer, which, :, :], m, g, ALU.mult))

            def chunks_full(layer, which, part_shift, segs, midway=None):
                c0 = segs[0] * SEG
                settle()

                def lo_of(k):
                    t.add("hi")
                    dve.wait_ge(hi_ready, t.at("hi"))
                    for s in segs:
                        cs = slice(s * SEG, (s + 1) * SEG)
                        ins = dve.scalar_tensor_tensor(out=H_lo[:, k, cs], in0=TMP[:, k % 2, cs],
                                                       scalar=mod[:, layer, part_shift, k, s:s + 1],
                                                       in1=H_hi[:, k, cs].bitcast(F32), op0=ALU.add,
                                                       op1=ALU.subtract)
                    ins.then_inc(lo_ready, 1)
                    t.add("lo")

                for k in range(KD):
                    if k == KD // 2 and midway:
                        midway()
                    if k >= 2:
                        dve.wait_ge(lo_ready, t.at("lo"))
                    for s in segs:
                        cs = slice(s * SEG, (s + 1) * SEG)
                        ins = dve.scalar_tensor_tensor(out=TMP[:, k % 2, cs], in0=X[:, k, cs],
                                                       scalar=pre_gain[:, layer, which, k, s:s + 1],
                                                       in1=R[:, cs], op0=ALU.mult, op1=ALU.mult)
                    ins.then_inc(full_ready, 1)
                    if k >= 1:
                        lo_of(k - 1)
                lo_of(KD - 1)

            def update_x(layer, which, segs):
                c0 = segs[0] * SEG
                settle()
                for k in range(KD + 1):
                    if k < KD:
                        chain(dve.tensor_tensor(Y[:, k, c0:T], Y[:, k, c0:T], R[:, c0:T], ALU.mult))
                    if k >= 1:
                        dve.wait_ge(dve_chain, t.at("chain", -1 if k < KD else 0))
                        for s in segs:
                            cs = slice(s * SEG, (s + 1) * SEG)
                            ins = dve.scalar_tensor_tensor(out=X[:, k - 1, cs], in0=Y[:, k - 1, cs],
                                                           scalar=post_gain[:, layer, which, k - 1, s:s + 1],
                                                           in1=X[:, k - 1, cs], op0=ALU.mult, op1=ALU.add)
                        ins.then_inc(x_ready, 1)
                        t.add("x")
                dve.wait_ge(x_ready, t.at("x"))

            def clear_acc():
                chain(dve.memset(ACC[:, :], 0.0))
                settle()

            def keep_and_add(out, k):
                done(dve.tensor_copy(out[:, k, :], job()[:, :]))
                if t.first("acc"):
                    dve.wait_ge(acc_done, t.at("acc"))
                dve.tensor_tensor(ACC[:, :], ACC[:, :], SQ[:, k % 2, :], ALU.add).then_inc(acc_done, 1)
                t.add("acc")

            done(dve.tensor_copy(bcol[:, :], job()[:, 0:96]))
            b = job()
            done(dve.tensor_copy(gcol[:, :], b[:, 0:88]))
            dve.wait_ge(dve_out, 2)
            dve.sem_inc(cond_e, 1)
            clear_acc()
            split()
            for k in range(KD):
                keep_and_add(X, k)
            dve.wait_ge(cond_e, 2)
            chain(dve.tensor_scalar(silu_e[:, :], silu_e[:, :], 1.0, None, ALU.add))
            settle()
            chain(dve.reciprocal(silu_e[:, :], silu_e[:, :]))
            settle()
            dve.wait_ge(rows_zero, 3)
            for s, c0 in ((1, 0), (0, 8)):
                dve.tensor_tensor(cond[:, :, s], gcol[:, 71 + c0:79 + c0], silu_e[:, c0:c0 + 8],
                                  ALU.mult).then_inc(cond_ready, 1)
            norm_recip(T)
            ada(0, SHIFT1)
            ada(0, SCALE1)
            chunks_full(0, 0, SHIFT1, (0, 1), midway=split)

            for k in range(2):
                done(dve.tensor_copy(LORA[:, k, :], job()[:, :]))
            split()
            done(dve.tensor_copy(LORA[:, 2, :], job()[:, :]))
            skip()

            def lora(k, col):
                dve.scalar_tensor_tensor(out=LORA[:, k, :], in0=LORA[:, k, :], scalar=gcol[:, col:col + 1],
                                         in1=R[:, :], op0=ALU.mult, op1=ALU.mult).then_inc(full_ready, 1)

            norm_recip(T)
            split()
            lora(0, 64)
            lora(1, 65)
            lo(QN_lo[:, 0, :], LORA[:, 0, :], QN_hi[:, 0, :])
            lo(QN_lo[:, 1, :], LORA[:, 1, :], QN_hi[:, 1, :])
            norm_recip(T)
            lora(2, 66)
            lo(QN_lo[:, 2, :], LORA[:, 2, :], QN_hi[:, 2, :])

            def rotate(x, sw, cos, sin, shape):
                chain(dve.stream_shuffle(sw, x, [(n // 16) * 16 + (n + 8) % 16 for n in range(32)]))
                settle()
                chain(dve.tensor_tensor(sw, sw, sin, ALU.mult))
                chain(dve.tensor_tensor(x, x, cos, ALU.mult))
                settle()
                dve.tensor_tensor(x, x, sw, ALU.add).then_inc(full_ready, 1)

            dve.wait_ge(consts_in, 16)
            dve.wait_ge(act_out, part_of("a", first_job("kr")))
            split(2 * HEADS * QH)
            rotate(KR[NOPE:QH, :], SW[NOPE:QH, 0, :], ropeA[NOPE:QH, 0, :], ropeA[NOPE:QH, 1, :], None)
            t.add("hi")
            dve.wait_ge(hi_ready, t.at("hi"))
            dve.tensor_tensor(K_lo[NOPE:QH, 0, :], KR[NOPE:QH, :], K_hi[NOPE:QH, 0, :].bitcast(F32), ALU.subtract)
            dve.tensor_tensor(K_lo[NOPE:QH, 1, :], KR[NOPE:QH, :], K_hi[NOPE:QH, 1, :].bitcast(F32),
                              ALU.subtract).then_inc(lo_ready, 1)
            t.add("lo")
            skip(POOL_GROUPS)
            split(D + POOL_GROUPS * P)
            for tt in range(4):
                job_lo(V_lo[:, tt, :], V_hi[:, tt, :])

            def pair_qk():
                skip(2)
                for hh in range(2):
                    b = job()
                    done(dve.tensor_tensor(K_lo[0:NOPE, hh, :], b[0:NOPE, :], K_hi[0:NOPE, hh, :].bitcast(F32),
                                           ALU.subtract))
                q = QF[NOPE:QH, :, :]
                cos, sin = [ropeA[NOPE:QH, n, :].unsqueeze(1).to_broadcast([ROPE, 2, T]) for n in range(2)]
                rotate(q, SW[NOPE:QH, :, :], cos, sin, None)
                lo(Q_lo[0:QH, :, :], QF[0:QH, :, :], Q_hi[0:QH, :, :])

            def pair_softmax():
                j0 = t.first("job")

                def row_max(n):
                    dve.wait_ge(acc_full, j0 + n + 1)
                    b = bank[(j0 + n) % BANKS]
                    if n < 4:
                        mx, nm = small[:, 25 + n:26 + n], small[:, 1 + n:2 + n]
                        chain(dve.tensor_reduce(mx, b[:, :], AXX, ALU.max))
                    else:
                        mx, nm = small[:, 21 + 2 * n:23 + 2 * n], small[:, 2 * n - 3:2 * n - 1]
                        chain(dve.tensor_reduce(mx, b[:, :].rearrange("p (h k) -> p h k", h=2), AXX, ALU.max))
                    settle()
                    dve.tensor_scalar(nm, mx, -ATT_SCALE, None, ALU.mult).then_inc(rowmax, 1)

                def normalise(n):
                    job()
                    if n < 4:
                        chain(dve.reciprocal(small[:, 17 + n:18 + n], small[:, 9 + n:10 + n]))
                        settle()
                        done(dve.tensor_scalar(PROB[:, n, :], PROB[:, n, :], small[:, 17 + n:18 + n], None, ALU.mult))
                        return
                    c0 = 2 * n - 4
                    chain(dve.reciprocal(small[:, 17 + c0:19 + c0], small[:, 9 + c0:11 + c0]))
                    settle()
                    dve.tensor_scalar(PROBC[:, n - 4, 0, :], PROBC[:, n - 4, 0, :], small[:, 17 + c0:18 + c0], None,
                                      ALU.mult)
                    done(dve.tensor_scalar(PROBC[:, n - 4, 1, :], PROBC[:, n - 4, 1, :], small[:, 18 + c0:19 + c0],
                                           None, ALU.mult))

                row_max(0)
                for n in range(6):
                    if n < 5:
                        row_max(n + 1)
                    normalise(n)

            def pair_values(p):
                def out(s):
                    b = job()
                    cs = slice(s * SEG, (s + 1) * SEG)
                    dve.tensor_tensor(H_lo[0:VD, p, cs], b[0:VD, 0:SEG], H_hi[0:VD, p, cs].bitcast(F32), ALU.subtract)
                    done(dve.tensor_tensor(H_lo[VD:P, p, cs], b[VD:P, SEG:T], H_hi[VD:P, p, cs].bitcast(F32),
                                           ALU.subtract))

                for kt in (2, 3, 0, 1):
                    job_lo(PT_lo[:, kt, :], PT_hi[:, kt, :])
                out(0)
                for kt in (2, 3):
                    job_lo(PT_lo[:, kt, :], PT_hi[:, kt, :])
                out(1)

            pair_qk()
            for p in range(PAIRS):
                pair_softmax()
                if p + 1 < PAIRS:
                    pair_qk()
                else:
                    split()
                ada(0, (GATE1, SHIFT2, SCALE2, GATE2)[p])
                pair_values(p)
            for g in range(POOL_GROUPS):
                lo(PD_lo[:, g, :], PD[:, g, :], PD_hi[:, g, :])
            for g in range(POOL_GROUPS):
                b = job()
                done(dve.scalar_tensor_tensor(out=H_lo[:, 4 + g, :], in0=b[:, :], scalar=gcol[:, 67 + g:68 + g],
                                              in1=H_hi[:, 4 + g, :].bitcast(F32), op0=ALU.mult, op1=ALU.subtract))

            clear_acc()
            split()
            for c in range(4):
                for m in range(2):
                    keep_and_add(Y, 2 * c + m)
                split()
            norm_recip(T)
            update_x(0, 0, (0, 1))
            ada(1, SHIFT1)
            norm_recip(T)
            ada(1, SCALE1)

            def ffn(layer, c0, last_layer):
                segs = (0, 1) if c0 == 0 else (1,)
                w = T - c0
                chunks_full(layer, 1, SHIFT2, segs)
                for half in range(2):
                    with t.loop(dve, 2, job=8, split=4, chain=8) as i:
                        for n in range(4):
                            for m in range(2):
                                job()
                                r = m % 2
                                chain(dve.tensor_tensor(TMP[:, r:r + 1, c0:T], TMP[:, r:r + 1, c0:T],
                                                        TMP[:, r:r + 1, c0:T], ALU.mult))
                                settle()
                                c = bass.ds(i * 8 + (2 * n + m), 1)
                                done(dve.tensor_tensor(HID_lo[:, c, c0:T], TMP[:, r:r + 1, c0:T],
                                                       HID_hi[:, c, c0:T].bitcast(F32), ALU.subtract))
                            split()
                    sums0 = t.first("job")

                    if half:
                        dve.wait_ge(dve_out, part_of("d", t.first("job") - 1))
                        chain(dve.memset(ACC[:, :], 0.0))
                        settle()

                    def two_chunks(i, c, more):
                        if more:
                            split()
                        for m in range(2):
                            job()
                            b = ffn_bank(sums0, t.first("job") - 1)
                            y = Y[:, bass.ds(i * 4 + (2 * c + m), 1), c0:T] if t.reg is not None else \
                                Y[:, 2 * c + m:2 * c + m + 1, c0:T]
                            ps = b[:, 0:w].unsqueeze(1)
                            if not half:
                                done(dve.tensor_copy(y, ps))
                                continue
                            done(dve.tensor_tensor(y, ps, y, ALU.add))
                            t.add("sq")
                            dve.wait_ge(sq_ready, t.at("sq"))
                            dve.wait_ge(acc_done, t.at("acc"))
                            dve.tensor_tensor(ACC[:, c0:T], ACC[:, c0:T], SQ[:, m, c0:T], ALU.add).then_inc(acc_done, 1)
                            t.add("acc")
                        if more:
                            split()

                    if last_layer and half:
                        for c in range(4):
                            two_chunks(0, c, c < 3)
                    else:
                        extra = dict(acc=4, sq=4) if half else {}
                        with t.loop(dve, 2, job=4, split=4, **extra) as i:
                            for c in range(2):
                                two_chunks(i, c, True)
                norm_recip(w, c0)
                update_x(layer, 1, segs)

            t.add("sq", KD)
            ffn(0, 0, False)
            ada(1, GATE1)
            norm_recip(T)
            ada(1, SHIFT2)
            t.add("sq", KD)

            chunks_full(1, 0, SHIFT1, (0, 1))
            dve.memset(Y[:, :, LAT:T], 0.0).then_inc(y_zero, 1)
            dve.wait_ge(y_zero, 1)
            dve.wait_ge(ret_in, 32)

            def head_qk():
                skip(2)
                dve.wait_ge(act_out, t.evacuated("a", t.first("job") - 1))
                cos = ropeR[:, 0, :].unsqueeze(1).to_broadcast([P, 2, SEG])
                chain(dve.tensor_tensor(ROT[:, :, :], QK[:, 0:2, :], cos, ALU.mult))

            def head_rotated():
                sin = ropeR[:, 1, :].unsqueeze(1).to_broadcast([P, 2, SEG])
                settle()
                b = job()
                done(dve.tensor_tensor(QK[:, 0:2, :], b[:, :].rearrange("p (a n) -> p a n", a=2), sin, ALU.mult))
                dve.wait_ge(dve_out, t.evacuated("d", t.first("job") - 1))
                dve.tensor_tensor(QK[:, 0:2, :], QK[:, 0:2, :], ROT[:, :, :], ALU.add).then_inc(full_ready, 1)
                lo(QK_lo[:, :, :], QK[:, :, :], QK_hi[:, :, :])
                split()

            def head_v():
                for jj in range(2):
                    job_lo(RV_lo[:, 2 * jj:2 * jj + 2, :], RV_hi[:, 2 * jj:2 * jj + 2, :])

            def head_attend():
                t.add("decay")
                dve.wait_ge(decay_in, t.at("decay") * 16)
                for jj in range(2):
                    b = job()
                    s = SA[:, 2 * jj:2 * jj + 2, :]
                    done(dve.tensor_tensor(s, b[:, :].rearrange("p (a n) -> p a n", a=2),
                                           DEC[:, 2 * jj:2 * jj + 2, :], ALU.mult))
                    dve.wait_ge(dve_out, t.evacuated("d", t.first("job") - 1))
                    dve.sem_inc(full_ready, 1)
                for jj in range(2):
                    s = slice(2 * jj, 2 * jj + 2)
                    lo(SA_lo[:, s, :], SA[:, s, :], SA_hi[:, s, :])
                split()
                for tt in range(2):
                    gate = job()
                    chain(dve.tensor_scalar(GE[:, tt, :], GE[:, tt, :], 1.0, None, ALU.add))
                    settle()
                    chain(dve.reciprocal(GE[:, tt, :], GE[:, tt, :]))
                    if tt == 0:
                        settle()
                        done(dve.tensor_tensor(GS[:, tt, :], gate[:, 0:R_DV], GE[:, tt, :], ALU.mult))
                banks = [bank[(t.first("job") + tt) % BANKS] for tt in range(2)]
                for tt in range(2):
                    dve.wait_ge(acc_full, t.at("job", tt + 1))
                    chain(dve.bn_stats(stats[:, tt, :], banks[tt][:, 0:R_DV]))
                settle()
                done(dve.tensor_tensor(GS[:, 1, :], gate[:, 0:R_DV], GE[:, 1, :], ALU.mult))
                for tt in range(2):
                    chain(dve.bn_aggr(mv[:, tt, :], stats[:, tt, :]))
                settle()
                t.add("stat")
                dve.tensor_scalar(mv[:, :, 1], mv[:, :, 1], EPS, None, ALU.add).then_inc(stat_ready, 1)
                dve.wait_ge(rstd_ready, t.at("stat"))
                for tt in range(2):
                    job()
                    done(dve.tensor_scalar(ON[:, tt, :], banks[tt][:, 0:R_DV], mv[:, tt, 0:1], rstd[:, tt:tt + 1],
                                           ALU.subtract, ALU.mult))
                dve.wait_ge(dve_out, t.evacuated("d", t.first("job") - 1))
                dve.tensor_tensor(ON[:, :, :], ON[:, :, :], GS[:, :, :], ALU.mult).then_inc(rows_ready, 1)
                split()

            def head_out():
                for jj in range(4):
                    b = job()
                    y = Y[:, 2 * jj:2 * jj + 2, LAT:T]
                    done(dve.tensor_tensor(y, b[:, :].rearrange("p (a n) -> p a n", a=2), y, ALU.add))

            head_qk()
            head_rotated()
            head_v()
            with t.loop(dve, HEADS - 1, job=16, split=4, chain=9, hi=3, lo=3, decay=1, stat=1):
                head_attend()
                head_qk()
                job_lo(YT_lo[:, :, :], YT_hi[:, :, :])
                head_rotated()
                head_v()
                split()
                head_out()
            head_attend()
            ada(1, SCALE2)
            job_lo(YT_lo[:, :, :], YT_hi[:, :, :])
            head_out()
            split()
            norm_recip(SEG, LAT)
            update_x(1, 0, (1,))
            t.add("sq", 2 * KD)
            ada(1, GATE2)
            norm_recip(SEG, LAT)
            ffn(1, LAT, True)
            skip(4)
            assert t.first("job") == len(JOBS) and t.first("split") == len(SPLIT_AT), (t.n, len(JOBS))


def tables():
    n = np.arange(SEG)
    row, col = (n // 64).astype(np.float64), (n % 64).astype(np.float64)

    def rotary(width):
        d = width // 2
        f = 10000.0 ** (-np.arange(0, d, 2) / d)
        angle = [pos[None, :] * f[:, None] for pos in (row, col)]
        cos = np.concatenate([np.concatenate([np.cos(a)] * 2) for a in angle])
        sin = np.concatenate([np.concatenate([-np.sin(a), np.sin(a)]) for a in angle])
        return cos, sin

    cos, sin = rotary(ROPE)
    att = np.zeros((ROPE, 2, T))
    att[:, 0, :SEG] = 1.0
    att[:, 0, LAT:], att[:, 1, LAT:] = cos, sin
    ret = np.stack(rotary(R_DK), axis=1)
    swap = np.zeros((P, P))
    for a in range(P):
        swap[(a // 64) * 64 + (a + 32) % 64, a] = 1.0
    inv = np.zeros((P, POOL_GROUPS, SEG))
    for g in range(POOL_GROUPS):
        w = 2 << g
        inv[:, g, :] = 1.0 / (np.clip(n + w // 2, 0, SEG) - np.clip(n - w // 2, 0, SEG))
    logs = np.log1p(-np.exp2(-5.0 - np.arange(HEADS)))
    decay = np.zeros((HEADS, P, 4, SEG))
    q = n[None, :]
    for h in range(HEADS):
        f, b = logs[h], logs[HEADS - 1 - h]
        key = n[:, None]
        context = np.exp(f * (q + SEG - key)) + np.exp(b * (SEG - q + key))
        latent = np.where(key <= q, np.exp(f * np.maximum(q - key, 0)), np.exp(b * np.maximum(key - q, 0)))
        both = np.concatenate([context, latent]) * R_DK ** -0.5
        decay[h] = both.reshape(4, P, SEG).transpose(1, 0, 2)
    return {name: np.ascontiguousarray(a, dtype=np.float32) for name, a in
            dict(rope_att=att, rope_ret=ret, swap=swap, pool_inv=inv, decay=decay).items()}


INPUTS = ["x", "c", "ctx", "c_ctx", "w_ada", "b_ada", "g_mix_pre", "g_mix_post", "g_ffn_pre", "g_ffn_post",
          "w_ffn_in", "w_ffn_out", "w_in_even", "g_q_lora", "g_kv_lora", "w_uq", "w_ukv", "w_pool", "pool_scale",
          "w_out_even", "w_in_odd", "w_out_odd"]


def kernel(**inputs):
    import concourse.bacc as bacc
    from concourse.bass_utils import run_bass_kernel_spmd

    nc = bacc.Bacc("TRN2", target_bir_lowering=False, num_devices=1)
    arrays = {name: np.ascontiguousarray(inputs[name]) for name in INPUTS}
    arrays.update(tables())
    arrays = {f"in_{name}": a for name, a in arrays.items()}
    A = {name[3:]: nc.dram_tensor(name, a.shape, mybir.dt.from_np(a.dtype), kind="ExternalInput").ap()
         for name, a in arrays.items()}
    out = nc.dram_tensor("latent_out", (1, SEG, D), F32, kind="ExternalOutput").ap()
    build(nc, A, out)
    result = run_bass_kernel_spmd(nc, [arrays], core_ids=[0])
    return result.results[0]["latent_out"]
```

```python
from contextlib import ExitStack, contextmanager

import numpy as np

import concourse.bass as bass
from concourse import mybir

F32 = mybir.dt.float32
F32R = mybir.dt.float32r
ALU = mybir.AluOpType
ACT = mybir.ActivationFunctionType
AXX = mybir.AxisListType.X

P = 128
D = 1024
KD = D // P
SEG = 256
T = 2 * SEG
LAT = SEG
EPS = 1e-6

Q_LORA, KV_LORA, ROPE, NOPE, VD = 256, 128, 32, 64, 64
HEADS = 8
PAIRS = HEADS // 2
QH = NOPE + ROPE
ATT_SCALE = float(QH) ** -0.5
POOL_GROUPS = 4
POOL0 = Q_LORA + KV_LORA + ROPE
PAD = 8

R_DK, R_DV = 128, 256
R_Q0, R_K0, R_V0, R_G0 = 0, HEADS * R_DK, 2 * HEADS * R_DK, 2 * HEADS * R_DK + HEADS * R_DV

DFF = 4 * D
HALF = DFF // 2
HC = HALF // P
PANEL_COLS = 256
PANEL = KD * PANEL_COLS
RAW_SLOTS = 4
BANKS = 8

SHIFT1, SCALE1, GATE1, SHIFT2, SCALE2, GATE2 = range(6)


def panel_plan():
    ada, one, two = ("ada", 1), ("split", 1), ("split", 2)
    plan = [ada] * 4 + [one] + [ada] * 4 + [one] * 4 + [two]
    plan += [ada] * 4 * (PAIRS - 1) + [one] + [ada] * 4
    plan += [one] * 5
    plan += [ada] * 8
    plan += [one] * 30
    plan += [two, one]
    plan += [ada] * 8
    plan += [one, two, one, one] * (HEADS - 1)
    plan += [one, two, one] + [ada] * 4 + [one] + [ada] * 4
    plan += [one] * 30
    return plan


PLAN = panel_plan()
SPLIT_AT = [n for n, (kind, _) in enumerate(PLAN) if kind == "split"]
ADA_AT = [n for n, (kind, _) in enumerate(PLAN) if kind == "ada"]


def arrivals(n):
    return 16 * sum(PLAN[m][1] for m in range(n % RAW_SLOTS, n + 1, RAW_SLOTS))


def job_plan():
    jobs = [("params", "d")] * 2 + [("x", "ad")] * KD + [("norm", "ad")]
    ada = [("ada", "a"), ("ada", "d")]
    jobs += ada * 2
    jobs += [("lora", "ad")] * 3 + [("kr", "a")] + [("norm", "ad")] * 2 + [("pool_in", "a")] * POOL_GROUPS
    q, k, scores = [("q", "a")] * 2, [("k", "ad")] * 2, [("scores", "ad")] * 6
    turn, values = [("turn", "ad")], [("values", "ad")]
    jobs += q + [("v", "ad")] * 4 + k + scores + q + k + ada
    for p in range(1, PAIRS - 1):
        jobs += scores + turn * 4 + q + k + values + turn * 2 + ada + values
    jobs += scores + turn * 4 + ada + values + turn * 2 + [("pool_out", "ad")] * POOL_GROUPS + values
    jobs += turn * 4 + values + turn * 2 + values
    jobs += [("mix_out", "ad")] * KD + [("norm", "ad")]
    jobs += ada + [("norm", "ad")] + ada
    ffn = ([("hidden", "ad")] * HC + [("ffn_out", "d")] * KD) * 2 + [("norm", "ad")]
    jobs += ffn + ada + [("norm", "ad")] + ada
    r_qk, swap, r_v = [("r_qk", "a")] * 2, [("r_swap", "d")], [("r_v", "ad")] * 2
    attend = [("r_scores", "d")] * 2 + [("r_gate", "ad")] * 2 + [("r_values", "d")] * 2
    turn, r_out = [("r_turn", "ad")], [("r_out", "d")] * 4
    jobs += r_qk + swap + r_v + (attend + r_qk + turn + swap + r_v + r_out) * (HEADS - 1)
    jobs += attend + ada + turn + r_out
    jobs += [("norm", "ad")] + ada + [("norm", "ad")] + ffn
    jobs += [("rows", "a")] * 4
    return jobs


JOBS = job_plan()


def part_of(engine, j):
    return sum(engine in JOBS[m][1] for m in range(j + 1))


def first_job(stage, nth=0):
    starts = [m for m in range(len(JOBS)) if JOBS[m][0] == stage and (m == 0 or JOBS[m - 1][0] != stage)]
    return starts[nth]


class Tally:

    def __init__(self):
        self.n = {}
        self.reg = None
        self.per = {}

    def at(self, name, more=0):
        v = self.n.get(name, 0) + more
        if self.reg is not None and self.per.get(name, 0):
            return self.reg * self.per[name] + v
        return v

    def evacuated(self, engine, j):
        if self.reg is None:
            return part_of(engine, j)
        rounds_jobs = self.per["job"]
        per = part_of(engine, self.start + rounds_jobs - 1) - part_of(engine, self.start - 1)
        v = part_of(engine, j) if j >= self.start else part_of(engine, j + rounds_jobs) - per
        return self.reg * per + v if per else v

    def first(self, name):
        return self.n.get(name, 0)

    def add(self, name, k=1):
        self.n[name] = self.n.get(name, 0) + k

    @contextmanager
    def loop(self, eng, rounds, **per):
        start = dict(self.n)
        with eng.Fori(0, rounds) as i:
            self.reg, self.per, self.start = i, per, start.get("job", 0)
            yield i
            self.reg = None
        for name in set(self.n) | set(per):
            added = self.n.get(name, 0) - start.get(name, 0)
            assert added == per.get(name, 0), (name, added, per.get(name, 0))
            self.n[name] = start.get(name, 0) + rounds * added


def mm3(pe, out, stat, mov, first, last):
    pe.matmul(out, stat[0], mov[0], start=first, stop=False)
    pe.matmul(out, stat[0], mov[1], start=False, stop=False)
    return pe.matmul(out, stat[1], mov[0], start=False, stop=last)


def build(nc, A, out):
    with ExitStack() as ctx:
        base = [16512]

        def place(name, shape, dt, at=None):
            size = 4 * int(np.prod(shape[1:]))
            if at is None:
                at = base[0]
                base[0] += (size + 31) // 32 * 32
            return nc.alloc_sbuf_tensor_at(name, shape, dt, offset=at)

        X = place("X", [P, KD, T], F32)
        h_hi_at = base[0]
        H_hi = place("H_hi", [P, KD, T], F32R)
        h_lo_at = base[0]
        H_lo = place("H_lo", [P, KD, T], F32R)
        RAW = [place(f"RAW{n}", [P, PANEL], F32) for n in range(RAW_SLOTS)]
        W_hi = [place(f"W_hi{n}", [P, PANEL], F32R) for n in range(2)]
        W_lo = [place(f"W_lo{n}", [P, PANEL], F32R) for n in range(2)]
        big = base[0]
        base[0] += 80 * 1024
        sq_at = base[0]
        SQ = place("SQ", [P, 2, T], F32)
        tmp_at = base[0]
        TMP = place("TMP", [P, 2, T], F32)
        ACC = place("ACC", [P, T], F32, tmp_at + 4 * T)
        R = place("R", [P, T], F32)
        ident = place("ident", [P, P], F32)
        ones = place("ones", [P, P], F32)
        bcol = place("bcol", [P, 96], F32)
        gcol = place("gcol", [P, 88], F32)
        cond = place("cond", [P, KD, 32], F32)
        mod = place("mod", [P, 2, 6, KD, 2], F32)
        pre_gain = place("pre_gain", [P, 2, 2, KD, 2], F32)
        post_gain = place("post_gain", [P, 2, 2, KD, 2], F32)
        adarow = place("adarow", [P, 256], F32)
        small = place("small", [P, 48], F32)
        assert base[0] <= nc.sbuf_usable_end, base[0]
        eps_col = small[:, 0:1]

        xrows = place("xrows", [P, 4, D], F32, big + 16384)
        brows = place("brows", [P, P], F32, big + 32768)
        grows = place("grows", [P, P], F32, big + 32768 + 512)
        silu_e = place("silu_e", [P, 16], F32, big + 32768 + 1024)
        at = [big]

        def region(name, shape, dt):
            t = place(name, shape, dt, at[0])
            at[0] += (4 * int(np.prod(shape[1:])) + 31) // 32 * 32
            return t

        q_at = at[0]
        Q_hi, Q_lo = region("Q_hi", [P, 2, T], F32R), region("Q_lo", [P, 2, T], F32R)
        K_hi, K_lo = region("K_hi", [P, 2, T], F32R), region("K_lo", [P, 2, T], F32R)
        V_hi, V_lo = region("V_hi", [P, 4, T], F32R), region("V_lo", [P, 4, T], F32R)
        QN_hi, QN_lo = region("QN_hi", [P, 3, T], F32R), region("QN_lo", [P, 3, T], F32R)
        lora_at = at[0]
        PROB = region("PROB", [P, 4, T], F32)
        PROBC = region("PROBC", [P, 2, 2, SEG], F32)
        pt_at = at[0]
        PT_hi, PT_lo = region("PT_hi", [P, 4, T], F32R), region("PT_lo", [P, 4, T], F32R)
        QF = region("QF", [P, 2, T], F32)
        SW = region("SW", [P, 2, T], F32)
        assert at[0] <= big + 80 * 1024
        LORA = place("LORA", [P, 3, T], F32, lora_at)
        KR = place("KR", [P, T], F32, lora_at + 12 * T)
        ropeA = place("ropeA", [P, 2, SEG], F32, tmp_at)
        PROBS = [place("PROB_even", [P, 4, T], F32, h_hi_at + 16 * T), PROB]
        PROBCS = [PROBC, place("PROBC_odd", [P, 2, 2, SEG], F32, sq_at)]
        WIDE = SEG + 2 * PAD
        PRAW = place("PRAW", [P, POOL_GROUPS, 2, WIDE], F32, pt_at)
        PS = [place(f"PS{n}", [P, 2, WIDE], F32, pt_at + (POOL_GROUPS + n) * 8 * WIDE) for n in range(2)]
        PD = place("PD", [P, POOL_GROUPS, T], F32, h_lo_at + 16 * T)
        pool_inv = place("pool_inv", [P, POOL_GROUPS, SEG], F32, sq_at)
        PD_hi, PD_lo = place("PD_hi", [P, 4, T], F32R, q_at), place("PD_lo", [P, 4, T], F32R, q_at + 16 * T)
        HID_hi, HID_lo = place("HID_hi", [P, HC, T], F32R, big), place("HID_lo", [P, HC, T], F32R, big + 32768)
        Y = place("Y", [P, KD, T], F32, big + 65536)
        at[0] = big
        QK = region("QK", [P, 3, SEG], F32)
        ROT = region("ROT", [P, 2, SEG], F32)
        QK_hi, QK_lo = region("QK_hi", [P, 3, SEG], F32R), region("QK_lo", [P, 3, SEG], F32R)
        ropeR = region("ropeR", [P, 2, SEG], F32)
        perm = region("perm", [P, P], F32)
        DEC = region("DEC", [P, 4, SEG], F32)
        RV_hi, RV_lo = region("RV_hi", [P, 4, SEG], F32R), region("RV_lo", [P, 4, SEG], F32R)
        SA = region("SA", [P, 4, SEG], F32)
        SA_hi, SA_lo = region("SA_hi", [P, 4, SEG], F32R), region("SA_lo", [P, 4, SEG], F32R)
        GE = region("GE", [P, 2, SEG], F32)
        GS = region("GS", [P, 2, SEG], F32)
        ON = region("ON", [P, 2, SEG], F32)
        YT_hi, YT_lo = region("YT_hi", [P, 2, SEG], F32R), region("YT_lo", [P, 2, SEG], F32R)
        stats = region("stats", [P, 2, 6], F32)
        mv = region("mv", [P, 2, 2], F32)
        rstd = region("rstd", [P, 2], F32)
        neg_half = region("neg_half", [P, 2], F32)
        assert at[0] <= big + 65536
        OUTR = place("OUTR", [P, 2, D], F32, big)

        bank = [ctx.enter_context(nc.psum_tensor(f"bank{n}", [P, 512], F32)) for n in range(BANKS)]

        def sem(name):
            return ctx.enter_context(nc.semaphore(name))

        raw_in = [sem(f"raw_in{n}") for n in range(RAW_SLOTS)]
        split_hi, split_lo = sem("split_hi"), sem("split_lo")
        half_sum, ada_used = sem("half_sum"), sem("ada_used")
        acc_full, act_out, dve_out = sem("acc_full"), sem("act_out"), sem("dve_out")
        full_ready, hi_ready, lo_ready = sem("full_ready"), sem("hi_ready"), sem("lo_ready")
        modulated = sem("modulated")
        sq_ready, ones_done, acc_done = sem("sq_ready"), sem("ones_done"), sem("acc_done")
        x_ready, rowmax = sem("x_ready"), sem("rowmax")
        params_in, x_in, consts_in, ret_in = sem("params_in"), sem("x_in"), sem("consts_in"), sem("ret_in")
        inv_in, rows_zero, ident_ready = sem("inv_in"), sem("rows_zero"), sem("ident_ready")
        cond_e, cond_ready = sem("cond_e"), sem("cond_ready")
        act_chain, dve_chain, pool_chain = sem("act_chain"), sem("dve_chain"), sem("pool_chain")
        pool_d = sem("pool_d")
        rows_ready = sem("rows_ready")
        decay_in, stat_ready, rstd_ready, y_zero = sem("decay_in"), sem("stat_ready"), sem("rstd_ready"), sem("y_zero")
        out_done = sem("out_done")

        def by_chunk(w):
            return w.rearrange("(k p) n -> p k n", p=P)

        ada_v = [by_chunk(A["w_ada"][l]) for l in range(2)]
        in_even = by_chunk(A["w_in_even"][0])
        out_even = by_chunk(A["w_out_even"][0])
        in_odd = by_chunk(A["w_in_odd"][0])
        out_odd = by_chunk(A["w_out_odd"][0])
        ffn_in = [by_chunk(A["w_ffn_in"][l]) for l in range(2)]
        ffn_out = [by_chunk(A["w_ffn_out"][l]) for l in range(2)]
        IN_PANELS = (0, 256, POOL0, POOL0 + 256)

        def w8(pair, s, k, c0, n):
            at = k * PANEL_COLS + c0
            return pair[0][s % 2][:, at:at + n], pair[1][s % 2][:, at:at + n]

        WW = (W_hi, W_lo)
        HH = (H_hi, H_lo)

        def h_buffer(k):
            return (TMP, SQ)[k % 4 // 2][:, k % 2, :]

        def ffn_bank(first, j):
            return bank[(first + (j - first) % 4) % BANKS]

        block = ctx.enter_context(nc.Block())

        @block.sync
        def _(sp):
            t = Tally()

            def load(*pairs):
                n = t.first("panel")
                slot = n % RAW_SLOTS
                kind, dmas = PLAN[n]
                assert dmas == len(pairs)
                if n >= RAW_SLOTS:
                    splits = sum(m <= n - RAW_SLOTS for m in SPLIT_AT)
                    adas = sum(m <= n - RAW_SLOTS for m in ADA_AT)
                    if t.reg is not None:
                        before = [PLAN[m][0] for m in range(n - RAW_SLOTS, n)]
                        assert before[0] == "ada" or "ada" not in before
                        splits = t.reg * RAW_SLOTS + (t.first("split") - 3)
                        sp.wait_ge(split_lo, splits)
                    elif splits:
                        sp.wait_ge(split_lo, splits)
                    if adas:
                        sp.wait_ge(ada_used, adas)
                for c0, src in pairs:
                    size = int(np.prod(src.shape[1:]))
                    dst = RAW[slot][:, c0:c0 + size]
                    if len(src.shape) == 3:
                        dst = dst.rearrange("p (k n) -> p k n", k=src.shape[1])
                    sp.dma_start(dst, src).then_inc(raw_in[slot], 16)
                t.add("panel")
                t.add("split", kind == "split")

            def ada(layer, part):
                for kk in range(4):
                    load((0, ada_v[layer][:, 2 * kk:2 * kk + 2, part * D:(part + 1) * D]))

            def ffn_panel(layer, n):
                load((0, ffn_in[layer][:, :, n * 256:(n + 1) * 256]))

            def ffn(layer, last):
                for n in range(2, 8):
                    ffn_panel(layer, n)
                for half in range(2):
                    if half:
                        with t.loop(sp, 2, panel=4, split=4) as i:
                            for n in range(4):
                                load((0, ffn_in[layer][:, :, bass.ds(i * 1024 + (HALF + n * 256), 256)]))
                    if last and half:
                        for c in range(4):
                            for kg in range(2):
                                load((0, ffn_out[layer][:, 16 * half + 8 * kg:16 * half + 8 * kg + 8,
                                                        c * 256:(c + 1) * 256]))
                        continue
                    with t.loop(sp, 2, panel=4, split=4) as i:
                        for n in range(4):
                            k0 = 16 * half + 8 * (n % 2)
                            load((0, ffn_out[layer][:, k0:k0 + 8, bass.ds(i * 512 + (n // 2) * 256, 256)]))

            def head_qk(h):
                q = in_odd[:, :, bass.ds(h * R_DK + R_Q0, R_DK)] if not isinstance(h, int) else \
                    in_odd[:, :, R_Q0 + h * R_DK:R_Q0 + (h + 1) * R_DK]
                k = in_odd[:, :, bass.ds(h * R_DK + R_K0, R_DK)] if not isinstance(h, int) else \
                    in_odd[:, :, R_K0 + h * R_DK:R_K0 + (h + 1) * R_DK]
                load((0, q), (KD * R_DK, k))

            for n, name in enumerate(("ctx", "x")):
                sp.dma_start(xrows[:, 2 * n:2 * n + 2, :], A[name][0].rearrange("(t p) n -> p t n", p=P))\
                  .then_inc(x_in, 16)
            sp.wait_ge(params_in, 16 * 10)
            ada(0, SHIFT1)
            load((0, in_even[:, :, 0:256]))
            ada(0, SCALE1)
            for c0 in IN_PANELS[1:]:
                load((0, in_even[:, :, c0:c0 + 256]))
            load((0, by_chunk(A["w_uq"][0])))
            load((0, by_chunk(A["w_ukv"][0])), (D, A["w_pool"][0].rearrange("g p n -> p g n")))
            for part in (GATE1, SHIFT2, SCALE2):
                ada(0, part)
            load((0, out_even[:, :, 0:256]))
            ada(0, GATE2)
            for c in range(1, 4):
                load((0, out_even[:, :, c * 256:(c + 1) * 256]))
            ffn_panel(0, 0)
            ffn_panel(0, 1)
            ada(1, SHIFT1)
            ada(1, SCALE1)
            ffn(0, False)

            def head_cols(h, first):
                c = bass.ds(h * R_DV + first, R_DV) if not isinstance(h, int) else \
                    slice(first + h * R_DV, first + (h + 1) * R_DV)
                load((0, in_odd[:, :, c]))

            head_qk(0)
            head_cols(0, R_V0)
            ada(1, GATE1)
            ada(1, SHIFT2)
            with t.loop(sp, HEADS - 1, panel=4, split=4) as h:
                head_cols(h, R_G0)
                head_qk(h + 1)
                head_cols(h + 1, R_V0)
                load((0, out_odd[:, bass.ds(h * 2, 2), :]))
            head_cols(HEADS - 1, R_G0)
            load((0, out_odd[:, 2 * HEADS - 2, :]), (D, out_odd[:, 2 * HEADS - 1, :]))
            ffn_panel(1, 0)
            ada(1, SCALE2)
            ffn_panel(1, 1)
            ada(1, GATE2)
            ffn(1, True)
            for n in range(4):
                sp.wait_ge(act_out, part_of("a", first_job("rows") + n))
                tt, half = n % 2, n // 2
                sp.dma_start(out[0, tt * P:(tt + 1) * P, half * 512:(half + 1) * 512],
                             OUTR[:, tt, half * 512:(half + 1) * 512]).then_inc(out_done, 16)
            sp.wait_ge(out_done, 64)

        @block.gpsimd
        def _(pool):
            t = Tally()

            def chain(ins):
                ins.then_inc(pool_chain, 1)
                t.add("chain")
                pool.wait_ge(pool_chain, t.at("chain"))

            pool.memset(brows[:, :], 0.0).then_inc(rows_zero, 1)
            pool.memset(grows[:, :], 0.0).then_inc(rows_zero, 1)
            pool.memset(cond[:, :, :], 0.0).then_inc(rows_zero, 1)
            pool.memset(eps_col, EPS).then_inc(rows_zero, 1)
            pool.memset(ones[:, :], 1.0).then_inc(rows_zero, 1)
            chain(pool.memset(ident[:, :], 0.0))
            pool.affine_select(out=ident[:, :], in_=ident[:, :], compare_op=ALU.not_equal, fill=1.0, base=0,
                               pattern=[[-1, P]], channel_multiplier=1).then_inc(ident_ready, 1)

            pool.memset(PRAW[:, :, :, :], 0.0).then_inc(rows_zero, 1)
            pool.wait_ge(lo_ready, KD)
            pool.dma_start(ropeA[NOPE:QH, :, :], A["rope_att"]).then_inc(consts_in, 16)
            pool.wait_ge(act_out, part_of("a", first_job("norm", 1) + 1))
            pool.dma_start(pool_inv[:, :, :], A["pool_inv"]).then_inc(inv_in, 16)
            pool.wait_ge(inv_in, 16)
            for n, g in enumerate((1, 0, 3, 2)):
                pool.wait_ge(act_out, part_of("a", first_job("pool_in") + g))
                raw = PRAW[:, g, :, :]
                lo, hi = 1, WIDE - 1
                chain(pool.tensor_tensor(PS[0][:, :, lo:hi], raw[:, :, lo - 1:hi - 1], raw[:, :, lo:hi], ALU.add))
                cur = 0
                for step in range(g):
                    d = 1 << step
                    lo, hi = lo + d, hi - d
                    chain(pool.tensor_tensor(PS[1 - cur][:, :, lo:hi], PS[cur][:, :, lo - d:hi - d],
                                             PS[cur][:, :, lo + d:hi + d], ALU.add))
                    cur = 1 - cur
                inv = pool_inv[:, g, :].unsqueeze(1).to_broadcast([P, 2, SEG])
                chain(pool.tensor_tensor(PS[1 - cur][:, :, PAD:PAD + SEG], PS[cur][:, :, PAD:PAD + SEG], inv,
                                         ALU.mult))
                if n == 0:
                    pool.wait_ge(act_out, part_of("a", first_job("pool_in") + POOL_GROUPS - 1))
                pool.tensor_tensor(PD[:, g, :].rearrange("p (s n) -> p s n", s=2), PS[1 - cur][:, :, PAD:PAD + SEG],
                                   raw[:, :, PAD:PAD + SEG], ALU.subtract).then_inc(pool_d, 1)
                pool.wait_ge(pool_d, n + 1)

            pool.wait_ge(dve_out, part_of("d", first_job("norm", 4) - 1))
            pool.dma_start(ropeR[:, :, :], A["rope_ret"]).then_inc(ret_in, 16)
            pool.dma_start(perm[:, :], A["swap"]).then_inc(ret_in, 16)

            chain(pool.memset(neg_half[:, :], -0.5))
            with t.loop(pool, HEADS, head=1):
                t.add("head")
                pool.wait_ge(stat_ready, t.at("head"))
                pool.tensor_tensor(rstd[:, :], mv[:, :, 1], neg_half[:, :], ALU.pow).then_inc(rstd_ready, 1)

        @block.tensor
        def _(pe):
            t = Tally()
            depth = [BANKS]

            def open_job(ahead=0):
                j = t.first("job") + ahead
                if j >= depth[0]:
                    wait_job(j - depth[0])
                return bank[j % BANKS]

            def wait_job(j):
                m = j if t.reg is None or j >= t.start else j + t.per["job"]
                if "d" in JOBS[m][1]:
                    pe.wait_ge(dve_out, t.evacuated("d", j))
                else:
                    pe.wait_ge(act_out, t.evacuated("a", j))

            def wait_all():
                pe.wait_ge(dve_out, t.evacuated("d", t.first("job") - 1))
                pe.wait_ge(act_out, t.evacuated("a", t.first("job") - 1))

            def close_job(ins):
                ins.then_inc(acc_full, 1)
                t.add("job")

            def wait_panel():
                pe.wait_ge(split_lo, t.at("split", 1))
                return t.first("split")

            def wait_lo(k=1):
                t.add("lo", k)
                pe.wait_ge(lo_ready, t.at("lo"))

            def ada(layer, part):
                b = open_job()
                for kk in range(4):
                    n = ADA_AT[t.first("ada")]
                    pe.wait_ge(raw_in[n % RAW_SLOTS], arrivals(n))
                    raw = RAW[n % RAW_SLOTS]
                    for k2 in range(2):
                        for j in range(4):
                            ins = pe.matmul(b[32 * j:32 * j + 32, 0:256], cond[:, 2 * kk + k2, :],
                                            raw[:, k2 * 1024 + j * 256:k2 * 1024 + (j + 1) * 256],
                                            start=(kk == 0 and k2 == 0), stop=(kk == 3 and k2 == 1))
                    t.add("ada")
                    if kk < 3:
                        ins.then_inc(ada_used, 1)
                close_job(ins)
                b = open_job()
                wait_job(t.first("job") - 1)
                pe.transpose(b[:, 0:P], adarow[:, 0:P], ident[:, :]).then_inc(ada_used, 1)
                close_job(pe.transpose(b[:, P:2 * P], adarow[:, P:2 * P], ident[:, :]))

            def sum_squares(count, width, c0=0, jobs=None):
                b = open_job()
                for k in range(count):
                    if jobs is None:
                        t.add("sq")
                        pe.wait_ge(sq_ready, t.at("sq"))
                    else:
                        pe.wait_ge(act_out, part_of("a", jobs + k))
                    ins = pe.matmul(b[:, 0:width], ones[:, :], SQ[:, k % 2, c0:c0 + width],
                                    start=(k == 0), stop=(k == count - 1))
                    if k < count - 1:
                        ins.then_inc(ones_done, 1)
                close_job(ins)

            def sum_acc(width, c0=0, from_sbuf=True):
                t.add("acc", KD)
                t.add("sq", KD * from_sbuf)
                pe.wait_ge(acc_done, t.at("acc"))
                b = open_job()
                close_job(pe.matmul(b[:, 0:width], ones[:, :], ACC[:, c0:c0 + width], start=True, stop=True))

            pe.wait_ge(ident_ready, 1)
            pe.wait_ge(params_in, 16 * 10)
            for rows in (brows, grows):
                b = open_job()
                close_job(pe.transpose(b[:, 0:P], rows[:, :], ident[:, :]))
            pe.wait_ge(x_in, 32)
            for k in range(KD):
                b = open_job()
                for tt in range(4):
                    ins = pe.transpose(b[:, tt * P:(tt + 1) * P], xrows[:, tt, k * P:(k + 1) * P], ident[:, :])
                close_job(ins)
            sum_acc(T, from_sbuf=False)
            pe.wait_ge(cond_ready, 2)
            ada(0, SHIFT1)
            ada(0, SCALE1)

            def side_by_side(stats, movs, first, last, ahead=0):
                banks = [open_job(ahead), open_job(ahead + 1)]

                def products(k):
                    for m in range(2):
                        mov = movs[m](k)
                        ins = mm3(pe, banks[m][:, 0:mov[0].shape[-1]], stats(k, m), mov, k == first, k == last)
                        if k == last:
                            close_job(ins)
                return products

            def pair_of_jobs(ready, stats, movs):
                products = side_by_side(stats, movs, 0, KD - 1)
                for k in range(KD):
                    ready(k)
                    products(k)

            def project(s, c0):
                b = open_job()
                for k in range(KD):
                    ins = mm3(pe, b[:, :], w8(WW, s, k, c0, P), (H_hi[:, k, :], H_lo[:, k, :]), k == 0, k == KD - 1)
                return ins

            full_h = lambda k: (H_hi[:, k, :], H_lo[:, k, :])

            s = wait_panel()
            pair_of_jobs(lambda k: wait_lo(), lambda k, m: w8(WW, s, k, m * P, P), [full_h, full_h])
            t.add("split")
            s = wait_panel()
            close_job(project(s, 0))
            close_job(project(s, NOPE))
            t.add("split")
            sum_squares(2, T, jobs=first_job("lora"))
            sum_squares(1, T, jobs=first_job("lora") + 2)
            for _ in range(2):
                s = wait_panel()
                close_job(project(s, 0))
                close_job(project(s, P))
                t.add("split")

            def pair_q(p):
                for hh in range(2):
                    b = open_job()
                    for k in range(2):
                        c0 = k * HEADS * QH + (2 * p + hh) * QH
                        ins = mm3(pe, b[0:QH, :], (W_hi[uq][:, c0:c0 + QH], W_lo[uq][:, c0:c0 + QH]),
                                  (QN_hi[:, k, :], QN_lo[:, k, :]), k == 0, k == 1)
                    close_job(ins)

            def pair_k(p):
                for hh in range(2):
                    b = open_job()
                    c0 = (2 * p + hh) * P
                    close_job(mm3(pe, b[:, :], (W_hi[ukv][:, c0:c0 + P], W_lo[ukv][:, c0:c0 + P]),
                                  (QN_hi[:, 2, :], QN_lo[:, 2, :]), True, True))

            pe.wait_ge(split_lo, t.at("split", 1))
            uq, ukv = t.first("split") % 2, (t.first("split") + 1) % 2
            wait_lo(3)
            pair_q(0)
            pe.wait_ge(split_lo, t.at("split", 2))
            t.add("split", 2)
            v_cols = [w[ukv][:, 0:1024].rearrange("p (h x e) -> p h x e", h=HEADS, x=2)[:, :, 1, :] for w in WW]
            for tt in range(4):
                b = open_job()
                cs = slice(tt * P, (tt + 1) * P)
                close_job(mm3(pe, b[:, :], (QN_hi[:, 2, cs], QN_lo[:, 2, cs]), v_cols, True, True))
            pair_k(0)

            def pair_scores(p):
                wait_lo(1)
                for tt in range(2):
                    for hh in range(2):
                        b = open_job()
                        cs = slice(LAT + tt * P, LAT + (tt + 1) * P)
                        close_job(mm3(pe, b[:, :], (Q_hi[0:QH, hh, cs], Q_lo[0:QH, hh, cs]),
                                      (K_hi[0:QH, hh, :], K_lo[0:QH, hh, :]), True, True))
                for tt in range(2):
                    b = open_job()
                    cs = slice(tt * P, (tt + 1) * P)
                    for hh in range(2):
                        ins = mm3(pe, b[:, hh * SEG:(hh + 1) * SEG], (Q_hi[0:QH, hh, cs], Q_lo[0:QH, hh, cs]),
                                  (K_hi[0:QH, hh, 0:SEG], K_lo[0:QH, hh, 0:SEG]), True, True)
                    close_job(ins)

            def turn(p, context, kt):
                b = open_job()
                for hh in range(2):
                    for tt in range(2):
                        c = (hh * 2 + tt) * P
                        src = PROBCS[p % 2][:, tt, hh, :] if context else PROBS[p % 2][:, tt * 2 + hh, :]
                        ins = pe.transpose(b[:, c:c + P], src[:, kt * P:(kt + 1) * P], ident[:, :])
                close_job(ins)

            def values(p, tiles, slot0, last_turn):
                wait_job(last_turn)
                b = open_job()
                vs = slice(p * P, (p + 1) * P)
                for kt in tiles:
                    ins = mm3(pe, b[:, :], (V_hi[:, kt, vs], V_lo[:, kt, vs]),
                              (PT_hi[:, slot0 + kt, :], PT_lo[:, slot0 + kt, :]), kt == tiles[0], kt == tiles[-1])
                close_job(ins)

            def pair_values(p, first_filler, second_filler):
                wait_job(first_job("scores", p) + 5)
                for kt in range(2):
                    turn(p, True, kt)
                context_turn = t.first("job") - 1
                for kt in range(2):
                    turn(p, False, kt)
                first_filler()
                values(p, (0, 1), 2, context_turn)
                for kt in range(2, 4):
                    turn(p, False, kt)
                latent_turn = t.first("job") - 1
                second_filler()
                values(p, (0, 1, 2, 3), 0, latent_turn)

            def next_qk(p):
                pair_q(p)
                pair_k(p)

            wait_lo(1)
            wait_job(first_job("k", 0) + 1)
            pair_scores(0)
            next_qk(1)
            ada(0, GATE1)
            for p in range(1, PAIRS - 1):
                wait_job(first_job("k", p) + 1)
                pair_scores(p)
                pair_values(p - 1, lambda: next_qk(p + 1), lambda: ada(0, (GATE1, SHIFT2, SCALE2)[p]))

            def pool_products():
                wait_lo(POOL_GROUPS)
                for g in range(POOL_GROUPS):
                    b = open_job()
                    c0 = D + g * P
                    close_job(mm3(pe, b[:, :], (W_hi[ukv][:, c0:c0 + P], W_lo[ukv][:, c0:c0 + P]),
                                  (PD_hi[:, g, :], PD_lo[:, g, :]), True, True))

            wait_job(first_job("k", PAIRS - 1) + 1)
            pair_scores(PAIRS - 1)
            pair_values(PAIRS - 2, lambda: ada(0, GATE2), pool_products)

            s = wait_panel()
            stats = lambda k, m: w8(WW, s, k, m * P, P)
            first_sums = []

            def first_pairs():
                first_sums.append(side_by_side(stats, [full_h, full_h], 0, PAIRS - 1, ahead=4))
                for k in range(PAIRS - 1):
                    first_sums[0](k)

            def pool_groups():
                for g in range(POOL_GROUPS):
                    first_sums[0](PAIRS + g)

            wait_job(t.first("job") - 1)
            pair_values(PAIRS - 1, first_pairs, pool_groups)
            wait_job(t.first("job") - 1)
            first_sums[0](PAIRS - 1)
            t.add("split")
            for _ in range(3):
                s = wait_panel()
                close_job(project(s, 0))
                close_job(project(s, P))
                t.add("split")
            sum_acc(T, from_sbuf=False)
            ada(1, SHIFT1)
            sum_squares(KD, T)
            ada(1, SCALE1)

            def ffn(c0, last_layer):
                w = T - c0
                wait_all()
                depth[0] = 4
                lo0 = t.first("lo")
                t.add("lo", KD)
                for half in range(2):
                    hidden0 = t.first("job")
                    with t.loop(pe, 2, job=8, split=4):
                        for n in range(4):
                            s = wait_panel()
                            chunk = lambda k: (H_hi[:, k, c0:T], H_lo[:, k, c0:T])
                            if n == 0 and half == 0:
                                pair_of_jobs(lambda k: pe.wait_ge(lo_ready, lo0 + k + 1),
                                             lambda k, m: w8(WW, s, k, m * P, P), [chunk, chunk])
                                t.add("split")
                                continue
                            for m in range(2):
                                b = open_job()
                                for k in range(KD):
                                    ins = mm3(pe, b[:, 0:w], w8(WW, s, k, m * P, P), chunk(k), k == 0, k == KD - 1)
                                close_job(ins)
                            t.add("split")
                    sums0 = t.first("job")

                    def two_chunks():
                        banks = []
                        for kg in range(2):
                            s = wait_panel()
                            pe.wait_ge(dve_out, part_of("d", hidden0 + 8 * kg + 7))
                            for m in range(2):
                                if kg == 0:
                                    j = t.first("job")
                                    if m == 0:
                                        wait_job(j - 3)
                                    banks.append(ffn_bank(sums0, j + m))
                                for k in range(KD):
                                    ins = mm3(pe, banks[m][:, 0:w], w8(WW, s, k, m * P, P),
                                              (HID_hi[:, kg * 8 + k, c0:T], HID_lo[:, kg * 8 + k, c0:T]),
                                              kg == 0 and k == 0, kg == 1 and k == KD - 1)
                                if kg == 1:
                                    ins.then_inc(acc_full, 1)
                                    t.add("job")
                                elif m == 1:
                                    ins.then_inc(half_sum, 1)
                            t.add("split")

                    if last_layer and half:
                        for _ in range(4):
                            two_chunks()
                    else:
                        with t.loop(pe, 2, job=4, split=4):
                            two_chunks()
                            two_chunks()
                sum_acc(w, c0)

            ffn(0, False)
            ada(1, GATE1)
            sum_squares(KD, T)
            ada(1, SHIFT2)

            def qk_weights(s, k, m):
                at = (m * KD + k) * R_DK
                return [w[s % 2][:, at:at + R_DK] for w in WW]

            q_and_k = [lambda k: (H_hi[:, k, LAT:T], H_lo[:, k, LAT:T]), lambda k: (H_hi[:, k, :], H_lo[:, k, :])]

            def head_qk():
                s = wait_panel()
                for m, width in enumerate((SEG, T)):
                    b = open_job()
                    for k in range(KD):
                        ins = mm3(pe, b[:, 0:width], qk_weights(s, k, m), q_and_k[m](k), k == 0, k == KD - 1)
                    close_job(ins)
                t.add("split")

            def head_swap(qk_job):
                wait_job(qk_job)
                b = open_job()
                close_job(pe.matmul(b[:, :], perm[:, :], QK[:, 0:2, :], start=True, stop=True))

            def head_tokens(s, b, col, tile):
                for k in range(KD):
                    cs = slice(tile * P, (tile + 1) * P)
                    ins = mm3(pe, b[:, col:col + 256], (H_hi[:, k, cs], H_lo[:, k, cs]), w8(WW, s, k, 0, 256),
                              k == 0, k == KD - 1)
                return ins

            def head_v():
                s = wait_panel()
                for jj in range(2):
                    b = open_job()
                    head_tokens(s, b, 0, 2 * jj)
                    close_job(head_tokens(s, b, 256, 2 * jj + 1))
                t.add("split")

            def head_attend():
                wait_lo(1)
                for jj in range(2):
                    b = open_job()
                    for n in range(2):
                        part = 2 if jj == 0 else 1
                        ins = mm3(pe, b[:, n * SEG:(n + 1) * SEG],
                                  (QK_hi[:, part, n * P:(n + 1) * P], QK_lo[:, part, n * P:(n + 1) * P]),
                                  (QK_hi[:, 0, :], QK_lo[:, 0, :]), True, True)
                    close_job(ins)
                s = wait_panel()
                for tt in range(2):
                    b = open_job()
                    close_job(head_tokens(s, b, 0, 2 + tt))
                t.add("split")
                wait_lo(2)
                for tt in range(2):
                    b = open_job()
                    for kt in range(4):
                        cs = slice(tt * P, (tt + 1) * P)
                        ins = mm3(pe, b[:, 0:R_DV], (SA_hi[:, kt, cs], SA_lo[:, kt, cs]),
                                  (RV_hi[:, kt, :], RV_lo[:, kt, :]), kt == 0, kt == 3)
                    close_job(ins)

            def head_turn():
                t.add("rows")
                pe.wait_ge(rows_ready, t.at("rows"))
                b = open_job()
                for c in range(2):
                    for tt in range(2):
                        ins = pe.transpose(b[:, (c * 2 + tt) * P:(c * 2 + tt + 1) * P],
                                           ON[:, tt, c * P:(c + 1) * P], ident[:, :])
                close_job(ins)

            def head_out(turn_job):
                s = wait_panel()
                wait_job(turn_job)
                for jj in range(4):
                    b = open_job()
                    for n in range(2):
                        for c in range(2):
                            c0 = c * D + (2 * jj + n) * P
                            ins = mm3(pe, b[:, n * SEG:(n + 1) * SEG], [w[s % 2][:, c0:c0 + P] for w in WW],
                                      (YT_hi[:, c, :], YT_lo[:, c, :]), c == 0, c == 1)
                    close_job(ins)
                t.add("split")

            s = wait_panel()
            pair_of_jobs(lambda k: wait_lo(), lambda k, m: qk_weights(s, k, m), q_and_k)
            t.add("split")
            pe.wait_ge(ret_in, 32)
            head_swap(t.first("job") - 1)
            head_v()
            wait_all()
            depth[0] = BANKS
            with t.loop(pe, HEADS - 1, job=16, split=4, lo=3, rows=1):
                head_attend()
                head_qk()
                head_turn()
                head_swap(t.first("job") - 2)
                head_v()
                head_out(t.first("job") - 4)
            head_attend()
            ada(1, SCALE2)
            head_turn()
            head_out(t.first("job") - 1)
            sum_squares(KD, SEG, LAT)
            ada(1, GATE2)
            sum_squares(KD, SEG, LAT)
            ffn(LAT, True)

            for half in range(2):
                t.add("xr", 4)
                pe.wait_ge(x_ready, 3 * KD + t.at("xr"))
                for tt in range(2):
                    b = open_job()
                    for k in range(4):
                        ins = pe.transpose(b[:, k * P:(k + 1) * P],
                                           X[:, half * 4 + k, LAT + tt * P:LAT + (tt + 1) * P], ident[:, :])
                    close_job(ins)
            assert t.first("job") == len(JOBS) and t.first("split") == len(SPLIT_AT), (t.n, len(JOBS))

        @block.scalar
        def _(act):
            t = Tally()

            def split():
                act.wait_ge(acc_full, t.at("job"))
                s = t.first("split")
                n = SPLIT_AT[s]
                v = arrivals(n)
                if t.reg is not None:
                    v = t.reg * (16 * PLAN[n + RAW_SLOTS][1]) + v
                act.wait_ge(raw_in[n % RAW_SLOTS], v)
                act.activation(W_hi[s % 2][:, :], RAW[n % RAW_SLOTS][:, :], ACT.Copy).then_inc(split_hi, 1)
                t.add("split")

            def split_part(cols):
                s = t.first("split")
                n = SPLIT_AT[s]
                act.wait_ge(raw_in[n % RAW_SLOTS], arrivals(n))
                act.activation(W_hi[s % 2][:, 0:cols], RAW[n % RAW_SLOTS][:, 0:cols], ACT.Copy).then_inc(split_hi, 1)
                t.add("split")

            def job(banks=BANKS):
                t.add("job")
                act.wait_ge(acc_full, t.at("job"))
                return bank[(t.first("job") - 1) % banks]

            def skip(k=1):
                t.add("job", k)

            def done(ins):
                ins.then_inc(act_out, 1)

            def squares_free(n):
                if n >= 2:
                    act.wait_ge(ones_done, t.first("ones") + n - 1)

            def norm_root(width, n, c0=0):
                b = job()
                done(act.activation(R[:, c0:c0 + width], b[:, 0:width], ACT.Sqrt, bias=eps_col, scale=1.0 / n))

            def job_square(k):
                b = job()
                if k >= 2:
                    act.wait_ge(acc_done, t.first("acc") + k - 1)
                done(act.activation(SQ[:, k % 2, :], b[:, :], ACT.Square))

            def hi(out, in_):
                t.add("full")
                act.wait_ge(full_ready, t.at("full"))
                act.activation(out, in_, ACT.Copy).then_inc(hi_ready, 1)

            def ada():
                b = job()
                done(act.activation(adarow[:, :], b[:, 0:256], ACT.Copy))
                skip()

            def chunks_hi(layer, which, part_shift, segs, midway=None):
                c0 = segs[0] * SEG
                for k in range(KD + 1):
                    if k == KD // 2 and midway:
                        midway()
                    if k < KD:
                        t.add("full")
                        act.wait_ge(full_ready, t.at("full"))
                        h = h_buffer(k)
                        for s in segs:
                            cs = slice(s * SEG, (s + 1) * SEG)
                            ins = act.activation(h[:, cs], h[:, cs], ACT.Identity,
                                                 bias=mod[:, layer, part_shift, k, s:s + 1],
                                                 scale=pre_gain[:, layer, which, k, s:s + 1])
                        ins.then_inc(modulated, 1)
                    if k >= 1:
                        t.add("modulated")
                        act.wait_ge(modulated, t.at("modulated"))
                        act.activation(H_hi[:, k - 1, c0:T], h_buffer(k - 1)[:, c0:T], ACT.Copy).then_inc(hi_ready, 1)

            def squares_of_x(c0, n0):
                for k in range(KD):
                    act.wait_ge(x_ready, n0 + k + 1)
                    squares_free(k)
                    act.activation(SQ[:, k % 2, c0:T], X[:, k, c0:T], ACT.Square).then_inc(sq_ready, 1)
                t.add("ones", KD - 1)

            act.wait_ge(rows_zero, 2)
            act.dma_start(brows[0:96, :], A["b_ada"].rearrange("l (c p) -> (l c) p", p=P)).then_inc(params_in, 16)
            r = 0
            for name in ("g_mix_pre", "g_mix_post", "g_ffn_pre", "g_ffn_post", "g_q_lora", "g_kv_lora",
                         "pool_scale", "c", "c_ctx"):
                src = A[name] if len(A[name].shape) == 2 else A[name].rearrange("(a n) -> a n", a=1)
                rows = src.shape[0] * src.shape[1] // P
                act.dma_start(grows[r:r + rows, :], src.rearrange("l (c p) -> (l c) p", p=P)).then_inc(params_in, 16)
                r += rows
            skip(2)
            act.wait_ge(cond_e, 1)
            act.activation(silu_e[:, :], gcol[:, 71:87], ACT.Exp, scale=-1.0).then_inc(cond_e, 1)
            for k in range(KD):
                job_square(k)
            t.add("acc", KD)
            act.wait_ge(rows_zero, 4)
            norm_root(T, D)
            ada()
            split()
            ada()
            chunks_hi(0, 0, SHIFT1, (0, 1), midway=split)

            for k in range(2):
                b = job()
                done(act.activation(SQ[:, k, :], b[:, :], ACT.Square))
            split()
            b = job()
            act.wait_ge(ones_done, t.first("ones") + 1)
            done(act.activation(SQ[:, 0, :], b[:, :], ACT.Square))
            t.add("ones")
            b = job()
            done(act.activation(KR[NOPE:QH, :], b[NOPE:QH, :], ACT.Copy))
            norm_root(T, Q_LORA)
            split()
            for k in range(2):
                hi(QN_hi[:, k, :], LORA[:, k, :])
            norm_root(T, KV_LORA)
            hi(QN_hi[:, 2, :], LORA[:, 2, :])
            act.wait_ge(rows_zero, 6)
            for g in range(POOL_GROUPS):
                b = job()
                done(act.activation(PRAW[:, g, :, PAD:PAD + SEG], b[:, :].rearrange("p (s n) -> p s n", s=2), ACT.Copy))
                if g == 1:
                    split_part(2 * HEADS * QH)
            split_part(D + POOL_GROUPS * P)

            def both(out, in_):
                done(act.activation(out, in_, ACT.Copy))

            t.add("full")
            act.wait_ge(full_ready, t.at("full"))
            act.activation(K_hi[NOPE:QH, 0, :], KR[NOPE:QH, :], ACT.Copy)
            act.activation(K_hi[NOPE:QH, 1, :], KR[NOPE:QH, :], ACT.Copy).then_inc(hi_ready, 1)

            def pair_q():
                for hh in range(2):
                    both(QF[0:QH, hh, :], job()[0:QH, :])

            def pair_k():
                for hh in range(2):
                    both(K_hi[0:NOPE, hh, :], job()[0:NOPE, :])
                hi(Q_hi[0:QH, :, :], QF[0:QH, :, :])

            pair_q()
            for tt in range(4):
                both(V_hi[:, tt, :], job()[:, :])
            pair_k()

            def pair_softmax(p):
                for tt in range(2):
                    for hh in range(2):
                        b = job()
                        t.add("max")
                        act.wait_ge(rowmax, t.at("max"))
                        n = tt * 2 + hh
                        done(act.activation(PROBS[p % 2][:, n, :], b[:, :], ACT.Exp, bias=small[:, 1 + n:2 + n],
                                            scale=ATT_SCALE, accum_out=small[:, 9 + n:10 + n]))
                if p == 1:
                    act.wait_ge(pool_d, POOL_GROUPS)
                for tt in range(2):
                    b = job()
                    t.add("max")
                    act.wait_ge(rowmax, t.at("max"))
                    for hh in range(2):
                        n = 4 + tt * 2 + hh
                        ins = act.activation(PROBCS[p % 2][:, tt, hh, :], b[:, hh * SEG:(hh + 1) * SEG], ACT.Exp,
                                             bias=small[:, 1 + n:2 + n], scale=ATT_SCALE,
                                             accum_out=small[:, 9 + n:10 + n])
                    done(ins)

            def pair_values(p, first_filler, second_filler):
                def out(s):
                    b = job()
                    cs = slice(s * SEG, (s + 1) * SEG)
                    act.activation(H_hi[0:VD, p, cs], b[0:VD, 0:SEG], ACT.Copy)
                    both(H_hi[VD:P, p, cs], b[VD:P, SEG:T])

                for kt in (2, 3, 0, 1):
                    both(PT_hi[:, kt, :], job()[:, :])
                first_filler()
                out(0)
                for kt in (2, 3):
                    both(PT_hi[:, kt, :], job()[:, :])
                second_filler()
                out(1)

            def next_qk():
                pair_q()
                pair_k()

            def pool_split():
                for g in range(POOL_GROUPS):
                    act.activation(PD_hi[:, g, :], PD[:, g, :], ACT.Copy).then_inc(hi_ready, 1)

            def pool_products():
                for g in range(POOL_GROUPS):
                    done(act.activation(H_hi[:, 4 + g, :], job()[:, :], ACT.Copy, scale=gcol[:, 67 + g:68 + g]))

            pair_softmax(0)
            next_qk()
            ada()
            for p in range(1, PAIRS - 1):
                pair_softmax(p)
                pair_values(p - 1, next_qk, ada)
            pair_softmax(PAIRS - 1)
            split()

            def last_fill():
                ada()
                pool_split()

            pair_values(PAIRS - 2, last_fill, pool_products)
            pair_values(PAIRS - 1, lambda: None, lambda: None)

            split()
            for c in range(4):
                for m in range(2):
                    job_square(2 * c + m)
                split()
            t.add("acc", KD)
            norm_root(T, D)
            ada()
            squares_of_x(0, 0)
            norm_root(T, D)
            ada()

            def ffn(layer, c0, last_layer):
                segs = (0, 1) if c0 == 0 else (1,)
                w = T - c0
                chunks_hi(layer, 1, SHIFT2, segs)
                for half in range(2):
                    with t.loop(act, 2, job=8, split=4, chain=8) as i:
                        for n in range(4):
                            for m in range(2):
                                b = job()
                                r = m % 2
                                act.wait_ge(dve_out, t.evacuated("d", t.first("job") - 3))
                                act.activation(TMP[:, r, c0:T], b[:, 0:w], ACT.Relu).then_inc(act_chain, 1)
                                t.add("chain")
                                act.wait_ge(act_chain, t.at("chain"))
                                done(act.activation(HID_hi[:, bass.ds(i * 8 + (2 * n + m), 1), c0:T],
                                                    TMP[:, r:r + 1, c0:T], ACT.Square))
                            split()

                    def two_chunks(i, c, more):
                        t.add("half_sum")
                        if more:
                            act.wait_ge(half_sum, t.at("half_sum"))
                            split()
                        for m in range(2):
                            t.add("job")
                            if half:
                                act.wait_ge(dve_out, t.evacuated("d", t.first("job") - 1))
                                act.wait_ge(acc_done, t.at("acc", -1))
                                y = Y[:, bass.ds(i * 4 + (2 * c + m), 1), c0:T] if t.reg is not None else \
                                    Y[:, 2 * c + m:2 * c + m + 1, c0:T]
                                act.activation(SQ[:, m:m + 1, c0:T], y, ACT.Square).then_inc(sq_ready, 1)
                                t.add("acc")
                        if more:
                            split()

                    if last_layer and half:
                        for c in range(4):
                            two_chunks(0, c, c < 3)
                    else:
                        extra = dict(acc=4) if half else {}
                        with t.loop(act, 2, job=4, split=4, half_sum=2, **extra) as i:
                            for c in range(2):
                                two_chunks(i, c, True)
                norm_root(w, D, c0)

            ffn(0, 0, False)
            ada()
            squares_of_x(0, KD)
            norm_root(T, D)
            ada()

            def decay_load(h):
                act.dma_start(DEC[:, :, :], A["decay"][h]).then_inc(decay_in, 16)

            def head_qk():
                both(QK[:, 0, :], job()[:, 0:SEG])
                b = job()
                act.activation(QK[:, 1, :], b[:, LAT:T], ACT.Copy)
                both(QK[:, 2, :], b[:, 0:SEG])
                split()

            def head_rotated():
                skip()
                hi(QK_hi[:, :, :], QK[:, :, :])

            def head_v():
                for jj in range(2):
                    both(RV_hi[:, 2 * jj:2 * jj + 2, :], job()[:, :])

            def head_attend(h, last):
                skip(2)
                for jj in range(2):
                    hi(SA_hi[:, 2 * jj:2 * jj + 2, :], SA[:, 2 * jj:2 * jj + 2, :])
                if not last:
                    act.dma_start(DEC[:, :, :], A["decay"][bass.ds(h + 1, 1)].rearrange("a p k n -> p (a k) n"))\
                       .then_inc(decay_in, 16)
                split()
                for tt in range(2):
                    done(act.activation(GE[:, tt, :], job()[:, 0:R_DV], ACT.Exp, scale=-1.0))
                split()
                skip(2)

            chunks_hi(1, 0, SHIFT1, (0, 1))
            decay_load(0)
            head_qk()
            head_rotated()
            head_v()
            with t.loop(act, HEADS - 1, job=16, split=4, full=3) as h:
                head_attend(h, False)
                head_qk()
                both(YT_hi[:, :, :], job()[:, :])
                head_rotated()
                head_v()
                split()
                skip(4)
            head_attend(HEADS - 1, True)
            ada()
            both(YT_hi[:, :, :], job()[:, :])
            skip(4)
            split()
            for k in range(KD):
                if k == 0:
                    act.wait_ge(dve_out, part_of("d", t.first("job") - 1))
                squares_free(k)
                act.activation(SQ[:, k % 2, LAT:T], Y[:, k, LAT:T], ACT.Square).then_inc(sq_ready, 1)
            t.add("ones", KD - 1)
            norm_root(SEG, D, LAT)
            ada()
            squares_of_x(LAT, 2 * KD)
            norm_root(SEG, D, LAT)
            ffn(1, LAT, True)
            for half in range(2):
                for tt in range(2):
                    both(OUTR[:, tt, half * 512:(half + 1) * 512], job()[:, :])
            assert t.first("job") == len(JOBS) and t.first("split") == len(SPLIT_AT), (t.n, len(JOBS))

        @block.vector
        def _(dve):
            t = Tally()

            def split(cols=PANEL):
                s = t.first("split")
                t.add("split")
                dve.wait_ge(split_hi, t.at("split"))
                raw = RAW[SPLIT_AT[s] % RAW_SLOTS]
                dve.tensor_tensor(W_lo[s % 2][:, 0:cols], raw[:, 0:cols], W_hi[s % 2][:, 0:cols].bitcast(F32),
                                  ALU.subtract).then_inc(split_lo, 1)

            def job(banks=BANKS):
                j = t.first("job")
                t.add("job")
                if "a" in JOBS[j][1]:
                    dve.wait_ge(act_out, t.evacuated("a", j))
                else:
                    dve.wait_ge(acc_full, t.at("job"))
                return bank[j % banks]

            def skip(k=1):
                t.add("job", k)

            def done(ins):
                ins.then_inc(dve_out, 1)

            def chain(ins):
                ins.then_inc(dve_chain, 1)
                t.add("chain")

            def settle():
                dve.wait_ge(dve_chain, t.at("chain"))

            def lo(out, full, hi_part):
                t.add("hi")
                dve.wait_ge(hi_ready, t.at("hi"))
                dve.tensor_tensor(out, full, hi_part.bitcast(F32), ALU.subtract).then_inc(lo_ready, 1)
                t.add("lo")

            def job_lo(out, hi_part):
                b = job()
                done(dve.tensor_tensor(out, b[:, :], hi_part.bitcast(F32), ALU.subtract))

            def norm_recip(width, c0=0):
                job()
                done(dve.reciprocal(R[:, c0:c0 + width], R[:, c0:c0 + width]))
                dve.wait_ge(dve_out, part_of("d", t.first("job") - 1))

            def ada(layer, part):
                skip()
                b = job()
                rows = b[:, 0:256].rearrange("p (c j s) -> p c j s", c=2, s=32)
                bias = bcol[:, layer * 48 + part * 8:layer * 48 + part * 8 + 8]
                for c in range(2):
                    o = mod[:, layer, part, :, :].rearrange("p (j c) s -> p c j s", c=2)[:, c, :, :]
                    ins = dve.tensor_tensor(o, rows[:, c, :, 0:2],
                                            bias.rearrange("p (j c) -> p c j", c=2)[:, c, :].unsqueeze(2)
                                            .to_broadcast([P, 4, 2]), ALU.add)
                    if c == 0:
                        chain(ins)
                done(ins)
                dve.wait_ge(dve_out, part_of("d", t.first("job") - 1))
                which = int(part >= SHIFT2)
                m = mod[:, layer, part, :, :]
                if part in (SCALE1, SCALE2):
                    g = gcol[:, which * 32 + layer * 8:which * 32 + layer * 8 + 8].unsqueeze(2).to_broadcast([P, 8, 2])
                    chain(dve.scalar_tensor_tensor(out=pre_gain[:, layer, which, :, :], in0=m, scalar=1.0, in1=g,
                                                   op0=ALU.add, op1=ALU.mult))
                if part in (GATE1, GATE2):
                    c0 = 16 + which * 32 + layer * 8
                    g = gcol[:, c0:c0 + 8].unsqueeze(2).to_broadcast([P, 8, 2])
                    chain(dve.tensor_tensor(post_gain[:, layer, which, :, :], m, g, ALU.mult))

            def chunks_full(segs, midway=None):
                c0 = segs[0] * SEG

                def lo_of(k):
                    lo(H_lo[:, k, c0:T], h_buffer(k)[:, c0:T], H_hi[:, k, c0:T])

                for k in range(KD):
                    if k == KD // 2 and midway:
                        midway()
                    if k >= 4:
                        dve.wait_ge(lo_ready, t.at("lo", -1))
                    dve.tensor_tensor(h_buffer(k)[:, c0:T], X[:, k, c0:T], R[:, c0:T], ALU.mult).then_inc(full_ready, 1)
                    if k >= 2:
                        lo_of(k - 2)
                lo_of(KD - 2)
                lo_of(KD - 1)

            def update_x(layer, which, segs):
                c0 = segs[0] * SEG
                settle()
                for k in range(KD + 1):
                    if k < KD:
                        chain(dve.tensor_tensor(Y[:, k, c0:T], Y[:, k, c0:T], R[:, c0:T], ALU.mult))
                    if k >= 1:
                        dve.wait_ge(dve_chain, t.at("chain", -1 if k < KD else 0))
                        for s in segs:
                            cs = slice(s * SEG, (s + 1) * SEG)
                            ins = dve.scalar_tensor_tensor(out=X[:, k - 1, cs], in0=Y[:, k - 1, cs],
                                                           scalar=post_gain[:, layer, which, k - 1, s:s + 1],
                                                           in1=X[:, k - 1, cs], op0=ALU.mult, op1=ALU.add)
                        ins.then_inc(x_ready, 1)
                        t.add("x")
                dve.wait_ge(x_ready, t.at("x"))

            def clear_acc():
                chain(dve.memset(ACC[:, :], 0.0))
                settle()

            def keep_and_add(out, k):
                done(dve.tensor_copy(out[:, k, :], job()[:, :]))
                if t.first("acc"):
                    dve.wait_ge(acc_done, t.at("acc"))
                dve.tensor_tensor(ACC[:, :], ACC[:, :], SQ[:, k % 2, :], ALU.add).then_inc(acc_done, 1)
                t.add("acc")

            done(dve.tensor_copy(bcol[:, :], job()[:, 0:96]))
            b = job()
            done(dve.tensor_copy(gcol[:, :], b[:, 0:88]))
            dve.wait_ge(dve_out, 2)
            dve.sem_inc(cond_e, 1)
            clear_acc()
            for k in range(KD):
                keep_and_add(X, k)
            dve.wait_ge(cond_e, 2)
            chain(dve.tensor_scalar(silu_e[:, :], silu_e[:, :], 1.0, None, ALU.add))
            settle()
            chain(dve.reciprocal(silu_e[:, :], silu_e[:, :]))
            settle()
            dve.wait_ge(rows_zero, 3)
            for s, c0 in ((1, 0), (0, 8)):
                dve.tensor_tensor(cond[:, :, s], gcol[:, 71 + c0:79 + c0], silu_e[:, c0:c0 + 8],
                                  ALU.mult).then_inc(cond_ready, 1)
            norm_recip(T)
            ada(0, SHIFT1)
            split()
            ada(0, SCALE1)
            settle()
            chunks_full((0, 1), midway=split)

            for k in range(2):
                done(dve.tensor_copy(LORA[:, k, :], job()[:, :]))
            split()
            done(dve.tensor_copy(LORA[:, 2, :], job()[:, :]))
            skip()

            def lora(k, col):
                dve.scalar_tensor_tensor(out=LORA[:, k, :], in0=LORA[:, k, :], scalar=gcol[:, col:col + 1],
                                         in1=R[:, :], op0=ALU.mult, op1=ALU.mult).then_inc(full_ready, 1)

            norm_recip(T)
            split()
            lora(0, 64)
            lora(1, 65)
            lo(QN_lo[:, 0, :], LORA[:, 0, :], QN_hi[:, 0, :])
            lo(QN_lo[:, 1, :], LORA[:, 1, :], QN_hi[:, 1, :])
            norm_recip(T)
            lora(2, 66)
            lo(QN_lo[:, 2, :], LORA[:, 2, :], QN_hi[:, 2, :])

            def rotate(x, sw, cos, sin):
                chain(dve.stream_shuffle(sw, x, [(n // 16) * 16 + (n + 8) % 16 for n in range(32)]))
                settle()
                chain(dve.tensor_tensor(sw, sw, sin, ALU.mult))
                chain(dve.tensor_tensor(x, x, cos, ALU.mult))
                settle()
                dve.tensor_tensor(x, x, sw, ALU.add).then_inc(full_ready, 1)

            dve.wait_ge(consts_in, 16)
            dve.wait_ge(act_out, part_of("a", first_job("kr")))
            split(2 * HEADS * QH)
            rotate(KR[NOPE:QH, LAT:T], SW[NOPE:QH, 0, 0:SEG], ropeA[NOPE:QH, 0, :], ropeA[NOPE:QH, 1, :])
            t.add("hi")
            dve.wait_ge(hi_ready, t.at("hi"))
            dve.tensor_tensor(K_lo[NOPE:QH, 0, :], KR[NOPE:QH, :], K_hi[NOPE:QH, 0, :].bitcast(F32), ALU.subtract)
            dve.tensor_tensor(K_lo[NOPE:QH, 1, :], KR[NOPE:QH, :], K_hi[NOPE:QH, 1, :].bitcast(F32),
                              ALU.subtract).then_inc(lo_ready, 1)
            t.add("lo")
            skip(POOL_GROUPS)
            split(D + POOL_GROUPS * P)

            def pair_q():
                skip(2)
                dve.wait_ge(act_out, part_of("a", t.first("job") - 1))
                cos, sin = [ropeA[NOPE:QH, n, :].unsqueeze(1).to_broadcast([ROPE, 2, SEG]) for n in range(2)]
                rotate(QF[NOPE:QH, :, LAT:T], SW[NOPE:QH, :, 0:SEG], cos, sin)

            def pair_k():
                for hh in range(2):
                    b = job()
                    done(dve.tensor_tensor(K_lo[0:NOPE, hh, :], b[0:NOPE, :], K_hi[0:NOPE, hh, :].bitcast(F32),
                                           ALU.subtract))
                lo(Q_lo[0:QH, :, :], QF[0:QH, :, :], Q_hi[0:QH, :, :])

            pair_q()
            for tt in range(4):
                job_lo(V_lo[:, tt, :], V_hi[:, tt, :])
            pair_k()

            def pair_softmax(p):
                PR, PC = PROBS[p % 2], PROBCS[p % 2]
                j0 = t.first("job")

                def row_max(n):
                    dve.wait_ge(acc_full, j0 + n + 1)
                    b = bank[(j0 + n) % BANKS]
                    if n < 4:
                        mx, nm = small[:, 25 + n:26 + n], small[:, 1 + n:2 + n]
                        chain(dve.tensor_reduce(mx, b[:, :], AXX, ALU.max))
                    else:
                        mx, nm = small[:, 21 + 2 * n:23 + 2 * n], small[:, 2 * n - 3:2 * n - 1]
                        chain(dve.tensor_reduce(mx, b[:, :].rearrange("p (h k) -> p h k", h=2), AXX, ALU.max))
                    settle()
                    dve.tensor_scalar(nm, mx, -ATT_SCALE, None, ALU.mult).then_inc(rowmax, 1)

                def normalise(n):
                    job()
                    if n < 4:
                        chain(dve.reciprocal(small[:, 17 + n:18 + n], small[:, 9 + n:10 + n]))
                        settle()
                        done(dve.tensor_scalar(PR[:, n, :], PR[:, n, :], small[:, 17 + n:18 + n], None, ALU.mult))
                        return
                    c0 = 2 * n - 4
                    chain(dve.reciprocal(small[:, 17 + c0:19 + c0], small[:, 9 + c0:11 + c0]))
                    settle()
                    dve.tensor_scalar(PC[:, n - 4, 0, :], PC[:, n - 4, 0, :], small[:, 17 + c0:18 + c0], None,
                                      ALU.mult)
                    done(dve.tensor_scalar(PC[:, n - 4, 1, :], PC[:, n - 4, 1, :], small[:, 18 + c0:19 + c0],
                                           None, ALU.mult))

                row_max(0)
                for n in range(6):
                    if n < 5:
                        row_max(n + 1)
                    normalise(n)

            def pair_values(p, first_filler, second_filler):
                def out(s):
                    b = job()
                    cs = slice(s * SEG, (s + 1) * SEG)
                    dve.tensor_tensor(H_lo[0:VD, p, cs], b[0:VD, 0:SEG], H_hi[0:VD, p, cs].bitcast(F32), ALU.subtract)
                    done(dve.tensor_tensor(H_lo[VD:P, p, cs], b[VD:P, SEG:T], H_hi[VD:P, p, cs].bitcast(F32),
                                           ALU.subtract))

                for kt in (2, 3, 0, 1):
                    job_lo(PT_lo[:, kt, :], PT_hi[:, kt, :])
                first_filler()
                out(0)
                for kt in (2, 3):
                    job_lo(PT_lo[:, kt, :], PT_hi[:, kt, :])
                second_filler()
                out(1)

            def next_qk():
                pair_q()
                pair_k()

            def pool_products():
                for g in range(POOL_GROUPS):
                    b = job()
                    done(dve.scalar_tensor_tensor(out=H_lo[:, 4 + g, :], in0=b[:, :], scalar=gcol[:, 67 + g:68 + g],
                                                  in1=H_hi[:, 4 + g, :].bitcast(F32), op0=ALU.mult,
                                                  op1=ALU.subtract))

            pair_softmax(0)
            next_qk()
            ada(0, GATE1)
            for p in range(1, PAIRS - 1):
                pair_softmax(p)
                pair_values(p - 1, next_qk, lambda: ada(0, (GATE1, SHIFT2, SCALE2)[p]))
            pair_softmax(PAIRS - 1)
            split()

            def last_fill():
                ada(0, GATE2)
                for g in range(POOL_GROUPS):
                    lo(PD_lo[:, g, :], PD[:, g, :], PD_hi[:, g, :])

            pair_values(PAIRS - 2, last_fill, pool_products)
            pair_values(PAIRS - 1, lambda: None, lambda: None)

            clear_acc()
            split()
            for c in range(4):
                for m in range(2):
                    keep_and_add(Y, 2 * c + m)
                split()
            norm_recip(T)
            update_x(0, 0, (0, 1))
            ada(1, SHIFT1)
            norm_recip(T)
            ada(1, SCALE1)

            def ffn(layer, c0, last_layer):
                segs = (0, 1) if c0 == 0 else (1,)
                w = T - c0
                settle()
                chunks_full(segs)
                for half in range(2):
                    with t.loop(dve, 2, job=8, split=4, chain=8) as i:
                        for n in range(4):
                            for m in range(2):
                                job()
                                r = m % 2
                                chain(dve.tensor_tensor(TMP[:, r:r + 1, c0:T], TMP[:, r:r + 1, c0:T],
                                                        TMP[:, r:r + 1, c0:T], ALU.mult))
                                settle()
                                c = bass.ds(i * 8 + (2 * n + m), 1)
                                done(dve.tensor_tensor(HID_lo[:, c, c0:T], TMP[:, r:r + 1, c0:T],
                                                       HID_hi[:, c, c0:T].bitcast(F32), ALU.subtract))
                            split()
                    sums0 = t.first("job")

                    if half:
                        dve.wait_ge(dve_out, part_of("d", t.first("job") - 1))
                        chain(dve.memset(ACC[:, :], 0.0))
                        settle()

                    def two_chunks(i, c, more):
                        if more:
                            split()
                        for m in range(2):
                            job()
                            b = ffn_bank(sums0, t.first("job") - 1)
                            y = Y[:, bass.ds(i * 4 + (2 * c + m), 1), c0:T] if t.reg is not None else \
                                Y[:, 2 * c + m:2 * c + m + 1, c0:T]
                            ps = b[:, 0:w].unsqueeze(1)
                            if not half:
                                done(dve.tensor_copy(y, ps))
                                continue
                            done(dve.tensor_tensor(y, ps, y, ALU.add))
                            t.add("sq")
                            dve.wait_ge(sq_ready, t.at("sq"))
                            dve.wait_ge(acc_done, t.at("acc"))
                            dve.tensor_tensor(ACC[:, c0:T], ACC[:, c0:T], SQ[:, m, c0:T], ALU.add).then_inc(acc_done, 1)
                            t.add("acc")
                        if more:
                            split()

                    if last_layer and half:
                        for c in range(4):
                            two_chunks(0, c, c < 3)
                    else:
                        extra = dict(acc=4, sq=4) if half else {}
                        with t.loop(dve, 2, job=4, split=4, **extra) as i:
                            for c in range(2):
                                two_chunks(i, c, True)
                norm_recip(w, c0)
                update_x(layer, 1, segs)

            t.add("sq", KD)
            ffn(0, 0, False)
            ada(1, GATE1)
            norm_recip(T)
            ada(1, SHIFT2)
            t.add("sq", KD)

            settle()
            chunks_full((0, 1))
            dve.memset(Y[:, :, LAT:T], 0.0).then_inc(y_zero, 1)
            dve.wait_ge(y_zero, 1)
            dve.wait_ge(ret_in, 32)

            def head_qk():
                skip(2)
                dve.wait_ge(act_out, t.evacuated("a", t.first("job") - 1))
                cos = ropeR[:, 0, :].unsqueeze(1).to_broadcast([P, 2, SEG])
                chain(dve.tensor_tensor(ROT[:, :, :], QK[:, 0:2, :], cos, ALU.mult))

            def head_rotated():
                sin = ropeR[:, 1, :].unsqueeze(1).to_broadcast([P, 2, SEG])
                settle()
                b = job()
                done(dve.tensor_tensor(QK[:, 0:2, :], b[:, :].rearrange("p (a n) -> p a n", a=2), sin, ALU.mult))
                dve.wait_ge(dve_out, t.evacuated("d", t.first("job") - 1))
                dve.tensor_tensor(QK[:, 0:2, :], QK[:, 0:2, :], ROT[:, :, :], ALU.add).then_inc(full_ready, 1)
                lo(QK_lo[:, :, :], QK[:, :, :], QK_hi[:, :, :])
                split()

            def head_v():
                for jj in range(2):
                    job_lo(RV_lo[:, 2 * jj:2 * jj + 2, :], RV_hi[:, 2 * jj:2 * jj + 2, :])

            def head_attend():
                t.add("decay")
                dve.wait_ge(decay_in, t.at("decay") * 16)
                for jj in range(2):
                    b = job()
                    s = SA[:, 2 * jj:2 * jj + 2, :]
                    done(dve.tensor_tensor(s, b[:, :].rearrange("p (a n) -> p a n", a=2),
                                           DEC[:, 2 * jj:2 * jj + 2, :], ALU.mult))
                    dve.wait_ge(dve_out, t.evacuated("d", t.first("job") - 1))
                    dve.sem_inc(full_ready, 1)
                for jj in range(2):
                    s = slice(2 * jj, 2 * jj + 2)
                    lo(SA_lo[:, s, :], SA[:, s, :], SA_hi[:, s, :])
                split()
                for tt in range(2):
                    gate = job()
                    chain(dve.tensor_scalar(GE[:, tt, :], GE[:, tt, :], 1.0, None, ALU.add))
                    settle()
                    chain(dve.reciprocal(GE[:, tt, :], GE[:, tt, :]))
                    if tt == 0:
                        settle()
                        done(dve.tensor_tensor(GS[:, tt, :], gate[:, 0:R_DV], GE[:, tt, :], ALU.mult))
                banks = [bank[(t.first("job") + tt) % BANKS] for tt in range(2)]
                for tt in range(2):
                    dve.wait_ge(acc_full, t.at("job", tt + 1))
                    chain(dve.bn_stats(stats[:, tt, :], banks[tt][:, 0:R_DV]))
                settle()
                done(dve.tensor_tensor(GS[:, 1, :], gate[:, 0:R_DV], GE[:, 1, :], ALU.mult))
                for tt in range(2):
                    chain(dve.bn_aggr(mv[:, tt, :], stats[:, tt, :]))
                settle()
                t.add("stat")
                dve.tensor_scalar(mv[:, :, 1], mv[:, :, 1], EPS, None, ALU.add).then_inc(stat_ready, 1)
                dve.wait_ge(rstd_ready, t.at("stat"))
                for tt in range(2):
                    job()
                    done(dve.tensor_scalar(ON[:, tt, :], banks[tt][:, 0:R_DV], mv[:, tt, 0:1], rstd[:, tt:tt + 1],
                                           ALU.subtract, ALU.mult))
                dve.wait_ge(dve_out, t.evacuated("d", t.first("job") - 1))
                dve.tensor_tensor(ON[:, :, :], ON[:, :, :], GS[:, :, :], ALU.mult).then_inc(rows_ready, 1)
                split()

            def head_out():
                for jj in range(4):
                    b = job()
                    y = Y[:, 2 * jj:2 * jj + 2, LAT:T]
                    done(dve.tensor_tensor(y, b[:, :].rearrange("p (a n) -> p a n", a=2), y, ALU.add))

            head_qk()
            head_rotated()
            head_v()
            with t.loop(dve, HEADS - 1, job=16, split=4, chain=9, hi=3, lo=3, decay=1, stat=1):
                head_attend()
                head_qk()
                job_lo(YT_lo[:, :, :], YT_hi[:, :, :])
                head_rotated()
                head_v()
                split()
                head_out()
            head_attend()
            ada(1, SCALE2)
            job_lo(YT_lo[:, :, :], YT_hi[:, :, :])
            head_out()
            split()
            norm_recip(SEG, LAT)
            update_x(1, 0, (1,))
            t.add("sq", 2 * KD)
            ada(1, GATE2)
            norm_recip(SEG, LAT)
            ffn(1, LAT, True)
            skip(4)
            assert t.first("job") == len(JOBS) and t.first("split") == len(SPLIT_AT), (t.n, len(JOBS))


def tables():
    n = np.arange(SEG)
    row, col = (n // 64).astype(np.float64), (n % 64).astype(np.float64)

    def rotary(width):
        d = width // 2
        f = 10000.0 ** (-np.arange(0, d, 2) / d)
        angle = [pos[None, :] * f[:, None] for pos in (row, col)]
        cos = np.concatenate([np.concatenate([np.cos(a)] * 2) for a in angle])
        sin = np.concatenate([np.concatenate([-np.sin(a), np.sin(a)]) for a in angle])
        return cos, sin

    cos, sin = rotary(ROPE)
    att = np.stack([cos, sin], axis=1)
    ret = np.stack(rotary(R_DK), axis=1)
    swap = np.zeros((P, P))
    for a in range(P):
        swap[(a // 64) * 64 + (a + 32) % 64, a] = 1.0
    inv = np.zeros((P, POOL_GROUPS, SEG))
    for g in range(POOL_GROUPS):
        w = 2 << g
        inv[:, g, :] = 1.0 / (np.clip(n + w // 2, 0, SEG) - np.clip(n - w // 2, 0, SEG))
    logs = np.log1p(-np.exp2(-5.0 - np.arange(HEADS)))
    decay = np.zeros((HEADS, P, 4, SEG))
    q = n[None, :]
    for h in range(HEADS):
        f, b = logs[h], logs[HEADS - 1 - h]
        key = n[:, None]
        context = np.exp(f * (q + SEG - key)) + np.exp(b * (SEG - q + key))
        latent = np.where(key <= q, np.exp(f * np.maximum(q - key, 0)), np.exp(b * np.maximum(key - q, 0)))
        both = np.concatenate([context, latent]) * R_DK ** -0.5
        decay[h] = both.reshape(4, P, SEG).transpose(1, 0, 2)
    return {name: np.ascontiguousarray(a, dtype=np.float32) for name, a in
            dict(rope_att=att, rope_ret=ret, swap=swap, pool_inv=inv, decay=decay).items()}


INPUTS = ["x", "c", "ctx", "c_ctx", "w_ada", "b_ada", "g_mix_pre", "g_mix_post", "g_ffn_pre", "g_ffn_post",
          "w_ffn_in", "w_ffn_out", "w_in_even", "g_q_lora", "g_kv_lora", "w_uq", "w_ukv", "w_pool", "pool_scale",
          "w_out_even", "w_in_odd", "w_out_odd"]


def kernel(**inputs):
    import concourse.bacc as bacc
    from concourse.bass_utils import run_bass_kernel_spmd

    nc = bacc.Bacc("TRN2", target_bir_lowering=False, num_devices=1)
    arrays = {name: np.ascontiguousarray(inputs[name]) for name in INPUTS}
    arrays.update(tables())
    arrays = {f"in_{name}": a for name, a in arrays.items()}
    A = {name[3:]: nc.dram_tensor(name, a.shape, mybir.dt.from_np(a.dtype), kind="ExternalInput").ap()
         for name, a in arrays.items()}
    out = nc.dram_tensor("latent_out", (1, SEG, D), F32, kind="ExternalOutput").ap()
    build(nc, A, out)
    result = run_bass_kernel_spmd(nc, [arrays], core_ids=[0])
    return result.results[0]["latent_out"]
```

```python
from contextlib import ExitStack, contextmanager

import numpy as np

import concourse.bass as bass
from concourse import mybir

F32 = mybir.dt.float32
F32R = mybir.dt.float32r
ALU = mybir.AluOpType
ACT = mybir.ActivationFunctionType
AXX = mybir.AxisListType.X

P = 128
D = 1024
KD = D // P
SEG = 256
T = 2 * SEG
LAT = SEG
EPS = 1e-6

Q_LORA, KV_LORA, ROPE, NOPE, VD = 256, 128, 32, 64, 64
HEADS = 8
PAIRS = HEADS // 2
QH = NOPE + ROPE
ATT_SCALE = float(QH) ** -0.5
POOL_GROUPS = 4
POOL0 = Q_LORA + KV_LORA + ROPE
PAD = 8

R_DK, R_DV = 128, 256
R_Q0, R_K0, R_V0, R_G0 = 0, HEADS * R_DK, 2 * HEADS * R_DK, 2 * HEADS * R_DK + HEADS * R_DV

DFF = 4 * D
HALF = DFF // 2
HC = HALF // P
PANEL_COLS = 256
PANEL = KD * PANEL_COLS
RAW_SLOTS = 4
BANKS = 8

SHIFT1, SCALE1, GATE1, SHIFT2, SCALE2, GATE2 = range(6)


def panel_plan():
    ada, one, two = ("ada", 1), ("split", 1), ("split", 2)
    plan = [ada] * 4 + [one] * 2 + [ada] * 4 + [one] * 3 + [two]
    plan += [ada] * 4 * PAIRS
    plan += [one] * 6
    plan += [ada] * 8
    plan += [one] * 30
    plan += [two, one]
    plan += [ada] * 8
    plan += [one, two, one, one] * (HEADS - 1)
    plan += [one, two] + [ada] * 4 + [one] * 2 + [ada] * 4
    plan += [one] * 30
    return plan


PLAN = panel_plan()
SPLIT_AT = [n for n, (kind, _) in enumerate(PLAN) if kind == "split"]
ADA_AT = [n for n, (kind, _) in enumerate(PLAN) if kind == "ada"]


def arrivals(n):
    return 16 * sum(PLAN[m][1] for m in range(n % RAW_SLOTS, n + 1, RAW_SLOTS))


def job_plan():
    norm = [("norm", "ad"), ("root", "")]
    ada = [("ada", "a"), ("ada", "d")]
    jobs = [("params", "d")] * 2 + [("x", "ad")] * KD + ada + norm + ada
    jobs += [("lora", "ad")] * 3 + [("kr", "a")] + norm[:1] * 2
    jobs += [("pool_in", "a")] * 2 + norm[1:] * 2 + [("pool_in", "a")] * 2
    q, k, scores = [("q", "a")] * 2, [("k", "ad")] * 2, [("scores", "a")] * 6
    turn, values = [("turn", "ad")], [("values", "ad")]
    jobs += q + k + [("v", "ad")] * 4 + scores + q + k + ada
    for p in range(1, PAIRS - 1):
        jobs += scores + turn * 4 + q + k + values + turn * 2 + ada + values
    jobs += scores + turn * 4 + ada + values + turn * 2 + [("pool_out", "ad")] * POOL_GROUPS + values
    jobs += turn * 4 + values + turn * 2 + values
    jobs += [("mix_out", "ad")] * KD + norm + ada + norm + ada
    hidden, ffn_out = [("hidden", "ad")] * HC, [("ffn_out", "d")] * KD
    ffn = (hidden + ffn_out) * 2 + norm
    jobs += ffn + ada + norm + ada
    r_qk, swap, r_v = [("r_qk", "a")] * 2, [("r_swap", "d")], [("r_v", "ad")] * 2
    attend = [("r_scores", "d")] * 2 + [("r_gate", "ad")] * 2 + [("r_values", "d")] * 2
    turn, r_out = [("r_turn", "ad")], [("r_out", "d")] * 4
    jobs += r_qk + swap + r_v + (attend + r_qk + turn + swap + r_v + r_out) * (HEADS - 1)
    jobs += attend + ada + turn + r_out
    jobs += norm + ada + norm + hidden + ffn_out + hidden + [("x_rows", "a")] * 4 + ffn_out + norm[:1]
    return jobs


JOBS = job_plan()


def part_of(engine, j):
    return sum(engine in JOBS[m][1] for m in range(j + 1))


def first_job(stage, nth=0):
    starts = [m for m in range(len(JOBS)) if JOBS[m][0] == stage and (m == 0 or JOBS[m - 1][0] != stage)]
    return starts[nth]


def pool_job(g):
    return first_job("pool_in", g // 2) + g % 2


class Tally:

    def __init__(self):
        self.n = {}
        self.reg = None
        self.per = {}

    def at(self, name, more=0):
        v = self.n.get(name, 0) + more
        if self.reg is not None and self.per.get(name, 0):
            return self.reg * self.per[name] + v
        return v

    def evacuated(self, engine, j):
        if self.reg is None:
            return part_of(engine, j)
        rounds_jobs = self.per["job"]
        per = part_of(engine, self.start + rounds_jobs - 1) - part_of(engine, self.start - 1)
        v = part_of(engine, j) if j >= self.start else part_of(engine, j + rounds_jobs) - per
        return self.reg * per + v if per else v

    def first(self, name):
        return self.n.get(name, 0)

    def add(self, name, k=1):
        self.n[name] = self.n.get(name, 0) + k

    @contextmanager
    def loop(self, eng, rounds, **per):
        start = dict(self.n)
        with eng.Fori(0, rounds) as i:
            self.reg, self.per, self.start = i, per, start.get("job", 0)
            yield i
            self.reg = None
        for name in set(self.n) | set(per):
            added = self.n.get(name, 0) - start.get(name, 0)
            assert added == per.get(name, 0), (name, added, per.get(name, 0))
            self.n[name] = start.get(name, 0) + rounds * added


def mm3(pe, out, stat, mov, first, last):
    pe.matmul(out, stat[0], mov[0], start=first, stop=False)
    pe.matmul(out, stat[0], mov[1], start=False, stop=False)
    return pe.matmul(out, stat[1], mov[0], start=False, stop=last)


def build(nc, A, out):
    with ExitStack() as ctx:
        base = [16512]

        def place(name, shape, dt, at=None):
            size = 4 * int(np.prod(shape[1:]))
            if at is None:
                at = base[0]
                base[0] += (size + 31) // 32 * 32
            return nc.alloc_sbuf_tensor_at(name, shape, dt, offset=at)

        X = place("X", [P, KD, T], F32)
        h_hi_at = base[0]
        H_hi = place("H_hi", [P, KD, T], F32R)
        h_lo_at = base[0]
        H_lo = place("H_lo", [P, KD, T], F32R)
        RAW = [place(f"RAW{n}", [P, PANEL], F32) for n in range(RAW_SLOTS)]
        W_hi = [place(f"W_hi{n}", [P, PANEL], F32R) for n in range(2)]
        W_lo = [place(f"W_lo{n}", [P, PANEL], F32R) for n in range(2)]
        big = base[0]
        base[0] += 80 * 1024
        sq_at = base[0]
        SQ = place("SQ", [P, 2, T], F32)
        tmp_at = base[0]
        TMP = place("TMP", [P, 2, T], F32)
        ACC = place("ACC", [P, T], F32, tmp_at + 4 * T)
        RQ = [place("RQ", [P, P], F32)]
        selector = place("selector", [P, 4, P], F32)
        ident = place("ident", [P, P], F32)
        ones = place("ones", [P, P], F32)
        bcol = place("bcol", [P, 96], F32)
        gcol = place("gcol", [P, 88], F32)
        cond = place("cond", [P, KD, 32], F32)
        mod = place("mod", [P, 2, 6, KD, 2], F32)
        pre_gain = place("pre_gain", [P, 2, 2, KD, 2], F32)
        post_gain = place("post_gain", [P, 2, 2, KD, 2], F32)
        adarow = place("adarow", [P, 256], F32)
        RQ.append(adarow)
        small = place("small", [P, 48], F32)
        assert base[0] <= nc.sbuf_usable_end, base[0]
        eps_col = small[:, 0:1]

        xrows = place("xrows", [P, 4, D], F32, big + 16384)
        brows = place("brows", [P, P], F32, big + 32768)
        grows = place("grows", [P, P], F32, big + 32768 + 512)
        silu_e = place("silu_e", [P, 16], F32, big + 32768 + 1024)
        at = [big]

        def region(name, shape, dt):
            t = place(name, shape, dt, at[0])
            at[0] += (4 * int(np.prod(shape[1:])) + 31) // 32 * 32
            return t

        q_at = at[0]
        Q_hi, Q_lo = region("Q_hi", [P, 2, T], F32R), region("Q_lo", [P, 2, T], F32R)
        K_hi, K_lo = region("K_hi", [P, 2, T], F32R), region("K_lo", [P, 2, T], F32R)
        V_hi, V_lo = region("V_hi", [P, 4, T], F32R), region("V_lo", [P, 4, T], F32R)
        QN_hi, QN_lo = region("QN_hi", [P, 3, T], F32R), region("QN_lo", [P, 3, T], F32R)
        lora_at = at[0]
        PROB = region("PROB", [P, 4, T], F32)
        PROBC = region("PROBC", [P, 2, 2, SEG], F32)
        pt_at = at[0]
        PT_hi, PT_lo = region("PT_hi", [P, 4, T], F32R), region("PT_lo", [P, 4, T], F32R)
        QF = region("QF", [P, 2, T], F32)
        SW = region("SW", [P, 2, T], F32)
        assert at[0] <= big + 80 * 1024
        LORA = place("LORA", [P, 3, T], F32, lora_at)
        KR = place("KR", [P, T], F32, lora_at + 12 * T)
        ropeA = place("ropeA", [P, 2, SEG], F32, tmp_at)
        PROBS = [place("PROB_even", [P, 4, T], F32, h_hi_at + 16 * T), PROB]
        PROBCS = [PROBC, place("PROBC_odd", [P, 2, 2, SEG], F32, sq_at)]
        WIDE = SEG + 2 * PAD
        PRAW = place("PRAW", [P, POOL_GROUPS, 2, WIDE], F32, pt_at)
        PS = [place(f"PS{n}", [P, 2, WIDE], F32, pt_at + (POOL_GROUPS + n) * 8 * WIDE) for n in range(3)]
        PD = place("PD", [P, POOL_GROUPS, T], F32, h_lo_at + 16 * T)
        pool_inv = place("pool_inv", [P, POOL_GROUPS, SEG], F32, sq_at)
        PD_hi, PD_lo = place("PD_hi", [P, 4, T], F32R, q_at), place("PD_lo", [P, 4, T], F32R, q_at + 16 * T)
        HID_hi, HID_lo = place("HID_hi", [P, HC, T], F32R, big), place("HID_lo", [P, HC, T], F32R, big + 32768)
        Y = place("Y", [P, KD, T], F32, big + 65536)
        at[0] = big
        QK = region("QK", [P, 3, SEG], F32)
        ROT = region("ROT", [P, 2, SEG], F32)
        QK_hi, QK_lo = region("QK_hi", [P, 3, SEG], F32R), region("QK_lo", [P, 3, SEG], F32R)
        ropeR = region("ropeR", [P, 2, SEG], F32)
        perm = region("perm", [P, P], F32)
        DEC = region("DEC", [P, 4, SEG], F32)
        RV_hi, RV_lo = region("RV_hi", [P, 4, SEG], F32R), region("RV_lo", [P, 4, SEG], F32R)
        SA = region("SA", [P, 4, SEG], F32)
        SA_hi, SA_lo = region("SA_hi", [P, 4, SEG], F32R), region("SA_lo", [P, 4, SEG], F32R)
        GE = region("GE", [P, 2, SEG], F32)
        GS = region("GS", [P, 2, SEG], F32)
        ON = region("ON", [P, 2, SEG], F32)
        YT_hi, YT_lo = region("YT_hi", [P, 2, SEG], F32R), region("YT_lo", [P, 2, SEG], F32R)
        stats = region("stats", [P, 2, 6], F32)
        mv = region("mv", [P, 2, 2], F32)
        rstd = region("rstd", [P, 2], F32)
        neg_half = region("neg_half", [P, 2], F32)
        assert at[0] <= big + 65536
        OUTR = place("OUTR", [P, 2, D], F32, h_hi_at)
        Z = place("Z", [P, KD, SEG], F32, h_lo_at)

        bank = [ctx.enter_context(nc.psum_tensor(f"bank{n}", [P, 512], F32)) for n in range(BANKS)]

        def sem(name):
            return ctx.enter_context(nc.semaphore(name))

        raw_in = [sem(f"raw_in{n}") for n in range(RAW_SLOTS)]
        split_hi, split_lo = sem("split_hi"), sem("split_lo")
        half_sum, ada_used = sem("half_sum"), sem("ada_used")
        acc_full, act_out, dve_out = sem("acc_full"), sem("act_out"), sem("dve_out")
        full_ready, hi_ready, lo_ready = sem("full_ready"), sem("hi_ready"), sem("lo_ready")
        modulated, gains_ready = sem("modulated"), sem("gains_ready")
        sq_ready, ones_done, acc_done = sem("sq_ready"), sem("ones_done"), sem("acc_done")
        x_ready, rowmax, normalised = sem("x_ready"), sem("rowmax"), sem("normalised")
        params_issued = sem("params_issued")
        params_in, x_in, consts_in, ret_in = sem("params_in"), sem("x_in"), sem("consts_in"), sem("ret_in")
        inv_in, rows_zero, ident_ready = sem("inv_in"), sem("rows_zero"), sem("ident_ready")
        cond_e, cond_ready = sem("cond_e"), sem("cond_ready")
        act_chain, dve_chain, pool_chain = sem("act_chain"), sem("dve_chain"), sem("pool_chain")
        pool_d = sem("pool_d")
        rows_ready = sem("rows_ready")
        z_ready, z_turned, result_ready = sem("z_ready"), sem("z_turned"), sem("result_ready")
        decay_in, stat_ready, rstd_ready, y_zero = sem("decay_in"), sem("stat_ready"), sem("rstd_ready"), sem("y_zero")
        out_done = sem("out_done")

        def by_chunk(w):
            return w.rearrange("(k p) n -> p k n", p=P)

        ada_v = [by_chunk(A["w_ada"][l]) for l in range(2)]
        in_even = by_chunk(A["w_in_even"][0])
        out_even = by_chunk(A["w_out_even"][0])
        in_odd = by_chunk(A["w_in_odd"][0])
        out_odd = by_chunk(A["w_out_odd"][0])
        ffn_in = [by_chunk(A["w_ffn_in"][l]) for l in range(2)]
        ffn_out = [by_chunk(A["w_ffn_out"][l]) for l in range(2)]
        IN_PANELS = (0, 256, POOL0, POOL0 + 256)

        def w8(pair, s, k, c0, n):
            at = k * PANEL_COLS + c0
            return pair[0][s % 2][:, at:at + n], pair[1][s % 2][:, at:at + n]

        WW = (W_hi, W_lo)
        HH = (H_hi, H_lo)

        def h_buffer(k):
            return (TMP, SQ)[k % 4 // 2][:, k % 2, :]

        def ffn_bank(first, j):
            return bank[(first + (j - first) % 4) % BANKS]

        def row_bank(half, tt):
            return bank[(first_job("x_rows") + 2 * half + tt) % BANKS]

        block = ctx.enter_context(nc.Block())

        @block.sync
        def _(sp):
            t = Tally()

            def load(*pairs):
                n = t.first("panel")
                slot = n % RAW_SLOTS
                kind, dmas = PLAN[n]
                assert dmas == len(pairs)
                if n >= RAW_SLOTS:
                    splits = sum(m <= n - RAW_SLOTS for m in SPLIT_AT)
                    adas = sum(m <= n - RAW_SLOTS for m in ADA_AT)
                    if t.reg is not None:
                        before = [PLAN[m][0] for m in range(n - RAW_SLOTS, n)]
                        assert before[0] == "ada" or "ada" not in before
                        splits = t.reg * RAW_SLOTS + (t.first("split") - 3)
                        sp.wait_ge(split_lo, splits)
                    elif splits:
                        sp.wait_ge(split_lo, splits)
                    if adas:
                        sp.wait_ge(ada_used, adas)
                for c0, src in pairs:
                    size = int(np.prod(src.shape[1:]))
                    dst = RAW[slot][:, c0:c0 + size]
                    if len(src.shape) == 3:
                        dst = dst.rearrange("p (k n) -> p k n", k=src.shape[1])
                    sp.dma_start(dst, src).then_inc(raw_in[slot], 16)
                t.add("panel")
                t.add("split", kind == "split")

            def ada(layer, part):
                for kk in range(4):
                    load((0, ada_v[layer][:, 2 * kk:2 * kk + 2, part * D:(part + 1) * D]))

            def ffn_panel(layer, n):
                load((0, ffn_in[layer][:, :, n * 256:(n + 1) * 256]))

            def ffn(layer, last):
                for n in range(2, 8):
                    ffn_panel(layer, n)
                for half in range(2):
                    if half:
                        with t.loop(sp, 2, panel=4, split=4) as i:
                            for n in range(4):
                                load((0, ffn_in[layer][:, :, bass.ds(i * 1024 + (HALF + n * 256), 256)]))
                    if last and half:
                        for c in range(4):
                            for kg in range(2):
                                load((0, ffn_out[layer][:, 16 * half + 8 * kg:16 * half + 8 * kg + 8,
                                                        c * 256:(c + 1) * 256]))
                        continue
                    with t.loop(sp, 2, panel=4, split=4) as i:
                        for n in range(4):
                            k0 = 16 * half + 8 * (n % 2)
                            load((0, ffn_out[layer][:, k0:k0 + 8, bass.ds(i * 512 + (n // 2) * 256, 256)]))

            def head_qk(h):
                q = in_odd[:, :, bass.ds(h * R_DK + R_Q0, R_DK)] if not isinstance(h, int) else \
                    in_odd[:, :, R_Q0 + h * R_DK:R_Q0 + (h + 1) * R_DK]
                k = in_odd[:, :, bass.ds(h * R_DK + R_K0, R_DK)] if not isinstance(h, int) else \
                    in_odd[:, :, R_K0 + h * R_DK:R_K0 + (h + 1) * R_DK]
                load((0, q), (KD * R_DK, k))

            for n, name in enumerate(("ctx", "x")):
                sp.dma_start(xrows[:, 2 * n:2 * n + 2, :], A[name][0].rearrange("(t p) n -> p t n", p=P))\
                  .then_inc(x_in, 16)
            sp.wait_ge(params_issued, 1)
            ada(0, SHIFT1)
            for c0 in IN_PANELS[:2]:
                load((0, in_even[:, :, c0:c0 + 256]))
            ada(0, SCALE1)
            for c0 in IN_PANELS[2:]:
                load((0, in_even[:, :, c0:c0 + 256]))
            load((0, by_chunk(A["w_uq"][0])))
            load((0, by_chunk(A["w_ukv"][0])), (D, A["w_pool"][0].rearrange("g p n -> p g n")))
            for part in (GATE1, SHIFT2, SCALE2, GATE2):
                ada(0, part)
            for c in range(4):
                load((0, out_even[:, :, c * 256:(c + 1) * 256]))
            ffn_panel(0, 0)
            ffn_panel(0, 1)
            ada(1, SHIFT1)
            ada(1, SCALE1)
            ffn(0, False)

            def head_cols(h, first):
                c = bass.ds(h * R_DV + first, R_DV) if not isinstance(h, int) else \
                    slice(first + h * R_DV, first + (h + 1) * R_DV)
                load((0, in_odd[:, :, c]))

            head_qk(0)
            head_cols(0, R_V0)
            ada(1, GATE1)
            ada(1, SHIFT2)
            with t.loop(sp, HEADS - 1, panel=4, split=4) as h:
                head_cols(h, R_G0)
                head_qk(h + 1)
                head_cols(h + 1, R_V0)
                load((0, out_odd[:, bass.ds(h * 2, 2), :]))
            head_cols(HEADS - 1, R_G0)
            load((0, out_odd[:, 2 * HEADS - 2, :]), (D, out_odd[:, 2 * HEADS - 1, :]))
            ada(1, SCALE2)
            ffn_panel(1, 0)
            ffn_panel(1, 1)
            ada(1, GATE2)
            ffn(1, True)
            for n in range(4):
                sp.wait_ge(result_ready, n + 1)
                tt, half = n % 2, n // 2
                sp.dma_start(out[0, tt * P:(tt + 1) * P, half * 512:(half + 1) * 512],
                             OUTR[:, tt, half * 512:(half + 1) * 512]).then_inc(out_done, 16)
            sp.wait_ge(out_done, 64)

        @block.gpsimd
        def _(pool):
            t = Tally()

            def chain(ins):
                ins.then_inc(pool_chain, 1)
                t.add("chain")
                pool.wait_ge(pool_chain, t.at("chain"))

            pool.memset(brows[:, :], 0.0).then_inc(rows_zero, 1)
            pool.memset(grows[:, :], 0.0).then_inc(rows_zero, 1)
            pool.memset(cond[:, :, :], 0.0).then_inc(rows_zero, 1)
            pool.memset(eps_col, EPS).then_inc(rows_zero, 1)
            pool.memset(ones[:, :], 1.0).then_inc(rows_zero, 1)
            chain(pool.memset(ident[:, :], 0.0))
            pool.affine_select(out=ident[:, :], in_=ident[:, :], compare_op=ALU.not_equal, fill=1.0, base=0,
                               pattern=[[-1, P]], channel_multiplier=1).then_inc(ident_ready, 1)

            chain(pool.memset(selector[:, :, :], 0.0))
            for j in range(4):
                pool.memset(selector[32 * j:32 * j + 1, j, :], 1.0).then_inc(rows_zero, 1)
                pool.wait_ge(rows_zero, 6 + j)
            pool.memset(PRAW[:, :, :, :], 0.0).then_inc(rows_zero, 1)
            pool.wait_ge(lo_ready, KD)
            pool.dma_start(ropeA[NOPE:QH, :, :], A["rope_att"]).then_inc(consts_in, 16)
            pool.wait_ge(act_out, part_of("a", first_job("norm", 1) + 1))
            pool.dma_start(pool_inv[:, :, :], A["pool_inv"]).then_inc(inv_in, 16)
            pool.wait_ge(inv_in, 16)
            def windows(g, a, b):
                pool.wait_ge(act_out, part_of("a", pool_job(g)))
                raw = PRAW[:, g, :, :]
                lo, hi = 1, WIDE - 1
                chain(pool.tensor_tensor(a[:, :, lo:hi], raw[:, :, lo - 1:hi - 1], raw[:, :, lo:hi], ALU.add))
                for step in range(g):
                    d = 1 << step
                    lo, hi = lo + d, hi - d
                    chain(pool.tensor_tensor(b[:, :, lo:hi], a[:, :, lo - d:hi - d], a[:, :, lo + d:hi + d], ALU.add))
                    a, b = b, a
                inv = pool_inv[:, g, :].unsqueeze(1).to_broadcast([P, 2, SEG])
                chain(pool.tensor_tensor(b[:, :, PAD:PAD + SEG], a[:, :, PAD:PAD + SEG], inv, ALU.mult))
                return b

            def less_token(g, means):
                pool.tensor_tensor(PD[:, g, :].rearrange("p (s n) -> p s n", s=2), means[:, :, PAD:PAD + SEG],
                                   PRAW[:, g, :, PAD:PAD + SEG], ALU.subtract).then_inc(pool_d, 1)
                t.add("group")
                pool.wait_ge(pool_d, t.at("group"))

            means = {1: windows(1, PS[0], PS[1]), 0: windows(0, PS[1], PS[2])}
            pool.wait_ge(act_out, part_of("a", pool_job(POOL_GROUPS - 1)))
            less_token(1, means[1])
            less_token(0, means[0])
            for g in (3, 2):
                less_token(g, windows(g, PS[0], PS[1]))

            pool.wait_ge(dve_out, part_of("d", first_job("norm", 4) - 1))
            pool.dma_start(ropeR[:, :, :], A["rope_ret"]).then_inc(ret_in, 16)
            pool.dma_start(perm[:, :], A["swap"]).then_inc(ret_in, 16)

            pool.wait_ge(x_ready, 2 * KD)
            pool.memset(Y[:, :, LAT:T], 0.0).then_inc(y_zero, 1)
            pool.wait_ge(y_zero, 1)

            chain(pool.memset(neg_half[:, :], -0.5))
            with t.loop(pool, HEADS, head=1):
                t.add("head")
                pool.wait_ge(stat_ready, t.at("head"))
                pool.tensor_tensor(rstd[:, :], mv[:, :, 1], neg_half[:, :], ALU.pow).then_inc(rstd_ready, 1)

        @block.tensor
        def _(pe):
            t = Tally()
            depth = [BANKS]

            def open_job(ahead=0):
                j = t.first("job") + ahead
                if j >= depth[0]:
                    wait_job(j - depth[0])
                return bank[j % BANKS]

            def wait_job(j):
                m = j if t.reg is None or j >= t.start else j + t.per["job"]
                if "d" in JOBS[m][1]:
                    pe.wait_ge(dve_out, t.evacuated("d", j))
                else:
                    pe.wait_ge(act_out, t.evacuated("a", j))

            def close_job(ins):
                ins.then_inc(acc_full, 1)
                t.add("job")

            def wait_panel():
                pe.wait_ge(split_lo, t.at("split", 1))
                return t.first("split")

            def wait_lo(k=1):
                t.add("lo", k)
                pe.wait_ge(lo_ready, t.at("lo"))

            def ada(layer, part):
                b = open_job()
                for kk in range(4):
                    n = ADA_AT[t.first("ada")]
                    pe.wait_ge(raw_in[n % RAW_SLOTS], arrivals(n))
                    raw = RAW[n % RAW_SLOTS]
                    for k2 in range(2):
                        for j in range(4):
                            ins = pe.matmul(b[32 * j:32 * j + 32, 0:256], cond[:, 2 * kk + k2, :],
                                            raw[:, k2 * 1024 + j * 256:k2 * 1024 + (j + 1) * 256],
                                            start=(kk == 0 and k2 == 0), stop=(kk == 3 and k2 == 1))
                    t.add("ada")
                    if kk < 3:
                        ins.then_inc(ada_used, 1)
                close_job(ins)
                b = open_job()
                wait_job(t.first("job") - 1)
                pe.transpose(b[:, 0:P], adarow[:, 0:P], ident[:, :]).then_inc(ada_used, 1)
                close_job(pe.transpose(b[:, P:2 * P], adarow[:, P:2 * P], ident[:, :]))

            def sum_quarters(b, squares, width, c0, first, last):
                w = width // 4
                for j in range(4):
                    ins = pe.matmul(b[32 * j:32 * j + 32, 0:w], ones[:, 0:32],
                                    squares[:, c0 + j * w:c0 + (j + 1) * w], start=first, stop=last)
                return ins

            def root(width, norm_job=None, place=0):
                wait_job(t.first("job") - 1 if norm_job is None else norm_job)
                b = open_job()
                w = width // 4
                for j in range(4):
                    ins = pe.matmul(b[:, j * w:(j + 1) * w], selector[:, j, :], RQ[place][:, 0:w], start=True,
                                    stop=True)
                close_job(ins)

            def sum_squares(count, width, c0=0, jobs=None):
                b = open_job()
                for k in range(count):
                    if jobs is None:
                        t.add("sq")
                        pe.wait_ge(sq_ready, t.at("sq"))
                    else:
                        pe.wait_ge(act_out, part_of("a", jobs + k))
                    ins = sum_quarters(b, SQ[:, k % 2, :], width, c0, k == 0, k == count - 1)
                    if k < count - 1:
                        ins.then_inc(ones_done, 1)
                close_job(ins)

            def sum_acc(width, c0=0, from_sbuf=True):
                t.add("acc", KD)
                t.add("sq", KD * from_sbuf)
                pe.wait_ge(acc_done, t.at("acc"))
                b = open_job()
                close_job(sum_quarters(b, ACC, width, c0, True, True))

            pe.wait_ge(ident_ready, 1)
            pe.wait_ge(params_in, 16 * 10)
            for rows in (brows, grows):
                b = open_job()
                close_job(pe.transpose(b[:, 0:P], rows[:, :], ident[:, :]))
            pe.wait_ge(x_in, 32)
            for k in range(KD):
                b = open_job()
                for tt in range(4):
                    ins = pe.transpose(b[:, tt * P:(tt + 1) * P], xrows[:, tt, k * P:(k + 1) * P], ident[:, :])
                close_job(ins)
            pe.wait_ge(cond_ready, 2)
            ada(0, SHIFT1)
            sum_acc(T, from_sbuf=False)
            pe.wait_ge(rows_zero, 9)
            root(T)
            ada(0, SCALE1)

            def side_by_side(stats, movs, first, last, ahead=0):
                banks = [open_job(ahead), open_job(ahead + 1)]

                def products(k):
                    for m in range(2):
                        mov = movs[m](k)
                        ins = mm3(pe, banks[m][:, 0:mov[0].shape[-1]], stats(k, m), mov, k == first, k == last)
                        if k == last:
                            close_job(ins)
                return products

            def pair_of_jobs(ready, stats, movs):
                products = side_by_side(stats, movs, 0, KD - 1)
                for k in range(KD):
                    ready(k)
                    products(k)

            def project(s, c0):
                b = open_job()
                for k in range(KD):
                    ins = mm3(pe, b[:, :], w8(WW, s, k, c0, P), (H_hi[:, k, :], H_lo[:, k, :]), k == 0, k == KD - 1)
                return ins

            full_h = lambda k: (H_hi[:, k, :], H_lo[:, k, :])

            s = wait_panel()
            pair_of_jobs(lambda k: wait_lo(), lambda k, m: w8(WW, s, k, m * P, P), [full_h, full_h])
            t.add("split")
            s = wait_panel()
            close_job(project(s, 0))
            close_job(project(s, NOPE))
            t.add("split")
            sum_squares(2, T, jobs=first_job("lora"))
            sum_squares(1, T, jobs=first_job("lora") + 2)
            for n in range(2):
                s = wait_panel()
                close_job(project(s, 0))
                close_job(project(s, P))
                t.add("split")
                if n == 0:
                    for place in range(2):
                        root(T, first_job("norm", 1) + place, place)

            def pair_q(p):
                for hh in range(2):
                    b = open_job()
                    for k in range(2):
                        c0 = k * HEADS * QH + (2 * p + hh) * QH
                        ins = mm3(pe, b[0:QH, :], (W_hi[uq][:, c0:c0 + QH], W_lo[uq][:, c0:c0 + QH]),
                                  (QN_hi[:, k, :], QN_lo[:, k, :]), k == 0, k == 1)
                    close_job(ins)

            def pair_k(p):
                for hh in range(2):
                    b = open_job()
                    c0 = (2 * p + hh) * P
                    close_job(mm3(pe, b[:, :], (W_hi[ukv][:, c0:c0 + P], W_lo[ukv][:, c0:c0 + P]),
                                  (QN_hi[:, 2, :], QN_lo[:, 2, :]), True, True))

            pe.wait_ge(split_lo, t.at("split", 1))
            uq, ukv = t.first("split") % 2, (t.first("split") + 1) % 2
            wait_lo(3)
            pair_q(0)
            pe.wait_ge(split_lo, t.at("split", 2))
            t.add("split", 2)
            pair_k(0)
            v_cols = [w[ukv][:, 0:1024].rearrange("p (h x e) -> p h x e", h=HEADS, x=2)[:, :, 1, :] for w in WW]
            for tt in range(4):
                b = open_job()
                cs = slice(tt * P, (tt + 1) * P)
                close_job(mm3(pe, b[:, :], (QN_hi[:, 2, cs], QN_lo[:, 2, cs]), v_cols, True, True))

            def pair_scores(p):
                wait_lo(1)
                for tt in range(2):
                    for hh in range(2):
                        b = open_job()
                        cs = slice(LAT + tt * P, LAT + (tt + 1) * P)
                        close_job(mm3(pe, b[:, :], (Q_hi[0:QH, hh, cs], Q_lo[0:QH, hh, cs]),
                                      (K_hi[0:QH, hh, :], K_lo[0:QH, hh, :]), True, True))
                for tt in range(2):
                    b = open_job()
                    cs = slice(tt * P, (tt + 1) * P)
                    for hh in range(2):
                        ins = mm3(pe, b[:, hh * SEG:(hh + 1) * SEG], (Q_hi[0:QH, hh, cs], Q_lo[0:QH, hh, cs]),
                                  (K_hi[0:QH, hh, 0:SEG], K_lo[0:QH, hh, 0:SEG]), True, True)
                    close_job(ins)

            def turn(p, context, kt):
                b = open_job()
                for hh in range(2):
                    for tt in range(2):
                        c = (hh * 2 + tt) * P
                        src = PROBCS[p % 2][:, tt, hh, :] if context else PROBS[p % 2][:, tt * 2 + hh, :]
                        ins = pe.transpose(b[:, c:c + P], src[:, kt * P:(kt + 1) * P], ident[:, :])
                close_job(ins)

            def values(p, tiles, slot0, last_turn):
                wait_job(last_turn)
                b = open_job()
                vs = slice(p * P, (p + 1) * P)
                for kt in tiles:
                    ins = mm3(pe, b[:, :], (V_hi[:, kt, vs], V_lo[:, kt, vs]),
                              (PT_hi[:, slot0 + kt, :], PT_lo[:, slot0 + kt, :]), kt == tiles[0], kt == tiles[-1])
                close_job(ins)

            def pair_values(p, first_filler, second_filler):
                pe.wait_ge(normalised, 6 * (p + 1))
                for kt in range(2):
                    turn(p, True, kt)
                context_turn = t.first("job") - 1
                for kt in range(2):
                    turn(p, False, kt)
                first_filler()
                values(p, (0, 1), 2, context_turn)
                for kt in range(2, 4):
                    turn(p, False, kt)
                latent_turn = t.first("job") - 1
                second_filler()
                values(p, (0, 1, 2, 3), 0, latent_turn)

            def next_qk(p):
                pair_q(p)
                pair_k(p)

            wait_lo(1)
            wait_job(first_job("k", 0) + 1)
            pair_scores(0)
            next_qk(1)
            ada(0, GATE1)
            for p in range(1, PAIRS - 1):
                wait_job(first_job("k", p) + 1)
                pair_scores(p)
                pair_values(p - 1, lambda: next_qk(p + 1), lambda: ada(0, (GATE1, SHIFT2, SCALE2)[p]))

            def pool_products():
                wait_lo(POOL_GROUPS)
                for g in range(POOL_GROUPS):
                    b = open_job()
                    c0 = D + g * P
                    close_job(mm3(pe, b[:, :], (W_hi[ukv][:, c0:c0 + P], W_lo[ukv][:, c0:c0 + P]),
                                  (PD_hi[:, g, :], PD_lo[:, g, :]), True, True))

            wait_job(first_job("k", PAIRS - 1) + 1)
            pair_scores(PAIRS - 1)
            pair_values(PAIRS - 2, lambda: ada(0, GATE2), pool_products)

            s = wait_panel()
            stats = lambda k, m: w8(WW, s, k, m * P, P)
            first_sums = []

            def first_pairs():
                first_sums.append(side_by_side(stats, [full_h, full_h], 0, PAIRS - 1, ahead=4))
                for k in range(PAIRS - 1):
                    first_sums[0](k)

            def pool_groups():
                for g in range(POOL_GROUPS):
                    first_sums[0](PAIRS + g)

            wait_job(t.first("job") - 1)
            pair_values(PAIRS - 1, first_pairs, pool_groups)
            wait_job(t.first("job") - 1)
            first_sums[0](PAIRS - 1)
            t.add("split")
            for _ in range(3):
                s = wait_panel()
                close_job(project(s, 0))
                close_job(project(s, P))
                t.add("split")
            sum_acc(T, from_sbuf=False)
            root(T)
            ada(1, SHIFT1)
            sum_squares(KD, T)
            root(T)
            ada(1, SCALE1)

            def ffn(c0, last_layer):
                w = T - c0
                depth[0] = 4
                lo0 = t.first("lo")
                t.add("lo", KD)
                for half in range(2):
                    hidden0 = t.first("job")
                    with t.loop(pe, 2, job=8, split=4):
                        for n in range(4):
                            s = wait_panel()
                            chunk = lambda k: (H_hi[:, k, c0:T], H_lo[:, k, c0:T])
                            if n == 0 and half == 0:
                                pair_of_jobs(lambda k: pe.wait_ge(lo_ready, lo0 + k + 1),
                                             lambda k, m: w8(WW, s, k, m * P, P), [chunk, chunk])
                                t.add("split")
                                continue
                            for m in range(2):
                                b = open_job()
                                for k in range(KD):
                                    ins = mm3(pe, b[:, 0:w], w8(WW, s, k, m * P, P), chunk(k), k == 0, k == KD - 1)
                                close_job(ins)
                            t.add("split")
                    if last_layer and half:
                        for part in range(2):
                            for tt in range(2):
                                b = open_job()
                                for k in range(4):
                                    ins = pe.transpose(b[:, k * P:(k + 1) * P],
                                                       X[:, part * 4 + k, LAT + tt * P:LAT + (tt + 1) * P],
                                                       ident[:, :])
                                close_job(ins)
                    sums0 = t.first("job")

                    def two_chunks():
                        banks = []
                        for kg in range(2):
                            s = wait_panel()
                            pe.wait_ge(dve_out, part_of("d", hidden0 + 8 * kg + 7))
                            for m in range(2):
                                if kg == 0:
                                    j = t.first("job")
                                    if m == 0:
                                        wait_job(j - 3)
                                    banks.append(ffn_bank(sums0, j + m))
                                for k in range(KD):
                                    ins = mm3(pe, banks[m][:, 0:w], w8(WW, s, k, m * P, P),
                                              (HID_hi[:, kg * 8 + k, c0:T], HID_lo[:, kg * 8 + k, c0:T]),
                                              kg == 0 and k == 0, kg == 1 and k == KD - 1)
                                if kg == 1:
                                    ins.then_inc(acc_full, 1)
                                    t.add("job")
                                elif m == 1:
                                    ins.then_inc(half_sum, 1)
                            t.add("split")

                    def turn_two(c):
                        for k in (2 * c, 2 * c + 1):
                            pe.wait_ge(z_ready, k + 1)
                            for tt in range(2):
                                ins = pe.transpose(row_bank(k // 4, tt)[:, k % 4 * P:(k % 4 + 1) * P],
                                                   Z[:, k, tt * P:(tt + 1) * P], ident[:, :])
                        return ins

                    if last_layer and half:
                        for c in range(4):
                            two_chunks()
                            if c == 0:
                                pe.wait_ge(act_out, part_of("a", sums0 - 1))
                            else:
                                turn_two(c - 1)
                        turn_two(3).then_inc(z_turned, 1)
                    else:
                        with t.loop(pe, 2, job=4, split=4):
                            two_chunks()
                            two_chunks()
                if not last_layer:
                    sum_acc(w, c0)
                    root(w)
                    return
                t.add("acc", KD)
                pe.wait_ge(acc_done, t.at("acc"))
                b = open_job()
                for tt in range(2):
                    ins = pe.matmul(b[:, 2 * tt:2 * tt + 2], ACC[:, LAT + tt * P:LAT + (tt + 1) * P], ones[:, 0:2],
                                    start=True, stop=True)
                close_job(ins)

            ffn(0, False)
            ada(1, GATE1)
            sum_squares(KD, T)
            root(T)
            ada(1, SHIFT2)

            def qk_weights(s, k, m):
                at = (m * KD + k) * R_DK
                return [w[s % 2][:, at:at + R_DK] for w in WW]

            q_and_k = [lambda k: (H_hi[:, k, LAT:T], H_lo[:, k, LAT:T]), lambda k: (H_hi[:, k, :], H_lo[:, k, :])]

            def head_qk():
                s = wait_panel()
                for m, width in enumerate((SEG, T)):
                    b = open_job()
                    for k in range(KD):
                        ins = mm3(pe, b[:, 0:width], qk_weights(s, k, m), q_and_k[m](k), k == 0, k == KD - 1)
                    close_job(ins)
                t.add("split")

            def head_swap(qk_job):
                wait_job(qk_job)
                b = open_job()
                close_job(pe.matmul(b[:, :], perm[:, :], QK[:, 0:2, :], start=True, stop=True))

            def head_tokens(s, b, col, tile):
                for k in range(KD):
                    cs = slice(tile * P, (tile + 1) * P)
                    ins = mm3(pe, b[:, col:col + 256], (H_hi[:, k, cs], H_lo[:, k, cs]), w8(WW, s, k, 0, 256),
                              k == 0, k == KD - 1)
                return ins

            def head_v():
                s = wait_panel()
                for jj in range(2):
                    b = open_job()
                    head_tokens(s, b, 0, 2 * jj)
                    close_job(head_tokens(s, b, 256, 2 * jj + 1))
                t.add("split")

            def head_attend():
                wait_lo(1)
                for jj in range(2):
                    b = open_job()
                    for n in range(2):
                        part = 2 if jj == 0 else 1
                        ins = mm3(pe, b[:, n * SEG:(n + 1) * SEG],
                                  (QK_hi[:, part, n * P:(n + 1) * P], QK_lo[:, part, n * P:(n + 1) * P]),
                                  (QK_hi[:, 0, :], QK_lo[:, 0, :]), True, True)
                    close_job(ins)
                s = wait_panel()
                for tt in range(2):
                    b = open_job()
                    close_job(head_tokens(s, b, 0, 2 + tt))
                t.add("split")
                wait_lo(2)
                for tt in range(2):
                    b = open_job()
                    for kt in range(4):
                        cs = slice(tt * P, (tt + 1) * P)
                        ins = mm3(pe, b[:, 0:R_DV], (SA_hi[:, kt, cs], SA_lo[:, kt, cs]),
                                  (RV_hi[:, kt, :], RV_lo[:, kt, :]), kt == 0, kt == 3)
                    close_job(ins)

            def head_turn():
                t.add("rows")
                pe.wait_ge(rows_ready, t.at("rows"))
                b = open_job()
                for c in range(2):
                    for tt in range(2):
                        ins = pe.transpose(b[:, (c * 2 + tt) * P:(c * 2 + tt + 1) * P],
                                           ON[:, tt, c * P:(c + 1) * P], ident[:, :])
                close_job(ins)

            def head_out(turn_job):
                s = wait_panel()
                wait_job(turn_job)
                for jj in range(4):
                    b = open_job()
                    for n in range(2):
                        for c in range(2):
                            c0 = c * D + (2 * jj + n) * P
                            ins = mm3(pe, b[:, n * SEG:(n + 1) * SEG], [w[s % 2][:, c0:c0 + P] for w in WW],
                                      (YT_hi[:, c, :], YT_lo[:, c, :]), c == 0, c == 1)
                    close_job(ins)
                t.add("split")

            s = wait_panel()
            pair_of_jobs(lambda k: wait_lo(), lambda k, m: qk_weights(s, k, m), q_and_k)
            t.add("split")
            pe.wait_ge(ret_in, 32)
            head_swap(t.first("job") - 1)
            head_v()
            depth[0] = BANKS
            with t.loop(pe, HEADS - 1, job=16, split=4, lo=3, rows=1):
                head_attend()
                head_qk()
                head_turn()
                head_swap(t.first("job") - 2)
                head_v()
                head_out(t.first("job") - 4)
            head_attend()
            ada(1, SCALE2)
            head_turn()
            head_out(t.first("job") - 1)
            sum_squares(KD, SEG, LAT)
            root(SEG)
            ada(1, GATE2)
            sum_squares(KD, SEG, LAT)
            root(SEG)
            ffn(LAT, True)

            assert t.first("job") == len(JOBS) and t.first("split") == len(SPLIT_AT), (t.n, len(JOBS))

        @block.scalar
        def _(act):
            t = Tally()

            def split():
                act.wait_ge(acc_full, t.at("job"))
                s = t.first("split")
                n = SPLIT_AT[s]
                v = arrivals(n)
                if t.reg is not None:
                    v = t.reg * (16 * PLAN[n + RAW_SLOTS][1]) + v
                act.wait_ge(raw_in[n % RAW_SLOTS], v)
                act.activation(W_hi[s % 2][:, :], RAW[n % RAW_SLOTS][:, :], ACT.Copy).then_inc(split_hi, 1)
                t.add("split")

            def split_part(cols):
                s = t.first("split")
                n = SPLIT_AT[s]
                act.wait_ge(raw_in[n % RAW_SLOTS], arrivals(n))
                act.activation(W_hi[s % 2][:, 0:cols], RAW[n % RAW_SLOTS][:, 0:cols], ACT.Copy).then_inc(split_hi, 1)
                t.add("split")

            def job():
                t.add("job")
                act.wait_ge(acc_full, t.at("job"))
                return bank[(t.first("job") - 1) % BANKS]

            def skip(k=1):
                t.add("job", k)

            def done(ins):
                ins.then_inc(act_out, 1)

            def squares_free(n):
                if n >= 2:
                    act.wait_ge(ones_done, t.first("ones") + n - 1)

            def norm_root(width, n, place=0):
                w = width // 4
                b = job()
                done(act.activation(RQ[place][:, 0:w], b[:, 0:w], ACT.Sqrt, bias=eps_col, scale=1.0 / n))

            def job_square(k):
                b = job()
                if k >= 2:
                    act.wait_ge(acc_done, t.first("acc") + k - 1)
                done(act.activation(SQ[:, k % 2, :], b[:, :], ACT.Square))

            def hi(out, in_):
                t.add("full")
                act.wait_ge(full_ready, t.at("full"))
                act.activation(out, in_, ACT.Copy).then_inc(hi_ready, 1)

            def warm(column, function):
                act.activation(small[:, column:column + 1], eps_col, function)

            def ada():
                b = job()
                done(act.activation(adarow[:, :], b[:, 0:256], ACT.Copy))
                skip()

            def chunks_hi(layer, which, part_shift, segs, midway=None):
                c0 = segs[0] * SEG
                def hi_of(k):
                    t.add("modulated")
                    act.wait_ge(modulated, t.at("modulated"))
                    act.activation(H_hi[:, k, c0:T], h_buffer(k)[:, c0:T], ACT.Copy).then_inc(hi_ready, 1)

                for k in range(KD + 1):
                    if midway and k == midway[0]:
                        midway[1]()
                    if k == 1:
                        hi_of(0)
                    if k < KD:
                        t.add("full")
                        act.wait_ge(full_ready, t.at("full"))
                        h = h_buffer(k)
                        for s in segs:
                            cs = slice(s * SEG, (s + 1) * SEG)
                            ins = act.activation(h[:, cs], h[:, cs], ACT.Identity,
                                                 bias=mod[:, layer, part_shift, k, s:s + 1],
                                                 scale=pre_gain[:, layer, which, k, s:s + 1])
                        ins.then_inc(modulated, 1)
                    if k >= 2:
                        hi_of(k - 1)

            def squares_of_x(c0, n0):
                for k in range(KD):
                    act.wait_ge(x_ready, n0 + k + 1)
                    squares_free(k)
                    act.activation(SQ[:, k % 2, c0:T], X[:, k, c0:T], ACT.Square).then_inc(sq_ready, 1)
                t.add("ones", KD - 1)

            act.wait_ge(rows_zero, 2)
            act.dma_start(brows[0:96, :], A["b_ada"].rearrange("l (c p) -> (l c) p", p=P)).then_inc(params_in, 16)
            r = 0
            for name in ("g_mix_pre", "g_mix_post", "g_ffn_pre", "g_ffn_post", "g_q_lora", "g_kv_lora",
                         "pool_scale", "c", "c_ctx"):
                src = A[name] if len(A[name].shape) == 2 else A[name].rearrange("(a n) -> a n", a=1)
                rows = src.shape[0] * src.shape[1] // P
                act.dma_start(grows[r:r + rows, :], src.rearrange("l (c p) -> (l c) p", p=P)).then_inc(params_in, 16)
                r += rows
            act.sem_inc(params_issued, 1)
            skip(2)
            act.wait_ge(cond_e, 1)
            act.activation(silu_e[:, :], gcol[:, 71:87], ACT.Exp, scale=-1.0).then_inc(cond_e, 1)
            for k in range(KD):
                job_square(k)
            t.add("acc", KD)
            act.wait_ge(rows_zero, 4)
            ada()
            split_part(PANEL)
            norm_root(T, D)
            split_part(PANEL)
            skip()
            ada()
            act.wait_ge(gains_ready, 1)
            chunks_hi(0, 0, SHIFT1, (0, 1))

            for k in range(2):
                b = job()
                done(act.activation(SQ[:, k, :], b[:, :], ACT.Square))
            split()
            b = job()
            act.wait_ge(ones_done, t.first("ones") + 1)
            done(act.activation(SQ[:, 0, :], b[:, :], ACT.Square))
            t.add("ones")
            b = job()
            done(act.activation(KR[NOPE:QH, :], b[NOPE:QH, :], ACT.Copy))
            norm_root(T, Q_LORA)
            norm_root(T, KV_LORA, 1)
            warm(40, ACT.Exp)
            split()
            act.wait_ge(rows_zero, 10)
            for g in range(POOL_GROUPS):
                b = job()
                done(act.activation(PRAW[:, g, :, PAD:PAD + SEG], b[:, :].rearrange("p (s n) -> p s n", s=2), ACT.Copy))
                if g == 1:
                    skip(2)
                    for k in range(3):
                        hi(QN_hi[:, k, :], LORA[:, k, :])
                    split_part(2 * HEADS * QH)
                    t.add("full")
                    act.wait_ge(full_ready, t.at("full"))
                    act.activation(K_hi[NOPE:QH, 0, :], KR[NOPE:QH, :], ACT.Copy)
                    act.activation(K_hi[NOPE:QH, 1, :], KR[NOPE:QH, :], ACT.Copy).then_inc(hi_ready, 1)
            split_part(D + POOL_GROUPS * P)

            def both(out, in_):
                done(act.activation(out, in_, ACT.Copy))


            def pair_q():
                for hh in range(2):
                    both(QF[0:QH, hh, :], job()[0:QH, :])

            def pair_k():
                for hh in range(2):
                    both(K_hi[0:NOPE, hh, :], job()[0:NOPE, :])
                hi(Q_hi[0:QH, :, :], QF[0:QH, :, :])

            pair_q()
            pair_k()
            for tt in range(4):
                both(V_hi[:, tt, :], job()[:, :])

            def pair_softmax(p):
                for tt in range(2):
                    for hh in range(2):
                        b = job()
                        t.add("max")
                        act.wait_ge(rowmax, t.at("max"))
                        n = tt * 2 + hh
                        done(act.activation(PROBS[p % 2][:, n, :], b[:, :], ACT.Exp, bias=small[:, 1 + n:2 + n],
                                            scale=ATT_SCALE, accum_out=small[:, 9 + n:10 + n]))
                if p == 1:
                    act.wait_ge(pool_d, POOL_GROUPS)
                for tt in range(2):
                    b = job()
                    t.add("max")
                    act.wait_ge(rowmax, t.at("max"))
                    for hh in range(2):
                        n = 4 + tt * 2 + hh
                        ins = act.activation(PROBCS[p % 2][:, tt, hh, :], b[:, hh * SEG:(hh + 1) * SEG], ACT.Exp,
                                             bias=small[:, 1 + n:2 + n], scale=ATT_SCALE,
                                             accum_out=small[:, 9 + n:10 + n])
                    done(ins)

            def pair_values(p, first_filler, second_filler):
                def out(s):
                    b = job()
                    cs = slice(s * SEG, (s + 1) * SEG)
                    act.activation(H_hi[0:VD, p, cs], b[0:VD, 0:SEG], ACT.Copy)
                    both(H_hi[VD:P, p, cs], b[VD:P, SEG:T])

                for kt in (2, 3, 0, 1):
                    both(PT_hi[:, kt, :], job()[:, :])
                first_filler()
                out(0)
                for kt in (2, 3):
                    both(PT_hi[:, kt, :], job()[:, :])
                second_filler()
                out(1)

            def next_qk():
                pair_q()
                pair_k()

            def pool_split():
                for g in range(POOL_GROUPS):
                    act.activation(PD_hi[:, g, :], PD[:, g, :], ACT.Copy).then_inc(hi_ready, 1)

            def pool_products():
                for g in range(POOL_GROUPS):
                    done(act.activation(H_hi[:, 4 + g, :], job()[:, :], ACT.Copy, scale=gcol[:, 67 + g:68 + g]))

            pair_softmax(0)
            next_qk()
            ada()
            for p in range(1, PAIRS - 1):
                pair_softmax(p)
                pair_values(p - 1, next_qk, ada)
            pair_softmax(PAIRS - 1)

            def last_fill():
                ada()
                pool_split()

            def pool_products_and_split():
                split()
                pool_products()

            pair_values(PAIRS - 2, last_fill, pool_products_and_split)
            pair_values(PAIRS - 1, lambda: None, lambda: None)

            split()
            warm(41, ACT.Sqrt)
            for c in range(4):
                for m in range(2):
                    job_square(2 * c + m)
                split()
            t.add("acc", KD)
            norm_root(T, D)
            skip()
            ada()
            squares_of_x(0, 0)
            norm_root(T, D)
            skip()

            def ffn(layer, c0, last_layer):
                segs = (0, 1) if c0 == 0 else (1,)
                w = T - c0
                chunks_hi(layer, 1, SHIFT2, segs, None if last_layer else (3, ada))
                for half in range(2):
                    with t.loop(act, 2, job=8, split=4, chain=8) as i:
                        for n in range(4):
                            for m in range(2):
                                b = job()
                                r = m % 2
                                act.wait_ge(dve_out, t.evacuated("d", t.first("job") - 3))
                                act.activation(TMP[:, r, c0:T], b[:, 0:w], ACT.Relu).then_inc(act_chain, 1)
                                t.add("chain")
                                act.wait_ge(act_chain, t.at("chain"))
                                done(act.activation(HID_hi[:, bass.ds(i * 8 + (2 * n + m), 1), c0:T],
                                                    TMP[:, r:r + 1, c0:T], ACT.Square))
                            split()
                    if last_layer and half:
                        for part in range(2):
                            for tt in range(2):
                                both(OUTR[:, tt, part * 512:(part + 1) * 512], job()[:, :])

                    def two_chunks(i, c, more):
                        t.add("half_sum")
                        if more:
                            act.wait_ge(half_sum, t.at("half_sum"))
                            split()
                        for m in range(2):
                            t.add("job")
                            if half:
                                act.wait_ge(dve_out, t.evacuated("d", t.first("job") - 1))
                                act.wait_ge(acc_done, t.at("acc", -1))
                                y = Y[:, bass.ds(i * 4 + (2 * c + m), 1), c0:T] if t.reg is not None else \
                                    Y[:, 2 * c + m:2 * c + m + 1, c0:T]
                                act.activation(SQ[:, m:m + 1, c0:T], y, ACT.Square).then_inc(sq_ready, 1)
                                t.add("acc")
                            if half and last_layer:
                                k = 2 * c + m
                                act.activation(Z[:, k, :], Y[:, k, LAT:T], ACT.Copy,
                                               scale=post_gain[:, layer, 1, k, 1:2]).then_inc(z_ready, 1)
                        if more:
                            split()

                    if last_layer and half:
                        for c in range(4):
                            two_chunks(0, c, c < 3)
                    else:
                        extra = dict(acc=4) if half else {}
                        with t.loop(act, 2, job=4, split=4, half_sum=2, **extra) as i:
                            for c in range(2):
                                two_chunks(i, c, True)
                if not last_layer:
                    norm_root(w, D)
                    skip()
                    return
                b = job()
                done(act.activation(RQ[0][:, 0:4], b[:, 0:4], ACT.Sqrt, bias=eps_col, scale=1.0 / D))

            ffn(0, 0, False)
            ada()
            squares_of_x(0, KD)
            norm_root(T, D)
            skip()

            def decay_load(h):
                act.dma_start(DEC[:, :, :], A["decay"][h]).then_inc(decay_in, 16)

            def head_qk():
                both(QK[:, 0, :], job()[:, 0:SEG])
                b = job()
                act.activation(QK[:, 1, :], b[:, LAT:T], ACT.Copy)
                both(QK[:, 2, :], b[:, 0:SEG])
                split()

            def head_rotated():
                skip()
                hi(QK_hi[:, :, :], QK[:, :, :])

            def head_v():
                for jj in range(2):
                    both(RV_hi[:, 2 * jj:2 * jj + 2, :], job()[:, :])

            def head_attend(h, last):
                skip(2)
                for jj in range(2):
                    hi(SA_hi[:, 2 * jj:2 * jj + 2, :], SA[:, 2 * jj:2 * jj + 2, :])
                if not last:
                    act.dma_start(DEC[:, :, :], A["decay"][bass.ds(h + 1, 1)].rearrange("a p k n -> p (a k) n"))\
                       .then_inc(decay_in, 16)
                split()
                for tt in range(2):
                    done(act.activation(GE[:, tt, :], job()[:, 0:R_DV], ACT.Exp, scale=-1.0))
                if not last:
                    split()
                skip(2)

            chunks_hi(1, 0, SHIFT1, (0, 1), (3, ada))
            decay_load(0)
            head_qk()
            head_rotated()
            head_v()
            with t.loop(act, HEADS - 1, job=16, split=4, full=3) as h:
                head_attend(h, False)
                head_qk()
                both(YT_hi[:, :, :], job()[:, :])
                head_rotated()
                head_v()
                split()
                skip(4)
            head_attend(HEADS - 1, True)
            ada()
            both(YT_hi[:, :, :], job()[:, :])
            split()
            warm(42, ACT.Sqrt)
            first_out = t.first("job")
            skip(4)
            for k in range(KD):
                act.wait_ge(dve_out, part_of("d", first_out + k // 2))
                squares_free(k)
                act.activation(SQ[:, k % 2, LAT:T], Y[:, k, LAT:T], ACT.Square).then_inc(sq_ready, 1)
            split()
            t.add("ones", KD - 1)
            norm_root(SEG, D)
            skip()
            ada()
            squares_of_x(LAT, 2 * KD)
            norm_root(SEG, D)
            skip()
            ffn(1, LAT, True)
            assert t.first("job") == len(JOBS) and t.first("split") == len(SPLIT_AT), (t.n, len(JOBS))

        @block.vector
        def _(dve):
            t = Tally()

            def split(cols=PANEL):
                s = t.first("split")
                t.add("split")
                dve.wait_ge(split_hi, t.at("split"))
                raw = RAW[SPLIT_AT[s] % RAW_SLOTS]
                dve.tensor_tensor(W_lo[s % 2][:, 0:cols], raw[:, 0:cols], W_hi[s % 2][:, 0:cols].bitcast(F32),
                                  ALU.subtract).then_inc(split_lo, 1)

            def job():
                j = t.first("job")
                t.add("job")
                if "a" in JOBS[j][1]:
                    dve.wait_ge(act_out, t.evacuated("a", j))
                else:
                    dve.wait_ge(acc_full, t.at("job"))
                return bank[j % BANKS]

            def skip(k=1):
                t.add("job", k)

            def done(ins):
                ins.then_inc(dve_out, 1)

            def chain(ins):
                ins.then_inc(dve_chain, 1)
                t.add("chain")

            def settle():
                dve.wait_ge(dve_chain, t.at("chain"))

            def lo(out, full, hi_part):
                t.add("hi")
                dve.wait_ge(hi_ready, t.at("hi"))
                dve.tensor_tensor(out, full, hi_part.bitcast(F32), ALU.subtract).then_inc(lo_ready, 1)
                t.add("lo")

            def job_lo(out, hi_part):
                b = job()
                done(dve.tensor_tensor(out, b[:, :], hi_part.bitcast(F32), ALU.subtract))

            roots = []

            def norm_recip(width, place=0):
                job()
                w = width // 4
                done(dve.reciprocal(RQ[place][:, 0:w], RQ[place][:, 0:w]))

            def norm_spread(width):
                roots[:] = [job()[:, 0:width]]

            def norm_rms(width):
                norm_recip(width)
                norm_spread(width)

            def ada(layer, part):
                skip()
                b = job()
                rows = b[:, 0:256].rearrange("p (c j s) -> p c j s", c=2, s=32)
                bias = bcol[:, layer * 48 + part * 8:layer * 48 + part * 8 + 8]
                for c in range(2):
                    o = mod[:, layer, part, :, :].rearrange("p (j c) s -> p c j s", c=2)[:, c, :, :]
                    ins = dve.tensor_tensor(o, rows[:, c, :, 0:2],
                                            bias.rearrange("p (j c) -> p c j", c=2)[:, c, :].unsqueeze(2)
                                            .to_broadcast([P, 4, 2]), ALU.add)
                    if c == 0:
                        chain(ins)
                done(ins)
                dve.wait_ge(dve_out, part_of("d", t.first("job") - 1))
                which = int(part >= SHIFT2)
                m = mod[:, layer, part, :, :]
                if part in (SCALE1, SCALE2):
                    g = gcol[:, which * 32 + layer * 8:which * 32 + layer * 8 + 8].unsqueeze(2).to_broadcast([P, 8, 2])
                    chain(dve.scalar_tensor_tensor(out=pre_gain[:, layer, which, :, :], in0=m, scalar=1.0, in1=g,
                                                   op0=ALU.add, op1=ALU.mult))
                if part in (GATE1, GATE2):
                    c0 = 16 + which * 32 + layer * 8
                    g = gcol[:, c0:c0 + 8].unsqueeze(2).to_broadcast([P, 8, 2])
                    chain(dve.tensor_tensor(post_gain[:, layer, which, :, :], m, g, ALU.mult))

            def chunks_full(segs, midway=None):
                c0 = segs[0] * SEG

                def lo_of(k):
                    lo(H_lo[:, k, c0:T], h_buffer(k)[:, c0:T], H_hi[:, k, c0:T])

                def over_rms(k):
                    dve.tensor_tensor(h_buffer(k)[:, c0:T], X[:, k, c0:T], roots[0], ALU.mult).then_inc(full_ready, 1)

                for k in range(4):
                    over_rms(k)
                for k in range(KD):
                    if midway and k == midway[0]:
                        midway[1]()
                    lo_of(k)
                    if k + 4 < KD:
                        dve.wait_ge(lo_ready, t.at("lo"))
                        over_rms(k + 4)

            def update_x(layer, which, segs):
                c0 = segs[0] * SEG
                settle()
                for k in range(KD + 1):
                    if k < KD:
                        chain(dve.tensor_tensor(Y[:, k, c0:T], Y[:, k, c0:T], roots[0], ALU.mult))
                    if k >= 1:
                        dve.wait_ge(dve_chain, t.at("chain", -1 if k < KD else 0))
                        for s in segs:
                            cs = slice(s * SEG, (s + 1) * SEG)
                            ins = dve.scalar_tensor_tensor(out=X[:, k - 1, cs], in0=Y[:, k - 1, cs],
                                                           scalar=post_gain[:, layer, which, k - 1, s:s + 1],
                                                           in1=X[:, k - 1, cs], op0=ALU.mult, op1=ALU.add)
                        ins.then_inc(x_ready, 1)
                        t.add("x")
                dve.wait_ge(x_ready, t.at("x"))

            def clear_acc():
                chain(dve.memset(ACC[:, :], 0.0))
                settle()

            def keep_and_add(out, k):
                done(dve.tensor_copy(out[:, k, :], job()[:, :]))
                if t.first("acc"):
                    dve.wait_ge(acc_done, t.at("acc"))
                dve.tensor_tensor(ACC[:, :], ACC[:, :], SQ[:, k % 2, :], ALU.add).then_inc(acc_done, 1)
                t.add("acc")

            done(dve.tensor_copy(bcol[:, :], job()[:, 0:96]))
            b = job()
            done(dve.tensor_copy(gcol[:, :], b[:, 0:88]))
            dve.wait_ge(dve_out, 2)
            dve.sem_inc(cond_e, 1)
            dve.wait_ge(cond_e, 2)
            chain(dve.tensor_scalar(silu_e[:, :], silu_e[:, :], 1.0, None, ALU.add))
            settle()
            chain(dve.reciprocal(silu_e[:, :], silu_e[:, :]))
            settle()
            dve.wait_ge(rows_zero, 3)
            for s, c0 in ((1, 0), (0, 8)):
                dve.tensor_tensor(cond[:, :, s], gcol[:, 71 + c0:79 + c0], silu_e[:, c0:c0 + 8],
                                  ALU.mult).then_inc(cond_ready, 1)
            clear_acc()
            for k in range(KD):
                keep_and_add(X, k)
            ada(0, SHIFT1)
            split()
            norm_rms(T)
            split()

            def last_modulation():
                ada(0, SCALE1)
                settle()
                dve.sem_inc(gains_ready, 1)

            chunks_full((0, 1), (0, last_modulation))

            for k in range(2):
                done(dve.tensor_copy(LORA[:, k, :], job()[:, :]))
            split()
            done(dve.tensor_copy(LORA[:, 2, :], job()[:, :]))
            skip()

            def lora(k, col):
                dve.scalar_tensor_tensor(out=LORA[:, k, :], in0=LORA[:, k, :], scalar=gcol[:, col:col + 1],
                                         in1=roots[0], op0=ALU.mult, op1=ALU.mult).then_inc(full_ready, 1)

            norm_recip(T)
            norm_recip(T, 1)
            split()
            skip(2)
            norm_spread(T)
            lora(0, 64)
            lora(1, 65)
            norm_spread(T)
            lora(2, 66)
            for k in range(3):
                lo(QN_lo[:, k, :], LORA[:, k, :], QN_hi[:, k, :])

            def rotate(x, sw, cos, sin):
                chain(dve.stream_shuffle(sw, x, [(n // 16) * 16 + (n + 8) % 16 for n in range(32)]))
                settle()
                chain(dve.tensor_tensor(sw, sw, sin, ALU.mult))
                chain(dve.tensor_tensor(x, x, cos, ALU.mult))
                settle()
                dve.tensor_tensor(x, x, sw, ALU.add).then_inc(full_ready, 1)

            dve.wait_ge(consts_in, 16)
            split(2 * HEADS * QH)
            rotate(KR[NOPE:QH, LAT:T], SW[NOPE:QH, 0, 0:SEG], ropeA[NOPE:QH, 0, :], ropeA[NOPE:QH, 1, :])
            t.add("hi")
            dve.wait_ge(hi_ready, t.at("hi"))
            dve.tensor_tensor(K_lo[NOPE:QH, 0, :], KR[NOPE:QH, :], K_hi[NOPE:QH, 0, :].bitcast(F32), ALU.subtract)
            dve.tensor_tensor(K_lo[NOPE:QH, 1, :], KR[NOPE:QH, :], K_hi[NOPE:QH, 1, :].bitcast(F32),
                              ALU.subtract).then_inc(lo_ready, 1)
            t.add("lo")
            skip(2)
            split(D + POOL_GROUPS * P)

            def pair_q():
                skip(2)
                dve.wait_ge(act_out, part_of("a", t.first("job") - 1))
                cos, sin = [ropeA[NOPE:QH, n, :].unsqueeze(1).to_broadcast([ROPE, 2, SEG]) for n in range(2)]
                rotate(QF[NOPE:QH, :, LAT:T], SW[NOPE:QH, :, 0:SEG], cos, sin)

            def pair_k():
                for hh in range(2):
                    b = job()
                    done(dve.tensor_tensor(K_lo[0:NOPE, hh, :], b[0:NOPE, :], K_hi[0:NOPE, hh, :].bitcast(F32),
                                           ALU.subtract))
                lo(Q_lo[0:QH, :, :], QF[0:QH, :, :], Q_hi[0:QH, :, :])

            pair_q()
            pair_k()
            for tt in range(4):
                job_lo(V_lo[:, tt, :], V_hi[:, tt, :])

            def pair_maxima():
                j0 = t.first("job")
                skip(6)

                def row_max(n):
                    dve.wait_ge(acc_full, j0 + n + 1)
                    b = bank[(j0 + n) % BANKS]
                    if n < 4:
                        mx, nm = small[:, 25 + n:26 + n], small[:, 1 + n:2 + n]
                        chain(dve.tensor_reduce(mx, b[:, :], AXX, ALU.max))
                    else:
                        mx, nm = small[:, 21 + 2 * n:23 + 2 * n], small[:, 2 * n - 3:2 * n - 1]
                        chain(dve.tensor_reduce(mx, b[:, :].rearrange("p (h k) -> p h k", h=2), AXX, ALU.max))
                    settle()
                    dve.tensor_scalar(nm, mx, -ATT_SCALE, None, ALU.mult).then_inc(rowmax, 1)

                for n in range(6):
                    row_max(n)

            def pair_normalise(p):
                PR, PC = PROBS[p % 2], PROBCS[p % 2]
                for n in range(6):
                    dve.wait_ge(act_out, part_of("a", first_job("scores", p) + n))
                    if n < 4:
                        chain(dve.reciprocal(small[:, 17 + n:18 + n], small[:, 9 + n:10 + n]))
                        settle()
                        ins = dve.tensor_scalar(PR[:, n, :], PR[:, n, :], small[:, 17 + n:18 + n], None, ALU.mult)
                    else:
                        c0 = 2 * n - 4
                        chain(dve.reciprocal(small[:, 17 + c0:19 + c0], small[:, 9 + c0:11 + c0]))
                        settle()
                        for hh in range(2):
                            ins = dve.tensor_scalar(PC[:, n - 4, hh, :], PC[:, n - 4, hh, :],
                                                    small[:, 17 + c0 + hh:18 + c0 + hh], None, ALU.mult)
                    ins.then_inc(normalised, 1)

            def pair_values(p, first_filler, second_filler):
                def out(s):
                    b = job()
                    cs = slice(s * SEG, (s + 1) * SEG)
                    dve.tensor_tensor(H_lo[0:VD, p, cs], b[0:VD, 0:SEG], H_hi[0:VD, p, cs].bitcast(F32), ALU.subtract)
                    done(dve.tensor_tensor(H_lo[VD:P, p, cs], b[VD:P, SEG:T], H_hi[VD:P, p, cs].bitcast(F32),
                                           ALU.subtract))

                for kt in (2, 3, 0, 1):
                    job_lo(PT_lo[:, kt, :], PT_hi[:, kt, :])
                first_filler()
                out(0)
                for kt in (2, 3):
                    job_lo(PT_lo[:, kt, :], PT_hi[:, kt, :])
                second_filler()
                out(1)

            def next_qk():
                pair_q()
                pair_k()

            def pool_products():
                for g in range(POOL_GROUPS):
                    b = job()
                    done(dve.scalar_tensor_tensor(out=H_lo[:, 4 + g, :], in0=b[:, :], scalar=gcol[:, 67 + g:68 + g],
                                                  in1=H_hi[:, 4 + g, :].bitcast(F32), op0=ALU.mult,
                                                  op1=ALU.subtract))

            def normalise_and_ada(p, part):
                pair_normalise(p)
                ada(0, part)

            pair_maxima()
            next_qk()
            normalise_and_ada(0, GATE1)
            for p in range(1, PAIRS - 1):
                pair_maxima()
                pair_values(p - 1, next_qk, lambda: normalise_and_ada(p, (GATE1, SHIFT2, SCALE2)[p]))
            pair_maxima()

            def last_fill():
                normalise_and_ada(PAIRS - 1, GATE2)
                for g in range(POOL_GROUPS):
                    lo(PD_lo[:, g, :], PD[:, g, :], PD_hi[:, g, :])

            def pool_products_and_split():
                split()
                pool_products()

            pair_values(PAIRS - 2, last_fill, pool_products_and_split)
            pair_values(PAIRS - 1, lambda: None, lambda: None)

            clear_acc()
            split()
            for c in range(4):
                for m in range(2):
                    keep_and_add(Y, 2 * c + m)
                if c < 3:
                    split()
            norm_recip(T)
            split()
            norm_spread(T)
            update_x(0, 0, (0, 1))
            ada(1, SHIFT1)
            norm_rms(T)

            def ffn(layer, c0, last_layer):
                segs = (0, 1) if c0 == 0 else (1,)
                w = T - c0
                chunks_full(segs, None if last_layer else (3, lambda: ada(1, SCALE1)))
                for half in range(2):
                    with t.loop(dve, 2, job=8, split=4, chain=8) as i:
                        for n in range(4):
                            for m in range(2):
                                job()
                                r = m % 2
                                chain(dve.tensor_tensor(TMP[:, r:r + 1, c0:T], TMP[:, r:r + 1, c0:T],
                                                        TMP[:, r:r + 1, c0:T], ALU.mult))
                                settle()
                                c = bass.ds(i * 8 + (2 * n + m), 1)
                                done(dve.tensor_tensor(HID_lo[:, c, c0:T], TMP[:, r:r + 1, c0:T],
                                                       HID_hi[:, c, c0:T].bitcast(F32), ALU.subtract))
                            split()
                    if last_layer and half:
                        skip(4)
                    sums0 = t.first("job")

                    if half:
                        dve.wait_ge(dve_out, part_of("d", t.first("job") - 1))
                        chain(dve.memset(ACC[:, :], 0.0))
                        settle()

                    def two_chunks(i, c, more, second=True):
                        if more:
                            split()
                        for m in range(2):
                            job()
                            b = ffn_bank(sums0, t.first("job") - 1)
                            y = Y[:, bass.ds(i * 4 + (2 * c + m), 1), c0:T] if t.reg is not None else \
                                Y[:, 2 * c + m:2 * c + m + 1, c0:T]
                            ps = b[:, 0:w].unsqueeze(1)
                            if not half:
                                done(dve.tensor_copy(y, ps))
                                continue
                            done(dve.tensor_tensor(y, ps, y, ALU.add))
                            t.add("sq")
                            dve.wait_ge(sq_ready, t.at("sq"))
                            dve.wait_ge(acc_done, t.at("acc"))
                            dve.tensor_tensor(ACC[:, c0:T], ACC[:, c0:T], SQ[:, m, c0:T], ALU.add).then_inc(acc_done, 1)
                            t.add("acc")
                        if more and second:
                            split()

                    if half:
                        for c in range(4):
                            two_chunks(0, c, c < 3 or not last_layer, c < 3)
                    else:
                        with t.loop(dve, 2, job=4, split=4) as i:
                            for c in range(2):
                                two_chunks(i, c, True)
                if not last_layer:
                    norm_recip(w)
                    split()
                    norm_spread(w)
                    update_x(layer, 1, segs)
                    return
                job()
                done(dve.reciprocal(RQ[0][:, 0:4], RQ[0][:, 0:4]))
                dve.wait_ge(dve_out, part_of("d", t.first("job") - 1))
                dve.wait_ge(z_turned, 1)
                for part in range(2):
                    for tt in range(2):
                        rows = OUTR[:, tt, part * 512:(part + 1) * 512]
                        dve.scalar_tensor_tensor(out=rows, in0=row_bank(part, tt)[:, :],
                                                 scalar=RQ[0][:, 2 * tt:2 * tt + 1], in1=rows, op0=ALU.mult,
                                                 op1=ALU.add).then_inc(result_ready, 1)

            t.add("sq", KD)
            ffn(0, 0, False)
            ada(1, GATE1)
            norm_rms(T)
            t.add("sq", KD)

            chunks_full((0, 1), (3, lambda: ada(1, SHIFT2)))
            dve.wait_ge(y_zero, 1)
            dve.wait_ge(ret_in, 32)

            def head_qk():
                skip(2)
                dve.wait_ge(act_out, t.evacuated("a", t.first("job") - 1))
                cos = ropeR[:, 0, :].unsqueeze(1).to_broadcast([P, 2, SEG])
                chain(dve.tensor_tensor(ROT[:, :, :], QK[:, 0:2, :], cos, ALU.mult))

            def head_rotated():
                sin = ropeR[:, 1, :].unsqueeze(1).to_broadcast([P, 2, SEG])
                settle()
                b = job()
                done(dve.tensor_tensor(QK[:, 0:2, :], b[:, :].rearrange("p (a n) -> p a n", a=2), sin, ALU.mult))
                dve.wait_ge(dve_out, t.evacuated("d", t.first("job") - 1))
                dve.tensor_tensor(QK[:, 0:2, :], QK[:, 0:2, :], ROT[:, :, :], ALU.add).then_inc(full_ready, 1)
                lo(QK_lo[:, :, :], QK[:, :, :], QK_hi[:, :, :])
                split()

            def head_v():
                for jj in range(2):
                    job_lo(RV_lo[:, 2 * jj:2 * jj + 2, :], RV_hi[:, 2 * jj:2 * jj + 2, :])

            def head_attend(last=False):
                t.add("decay")
                dve.wait_ge(decay_in, t.at("decay") * 16)
                for jj in range(2):
                    b = job()
                    s = SA[:, 2 * jj:2 * jj + 2, :]
                    done(dve.tensor_tensor(s, b[:, :].rearrange("p (a n) -> p a n", a=2),
                                           DEC[:, 2 * jj:2 * jj + 2, :], ALU.mult))
                    dve.wait_ge(dve_out, t.evacuated("d", t.first("job") - 1))
                    dve.sem_inc(full_ready, 1)
                for jj in range(2):
                    s = slice(2 * jj, 2 * jj + 2)
                    lo(SA_lo[:, s, :], SA[:, s, :], SA_hi[:, s, :])
                split()
                for tt in range(2):
                    gate = job()
                    chain(dve.tensor_scalar(GE[:, tt, :], GE[:, tt, :], 1.0, None, ALU.add))
                    settle()
                    chain(dve.reciprocal(GE[:, tt, :], GE[:, tt, :]))
                    if tt == 0:
                        settle()
                        done(dve.tensor_tensor(GS[:, tt, :], gate[:, 0:R_DV], GE[:, tt, :], ALU.mult))
                banks = [bank[(t.first("job") + tt) % BANKS] for tt in range(2)]
                for tt in range(2):
                    dve.wait_ge(acc_full, t.at("job", tt + 1))
                    chain(dve.bn_stats(stats[:, tt, :], banks[tt][:, 0:R_DV]))
                settle()
                done(dve.tensor_tensor(GS[:, 1, :], gate[:, 0:R_DV], GE[:, 1, :], ALU.mult))
                for tt in range(2):
                    chain(dve.bn_aggr(mv[:, tt, :], stats[:, tt, :]))
                settle()
                t.add("stat")
                dve.tensor_scalar(mv[:, :, 1], mv[:, :, 1], EPS, None, ALU.add).then_inc(stat_ready, 1)
                dve.wait_ge(rstd_ready, t.at("stat"))
                for tt in range(2):
                    job()
                    done(dve.tensor_scalar(ON[:, tt, :], banks[tt][:, 0:R_DV], mv[:, tt, 0:1], rstd[:, tt:tt + 1],
                                           ALU.subtract, ALU.mult))
                dve.wait_ge(dve_out, t.evacuated("d", t.first("job") - 1))
                dve.tensor_tensor(ON[:, :, :], ON[:, :, :], GS[:, :, :], ALU.mult).then_inc(rows_ready, 1)
                if not last:
                    split()

            def head_out():
                for jj in range(4):
                    b = job()
                    y = Y[:, 2 * jj:2 * jj + 2, LAT:T]
                    done(dve.tensor_tensor(y, b[:, :].rearrange("p (a n) -> p a n", a=2), y, ALU.add))

            head_qk()
            head_rotated()
            head_v()
            with t.loop(dve, HEADS - 1, job=16, split=4, chain=9, hi=3, lo=3, decay=1, stat=1):
                head_attend()
                head_qk()
                job_lo(YT_lo[:, :, :], YT_hi[:, :, :])
                head_rotated()
                head_v()
                split()
                head_out()
            head_attend(last=True)
            ada(1, SCALE2)
            job_lo(YT_lo[:, :, :], YT_hi[:, :, :])
            split()
            head_out()
            norm_recip(SEG)
            split()
            norm_spread(SEG)
            update_x(1, 0, (1,))
            t.add("sq", 2 * KD)
            ada(1, GATE2)
            norm_rms(SEG)
            ffn(1, LAT, True)
            assert t.first("job") == len(JOBS) and t.first("split") == len(SPLIT_AT), (t.n, len(JOBS))


def tables():
    n = np.arange(SEG)
    row, col = (n // 64).astype(np.float64), (n % 64).astype(np.float64)

    def rotary(width):
        d = width // 2
        f = 10000.0 ** (-np.arange(0, d, 2) / d)
        angle = [pos[None, :] * f[:, None] for pos in (row, col)]
        cos = np.concatenate([np.concatenate([np.cos(a)] * 2) for a in angle])
        sin = np.concatenate([np.concatenate([-np.sin(a), np.sin(a)]) for a in angle])
        return cos, sin

    cos, sin = rotary(ROPE)
    att = np.stack([cos, sin], axis=1)
    ret = np.stack(rotary(R_DK), axis=1)
    swap = np.zeros((P, P))
    for a in range(P):
        swap[(a // 64) * 64 + (a + 32) % 64, a] = 1.0
    inv = np.zeros((P, POOL_GROUPS, SEG))
    for g in range(POOL_GROUPS):
        w = 2 << g
        inv[:, g, :] = 1.0 / (np.clip(n + w // 2, 0, SEG) - np.clip(n - w // 2, 0, SEG))
    logs = np.log1p(-np.exp2(-5.0 - np.arange(HEADS)))
    decay = np.zeros((HEADS, P, 4, SEG))
    q = n[None, :]
    for h in range(HEADS):
        f, b = logs[h], logs[HEADS - 1 - h]
        key = n[:, None]
        context = np.exp(f * (q + SEG - key)) + np.exp(b * (SEG - q + key))
        latent = np.where(key <= q, np.exp(f * np.maximum(q - key, 0)), np.exp(b * np.maximum(key - q, 0)))
        both = np.concatenate([context, latent]) * R_DK ** -0.5
        decay[h] = both.reshape(4, P, SEG).transpose(1, 0, 2)
    return {name: np.ascontiguousarray(a, dtype=np.float32) for name, a in
            dict(rope_att=att, rope_ret=ret, swap=swap, pool_inv=inv, decay=decay).items()}


INPUTS = ["x", "c", "ctx", "c_ctx", "w_ada", "b_ada", "g_mix_pre", "g_mix_post", "g_ffn_pre", "g_ffn_post",
          "w_ffn_in", "w_ffn_out", "w_in_even", "g_q_lora", "g_kv_lora", "w_uq", "w_ukv", "w_pool", "pool_scale",
          "w_out_even", "w_in_odd", "w_out_odd"]


def kernel(**inputs):
    import concourse.bacc as bacc
    from concourse.bass_utils import run_bass_kernel_spmd

    nc = bacc.Bacc("TRN2", target_bir_lowering=False, num_devices=1)
    arrays = {name: np.ascontiguousarray(inputs[name]) for name in INPUTS}
    arrays.update(tables())
    arrays = {f"in_{name}": a for name, a in arrays.items()}
    A = {name[3:]: nc.dram_tensor(name, a.shape, mybir.dt.from_np(a.dtype), kind="ExternalInput").ap()
         for name, a in arrays.items()}
    out = nc.dram_tensor("latent_out", (1, SEG, D), F32, kind="ExternalOutput").ap()
    build(nc, A, out)
    result = run_bass_kernel_spmd(nc, [arrays], core_ids=[0])
    return result.results[0]["latent_out"]
```
